# Optimizing a Trainium2 kernel written in Bass

```python
import math
import jax
import jax.numpy as jnp
from jax import lax
import numpy as np
import jax, jax.numpy as jnp

D_MODEL = 1024
BATCH = 1
SEQ = 256
DEPTH = 1

MEM_LEN = 256
EPS = 1e-6
NEG_INF = -1e30
BIG = 1e30

GLA_HEADS = 4
GLA_DK = 64
GLA_DV = 128
GLA_RANK = 16
GLA_TAU = 16.0
GLA_CHUNK = 64

NSA_HEADS = 8
NSA_KV_GROUPS = 2
NSA_HPG = NSA_HEADS // NSA_KV_GROUPS
NSA_DH = 64
CMP_BLOCK = 32
CMP_STRIDE = 16
CMP_HIDDEN = 128
SLC_BLOCK = 64
SLC_TOPK = 16
WINDOW = 512
Q_BLOCK = 128

REL_BUCKETS = 32
REL_MAX_DIST = 2048

XA_HEADS = 4
XA_DH = D_MODEL // XA_HEADS

PEER_HEADS = 8
PEER_NKEYS = 128
PEER_EXPERTS = PEER_NKEYS * PEER_NKEYS
PEER_TOPK = 16
PEER_DKEY = 128
PEER_TOKEN_CHUNK = 128

IN_SIZES = (GLA_HEADS * GLA_DK, GLA_HEADS * GLA_DK, GLA_HEADS * GLA_DV, GLA_HEADS * GLA_DV, GLA_RANK,
            NSA_HEADS * NSA_DH,
            NSA_KV_GROUPS * NSA_DH, NSA_KV_GROUPS * NSA_DH,
            NSA_KV_GROUPS * NSA_DH, NSA_KV_GROUPS * NSA_DH,
            NSA_KV_GROUPS * NSA_DH, NSA_KV_GROUPS * NSA_DH,
            NSA_HEADS * 3)
IN_COLS = sum(IN_SIZES)


def rms_norm(x, g):
    xf = x.astype(jnp.float32)
    y = xf * lax.rsqrt(jnp.mean(xf * xf, axis=-1, keepdims=True) + EPS)
    return (y * g.astype(jnp.float32)).astype(x.dtype)

def _masked_softmax(s, mask):
    s = jnp.where(mask, s.astype(jnp.float32), NEG_INF)
    p = jax.nn.softmax(s, axis=-1)
    return p * jnp.any(mask, axis=-1, keepdims=True)

def _t5_bucket(dist):
    n = jnp.maximum(dist, 0)
    max_exact = REL_BUCKETS // 2
    nf = jnp.maximum(n, 1).astype(jnp.float32)
    log_ratio = jnp.log(nf / max_exact) / math.log(REL_MAX_DIST / max_exact)
    large = max_exact + (log_ratio * (REL_BUCKETS - max_exact)).astype(jnp.int32)
    large = jnp.minimum(large, REL_BUCKETS - 1)
    return jnp.where(n < max_exact, n, large)

def _head_bias(dist, rel_bias):
    b = jnp.moveaxis(rel_bias[_t5_bucket(dist)], -1, 0)
    return b.reshape((NSA_KV_GROUPS, NSA_HPG) + dist.shape).astype(jnp.float32)

def _split_cols(z):
    offs = np.cumsum(np.array(IN_SIZES))[:-1].tolist()
    return jnp.split(z, offs, axis=-1)

def _gla_chunked(q, k, v, log_a):
    B, T, H, dk = q.shape
    dv = v.shape[-1]
    C = GLA_CHUNK
    nc = T // C

    def to_chunks(a):
        return a.astype(jnp.float32).reshape(B, nc, C, H, a.shape[-1]).transpose(1, 0, 3, 2, 4)

    qc, kc, vc, ac = to_chunks(q), to_chunks(k), to_chunks(v), to_chunks(log_a)
    causal = jnp.tril(jnp.ones((C, C), dtype=bool))[..., None]

    def step(S, inp):
        qi, ki, vi, ai = inp
        b = jnp.cumsum(ai, axis=-2)
        diff = b[..., :, None, :] - b[..., None, :, :]
        decay = jnp.exp(jnp.where(causal, diff, NEG_INF))
        A = jnp.einsum('bhtd,bhsd,bhtsd->bhts', qi, ki, decay)
        o = jnp.einsum('bhts,bhsv->bhtv', A, vi) + jnp.einsum('bhtd,bhdv->bhtv', qi * jnp.exp(b), S)
        b_last = b[..., -1:, :]
        S_new = jnp.exp(b_last[..., 0, :])[..., None] * S + jnp.einsum(
            'bhsd,bhsv->bhdv', ki * jnp.exp(b_last - b), vi)
        return S_new, o

    S0 = jnp.zeros((B, H, dk, dv), jnp.float32)
    _, o = lax.scan(step, S0, (qc, kc, vc, ac))
    return o.transpose(1, 0, 3, 2, 4).reshape(B, T, H, dv)

def gla_mixer(gq, gk, gv, gr, glr, gate_w2, gate_b, out_norm):
    B, T, _ = gq.shape
    q = gq.reshape(B, T, GLA_HEADS, GLA_DK) * (GLA_DK ** -0.5)
    k = gk.reshape(B, T, GLA_HEADS, GLA_DK)
    v = gv.reshape(B, T, GLA_HEADS, GLA_DV)
    log_a = jax.nn.log_sigmoid((glr @ gate_w2 + gate_b).astype(jnp.float32)) / GLA_TAU
    log_a = log_a.reshape(B, T, GLA_HEADS, GLA_DK)
    o = _gla_chunked(q, k, v, log_a)
    o = rms_norm(o, out_norm).reshape(B, T, GLA_HEADS * GLA_DV)
    return (o * jax.nn.silu(gr.astype(jnp.float32))).astype(gq.dtype)

def _compress(kv, pos, w1, w2):
    B, T, G, dh = kv.shape
    n_cmp = (T - CMP_BLOCK) // CMP_STRIDE + 1
    idx = jnp.arange(n_cmp)[:, None] * CMP_STRIDE + jnp.arange(CMP_BLOCK)[None, :]
    blocks = kv[:, idx] + pos[None, None, :, None, :]
    blocks = blocks.transpose(0, 3, 1, 2, 4).reshape(B, G, n_cmp, CMP_BLOCK * dh)
    return jax.nn.gelu(blocks @ w1) @ w2

def _slc_importance(p_grp, n_slc):
    n_cmp = p_grp.shape[-1]
    ratio = SLC_BLOCK // CMP_STRIDE
    back = CMP_BLOCK // CMP_STRIDE - 1
    pad_end = max(ratio * n_slc - n_cmp, 0)
    pp = jnp.pad(p_grp, [(0, 0)] * (p_grp.ndim - 1) + [(back, pad_end)])
    base = jnp.arange(n_slc) * ratio + back
    imp = 0.0
    for r in range(-back, ratio):
        lo = CMP_STRIDE * r
        overlap = min(lo + CMP_BLOCK, SLC_BLOCK) - max(lo, 0)
        imp = imp + (overlap / CMP_BLOCK) * pp[..., base + r]
    return imp

def nsa_mixer(nq, kc, vc, ks, vs, kw, vw, ng, rel_bias, pos_k, pos_v, ck_w1, ck_w2, cv_w1, cv_w2):
    B, T, _ = nq.shape
    G, HPG, dh = NSA_KV_GROUPS, NSA_HPG, NSA_DH
    n_cmp = (T - CMP_BLOCK) // CMP_STRIDE + 1
    n_slc = T // SLC_BLOCK
    n_sel = min(SLC_TOPK, n_slc)
    n_qblk = T // Q_BLOCK
    kv_shape = (B, T, G, dh)

    q = (nq.reshape(B, T, G, HPG, dh) * (dh ** -0.5)).transpose(0, 2, 3, 1, 4)
    gates = jax.nn.sigmoid(ng.astype(jnp.float32)).reshape(B, T, G, HPG, 3).transpose(0, 2, 3, 1, 4)

    k_cmp = _compress(kc.reshape(kv_shape), pos_k, ck_w1, ck_w2)
    v_cmp = _compress(vc.reshape(kv_shape), pos_v, cv_w1, cv_w2)
    k_slc = ks.reshape(kv_shape).transpose(0, 2, 1, 3).reshape(B, G, n_slc, SLC_BLOCK, dh)
    v_slc = vs.reshape(kv_shape).transpose(0, 2, 1, 3).reshape(B, G, n_slc, SLC_BLOCK, dh)
    pad = ((0, 0), (0, 0), (WINDOW, 0), (0, 0))
    k_win = jnp.pad(kw.reshape(kv_shape).transpose(0, 2, 1, 3), pad)
    v_win = jnp.pad(vw.reshape(kv_shape).transpose(0, 2, 1, 3), pad)

    qi = jnp.arange(Q_BLOCK)
    kj = jnp.arange(WINDOW + Q_BLOCK)
    dist_w = qi[:, None] + WINDOW - kj[None, :]
    band = (dist_w >= 0) & (dist_w < WINDOW)
    bias_w = _head_bias(dist_w, rel_bias)
    cmp_end = jnp.arange(n_cmp) * CMP_STRIDE + (CMP_BLOCK - 1)
    slc_ids = jnp.arange(n_slc)
    bidx = jnp.arange(B)[:, None, None, None]
    gidx = jnp.arange(G)[None, :, None, None]
    table_g = rel_bias.reshape(REL_BUCKETS, G, HPG).transpose(1, 0, 2)

    def block(i):
        s0 = i * Q_BLOCK
        t = s0 + qi
        qb = lax.dynamic_slice_in_dim(q, s0, Q_BLOCK, axis=3)
        gb = lax.dynamic_slice_in_dim(gates, s0, Q_BLOCK, axis=3)

        dist_c = t[:, None] - cmp_end[None, :]
        s_c = jnp.einsum('bghqd,bgnd->bghqn', qb, k_cmp) + _head_bias(dist_c, rel_bias)
        p_c = _masked_softmax(s_c, dist_c >= 0)
        o_c = jnp.einsum('bghqn,bgnd->bghqd', p_c.astype(v_cmp.dtype), v_cmp)

        imp = _slc_importance(p_c.sum(axis=2), n_slc)
        cur = (t // SLC_BLOCK)[:, None]
        forced = (slc_ids == 0) | (slc_ids == cur) | (slc_ids == cur - 1)
        visible = (slc_ids * SLC_BLOCK)[None, :] <= t[:, None]
        imp = jnp.where(forced, BIG, jnp.where(visible, imp, NEG_INF))
        _, sel = lax.top_k(imp, n_sel)
        k_sel = k_slc[bidx, gidx, sel].reshape(B, G, Q_BLOCK, n_sel * SLC_BLOCK, dh)
        v_sel = v_slc[bidx, gidx, sel].reshape(B, G, Q_BLOCK, n_sel * SLC_BLOCK, dh)
        kpos = (sel[..., None] * SLC_BLOCK + jnp.arange(SLC_BLOCK)).reshape(B, G, Q_BLOCK, -1)
        dist_s = t[:, None] - kpos
        bias_s = jnp.moveaxis(table_g[gidx, _t5_bucket(dist_s)], -1, 2).astype(jnp.float32)
        s_s = jnp.einsum('bghqd,bgqkd->bghqk', qb, k_sel) + bias_s
        p_s = _masked_softmax(s_s, (dist_s >= 0)[:, :, None])
        o_s = jnp.einsum('bghqk,bgqkd->bghqd', p_s.astype(v_sel.dtype), v_sel)

        k_w = lax.dynamic_slice_in_dim(k_win, s0, WINDOW + Q_BLOCK, axis=2)
        v_w = lax.dynamic_slice_in_dim(v_win, s0, WINDOW + Q_BLOCK, axis=2)
        valid_w = band & ((s0 - WINDOW + kj) >= 0)[None, :]
        s_w = jnp.einsum('bghqd,bgkd->bghqk', qb, k_w) + bias_w
        p_w = _masked_softmax(s_w, valid_w)
        o_w = jnp.einsum('bghqk,bgkd->bghqd', p_w.astype(v_w.dtype), v_w)

        o = gb[..., 0:1] * o_c + gb[..., 1:2] * o_s + gb[..., 2:3] * o_w
        return o.astype(nq.dtype)

    o = lax.map(block, jnp.arange(n_qblk))
    return o.transpose(1, 0, 4, 2, 3, 5).reshape(B, T, NSA_HEADS * dh)

def cross_attn(hn, memn, wq, wk, wv, wo):
    B, T, _ = hn.shape
    M = memn.shape[1]
    q = (hn @ wq).reshape(B, T, XA_HEADS, XA_DH) * (XA_DH ** -0.5)
    k = (memn @ wk).reshape(B, M, XA_HEADS, XA_DH)
    v = (memn @ wv).reshape(B, M, XA_HEADS, XA_DH)
    s = jnp.einsum('bqhd,bmhd->bhqm', q, k).astype(jnp.float32)
    p = jax.nn.softmax(s, axis=-1).astype(v.dtype)
    o = jnp.einsum('bhqm,bmhd->bqhd', p, v).reshape(B, T, XA_HEADS * XA_DH)
    return o @ wo

def peer_ffn(hn, wq, subkeys, down, up):
    B, T, D = hn.shape
    N = B * T
    H, K = PEER_HEADS, PEER_TOPK
    xt = hn.reshape(N, D)
    q = (xt @ wq).reshape(N, H, 2, PEER_DKEY // 2)
    s = jnp.einsum('nhpd,hpkd->nhpk', q, subkeys).astype(jnp.float32)
    s_half, i_half = lax.top_k(s, K)
    cand_s = (s_half[:, :, 0, :, None] + s_half[:, :, 1, None, :]).reshape(N, H, K * K)
    cand_i = (i_half[:, :, 0, :, None] * PEER_NKEYS + i_half[:, :, 1, None, :]).reshape(N, H, K * K)
    top_s, pos = lax.top_k(cand_s, K)
    eidx = jnp.take_along_axis(cand_i, pos, axis=-1)
    gate = jax.nn.softmax(top_s, axis=-1)
    n_chunks = N // PEER_TOKEN_CHUNK

    def chunk(args):
        xc, ec, gc = args
        u = down[ec]
        act = jax.nn.gelu(jnp.einsum('cd,chkd->chk', xc, u).astype(jnp.float32)) * gc
        return jnp.einsum('chk,chkd->cd', act.astype(up.dtype), up[ec])

    y = lax.map(chunk, (xt.reshape(n_chunks, PEER_TOKEN_CHUNK, D),
                        eidx.reshape(n_chunks, PEER_TOKEN_CHUNK, H, K),
                        gate.reshape(n_chunks, PEER_TOKEN_CHUNK, H, K)))
    return y.reshape(B, T, D).astype(hn.dtype)

def first_inputs(seed: int = 0) -> dict:
    key = jax.random.key(seed)
    ks = jax.random.split(key, 32)
    f32 = jnp.float32
    L, D = DEPTH, D_MODEL

    def nrm(k, shape, scale):
        return jax.random.normal(k, shape, f32) * scale

    def gain(k, shape):
        return 1.0 + 0.02 * jax.random.normal(k, shape, f32)

    return {
        'x': nrm(ks[0], (BATCH, SEQ, D), 1.0),
        'mem': nrm(ks[1], (BATCH, MEM_LEN, D), 1.0),
        'rel_bias': nrm(ks[2], (REL_BUCKETS, NSA_HEADS), 0.5),
        'norm_mix': gain(ks[3], (L, D)),
        'w_in': nrm(ks[4], (L, D, IN_COLS), D ** -0.5),
        'gla_gate_w2': nrm(ks[5], (L, GLA_RANK, GLA_HEADS * GLA_DK), GLA_RANK ** -0.5),
        'gla_gate_b': nrm(ks[6], (L, GLA_HEADS * GLA_DK), 0.1),
        'gla_out_norm': gain(ks[7], (L, GLA_DV)),
        'cmp_pos_k': nrm(ks[8], (L, CMP_BLOCK, NSA_DH), 0.1),
        'cmp_pos_v': nrm(ks[9], (L, CMP_BLOCK, NSA_DH), 0.1),
        'cmp_k_w1': nrm(ks[10], (L, CMP_BLOCK * NSA_DH, CMP_HIDDEN), (CMP_BLOCK * NSA_DH) ** -0.5),
        'cmp_k_w2': nrm(ks[11], (L, CMP_HIDDEN, NSA_DH), CMP_HIDDEN ** -0.5),
        'cmp_v_w1': nrm(ks[12], (L, CMP_BLOCK * NSA_DH, CMP_HIDDEN), (CMP_BLOCK * NSA_DH) ** -0.5),
        'cmp_v_w2': nrm(ks[13], (L, CMP_HIDDEN, NSA_DH), CMP_HIDDEN ** -0.5),
        'w_out': nrm(ks[14], (L, D, D), D ** -0.5),
        'norm_xattn': gain(ks[15], (L, D)),
        'norm_mem': gain(ks[16], (L, D)),
        'xa_wq': nrm(ks[17], (L, D, D), D ** -0.5),
        'xa_wk': nrm(ks[18], (L, D, D), D ** -0.5),
        'xa_wv': nrm(ks[19], (L, D, D), D ** -0.5),
        'xa_wo': nrm(ks[20], (L, D, D), D ** -0.5),
        'norm_ffn': gain(ks[21], (L, D)),
        'peer_wq': nrm(ks[22], (L, D, PEER_HEADS * PEER_DKEY), D ** -0.5),
        'peer_subkeys': nrm(ks[23], (L, PEER_HEADS, 2, PEER_NKEYS, PEER_DKEY // 2), (PEER_DKEY // 2) ** -0.5),
        'peer_down': nrm(ks[24], (L, PEER_EXPERTS, D), D ** -0.5),
        'peer_up': nrm(ks[25], (L, PEER_EXPERTS, D), PEER_HEADS ** -0.5),
        'norm_final': gain(ks[26], (D,)),
    }

def first_block(x, mem, rel_bias, norm_mix, w_in, gla_gate_w2, gla_gate_b, gla_out_norm,
              cmp_pos_k, cmp_pos_v, cmp_k_w1, cmp_k_w2, cmp_v_w1, cmp_v_w2, w_out,
              norm_xattn, norm_mem, xa_wq, xa_wk, xa_wv, xa_wo,
              norm_ffn, peer_wq, peer_subkeys, peer_down, peer_up, norm_final):
    h = x
    for l in range(DEPTH):
        hn = rms_norm(h, norm_mix[l])
        (gq, gk, gv, gr, glr, nq, kc, vc, ks_, vs_, kw, vw, ng) = _split_cols(hn @ w_in[l])
        o_gla = gla_mixer(gq, gk, gv, gr, glr, gla_gate_w2[l], gla_gate_b[l], gla_out_norm[l])
        o_nsa = nsa_mixer(nq, kc, vc, ks_, vs_, kw, vw, ng, rel_bias,
                          cmp_pos_k[l], cmp_pos_v[l], cmp_k_w1[l], cmp_k_w2[l], cmp_v_w1[l], cmp_v_w2[l])
        h = h + jnp.concatenate([o_gla, o_nsa], axis=-1) @ w_out[l]
        h = h + cross_attn(rms_norm(h, norm_xattn[l]), rms_norm(mem, norm_mem[l]),
                           xa_wq[l], xa_wk[l], xa_wv[l], xa_wo[l])
        h = h + peer_ffn(rms_norm(h, norm_ffn[l]), peer_wq[l], peer_subkeys[l], peer_down[l], peer_up[l])
    return rms_norm(h, norm_final)


HGRN_HEADS = 8
HGRN_DK = 128
HGRN_DV = D_MODEL // HGRN_HEADS
HGRN_KEY_WIDTH = HGRN_HEADS * HGRN_DK
HGRN_WIDTH = HGRN_HEADS * HGRN_DV
HGRN_CHUNK = 64

HYENA_WIDTH = D_MODEL
HYENA_SHORT = 3
HYENA_BANDS = 16
HYENA_EMB = 1 + 2 * HYENA_BANDS
HYENA_FILTER_HIDDEN = 64
HYENA_MIN_DECAY = -math.log(1e-2) / 1.5
HYENA_MAX_DECAY = -math.log(1e-2) / 0.3

PEER_EXPERTS_2 = PEER_NKEYS * PEER_NKEYS
PEER_QDIM = 256
PEER_TOKEN_BLOCK = 128

N_BRANCHES = 2
IN_SPLITS = (HGRN_KEY_WIDTH, 2 * HGRN_KEY_WIDTH, 3 * HGRN_KEY_WIDTH,
             3 * HGRN_KEY_WIDTH + HGRN_WIDTH, 3 * HGRN_KEY_WIDTH + 2 * HGRN_WIDTH,
             3 * HGRN_KEY_WIDTH + 2 * HGRN_WIDTH + 3 * HYENA_WIDTH)
IN_COLS_2 = 3 * HGRN_KEY_WIDTH + 2 * HGRN_WIDTH + 3 * HYENA_WIDTH + N_BRANCHES * D_MODEL
RMS_EPS = 1e-6


def rmsnorm(x, g):
    xf = x.astype(jnp.float32)
    y = xf * lax.rsqrt(jnp.mean(xf * xf, axis=-1, keepdims=True) + RMS_EPS)
    return (y * g.astype(jnp.float32)).astype(x.dtype)

def hgrn2_chunk_scan(q, k, logf, v):
    n, s, h, dk = q.shape
    dv = v.shape[-1]
    nc = s // HGRN_CHUNK

    def to_chunks(a):
        return a.reshape(n, nc, HGRN_CHUNK, h, a.shape[-1]).transpose(1, 0, 3, 2, 4)

    qc, kc, fc, vc = to_chunks(q), to_chunks(k), to_chunks(logf), to_chunks(v)
    incl = jnp.tril(jnp.ones((HGRN_CHUNK, HGRN_CHUNK), dtype=bool))[:, :, None]

    def step(state, inp):
        qb, kb, fb, vb = inp
        b = jnp.cumsum(fb, axis=2)
        b_last = b[:, :, -1:, :]
        inter = jnp.einsum('nhtk,nhkv->nhtv', qb * jnp.exp(b), state)
        diff = b[:, :, :, None, :] - b[:, :, None, :, :]
        decay = jnp.exp(jnp.where(incl, diff, -jnp.inf))
        scores = jnp.einsum('nhtk,nhsk,nhtsk->nhts', qb, kb, decay)
        intra = jnp.einsum('nhts,nhsv->nhtv', scores, vb)
        new_state = (jnp.exp(b_last[:, :, 0, :, None]) * state
                     + jnp.einsum('nhsk,nhsv->nhkv', kb * jnp.exp(b_last - b), vb))
        return new_state, inter + intra

    s0 = jnp.zeros((n, h, dk, dv), jnp.float32)
    _, out = lax.scan(step, s0, (qc, kc, fc, vc))
    return out.transpose(1, 0, 3, 2, 4).reshape(n, s, h, dv)

def centred_short_conv(x, w, b):
    L = x.shape[1]
    pad = HYENA_SHORT // 2
    xp = jnp.pad(x, ((0, 0), (pad, pad), (0, 0)))
    y = b
    for j in range(HYENA_SHORT):
        y = y + xp[:, j:j + L] * w[j]
    return y

def hyena_filters(seq_len, w1, b1, freq1, w2, b2, freq2, w3, decay_rate):
    f32 = jnp.float32
    pos = jnp.arange(seq_len, dtype=f32)
    t = pos / max(seq_len - 1, 1)
    bands = jnp.linspace(1e-4, HYENA_BANDS - 1, HYENA_BANDS, dtype=f32)
    ang = (2.0 * math.pi / seq_len) * pos[:, None] * bands[None, :]
    z = jnp.concatenate([t[:, None], jnp.cos(ang), -jnp.sin(ang)], axis=-1)
    hid = jnp.sin(freq1.astype(f32) * (z @ w1.astype(f32) + b1.astype(f32)))
    hid = jnp.sin(freq2.astype(f32) * (hid @ w2.astype(f32) + b2.astype(f32)))
    filt = (hid @ w3.astype(f32)) * jnp.exp(-t[:, None] * jnp.abs(decay_rate.astype(f32))[None, :])
    return filt[:, :HYENA_WIDTH], filt[:, HYENA_WIDTH:]

def bidirectional_fftconv(u, h_fwd, h_bwd, bias):
    L = u.shape[1]
    kern = jnp.concatenate([h_fwd, jnp.zeros_like(h_fwd[:1]), h_bwd[1:][::-1]], axis=0)
    uf32 = u.astype(jnp.float32)
    uf = jnp.fft.rfft(uf32, n=2 * L, axis=1)
    kf = jnp.fft.rfft(kern, n=2 * L, axis=0)
    y = jnp.fft.irfft(uf * kf[None], n=2 * L, axis=1)[:, :L]
    return (y + uf32 * bias.astype(jnp.float32)).astype(u.dtype)

def hybrid_mixer(xn, w_in, lb, hgrn_norm_g, conv_w, conv_b, filt_w1, filt_b1, filt_freq1,
                 filt_w2, filt_b2, filt_freq2, filt_w3, filt_decay, hyena_bias,
                 w_branch_a, w_branch_b, w_out):
    B, L, _ = xn.shape
    f32 = jnp.float32
    proj = jnp.einsum('bld,dc->blc', xn, w_in)
    q, zf_fwd, zf_bwd, inp, og, hy, gates = jnp.split(proj, IN_SPLITS, axis=-1)

    def heads(a, d):
        return a.astype(f32).reshape(B, L, HGRN_HEADS, d)

    lbh = lb.reshape(HGRN_HEADS, HGRN_DK)

    def forget(z):
        zh = heads(z, HGRN_DK)
        logf = jnp.log(lbh + (1.0 - lbh) * jax.nn.sigmoid(zh))
        k = (1.0 - lbh) * jax.nn.sigmoid(-zh)
        return logf, k

    logf_f, k_f = forget(zf_fwd)
    logf_b, k_b = forget(zf_bwd)
    qh = jax.nn.silu(heads(q, HGRN_DK))
    vh = heads(inp, HGRN_DV)
    rev = lambda a: a[:, ::-1]
    o2 = hgrn2_chunk_scan(jnp.concatenate([qh, rev(qh)], axis=0),
                          jnp.concatenate([k_f, rev(k_b)], axis=0),
                          jnp.concatenate([logf_f, rev(logf_b)], axis=0),
                          jnp.concatenate([vh, rev(vh)], axis=0))
    o = o2[:B] + rev(o2[B:])
    o = rmsnorm(o, hgrn_norm_g).reshape(B, L, HGRN_WIDTH)
    y_a = jnp.einsum('blc,cd->bld', (o * jax.nn.silu(og.astype(f32))).astype(xn.dtype), w_branch_a)

    hy = centred_short_conv(hy, conv_w, conv_b)
    x0, x1, v = jnp.split(hy, 3, axis=-1)
    h_f, h_b = hyena_filters(L, filt_w1, filt_b1, filt_freq1, filt_w2, filt_b2, filt_freq2,
                             filt_w3, filt_decay)
    y_b = x0 * bidirectional_fftconv(v * x1, h_f, h_b, hyena_bias)
    y_b = jnp.einsum('blc,cd->bld', y_b, w_branch_b)

    g_a, g_b = jnp.split(gates, N_BRANCHES, axis=-1)
    merged = jax.nn.sigmoid(g_a) * y_a + jax.nn.sigmoid(g_b) * y_b
    return jnp.einsum('bld,de->ble', merged, w_out)

def peer_ffn_2(xn, w_q, subkeys, u_tab, v_tab):
    B, L, D = xn.shape
    blocks = xn.reshape(-1, PEER_TOKEN_BLOCK, D)
    sk = subkeys.astype(jnp.float32)

    def block(xb):
        T = xb.shape[0]
        qh = (xb @ w_q).astype(jnp.float32).reshape(T, PEER_HEADS, 2, PEER_QDIM // 2)
        s = jnp.einsum('thpc,hpnc->thpn', qh, sk)
        s1, i1 = lax.top_k(s[:, :, 0], PEER_TOPK)
        s2, i2 = lax.top_k(s[:, :, 1], PEER_TOPK)
        cand_s = (s1[..., :, None] + s2[..., None, :]).reshape(T, PEER_HEADS, PEER_TOPK * PEER_TOPK)
        cand_i = (i1[..., :, None] * PEER_NKEYS + i2[..., None, :]).reshape(T, PEER_HEADS, PEER_TOPK * PEER_TOPK)
        top_s, pos = lax.top_k(cand_s, PEER_TOPK)
        experts = jnp.take_along_axis(cand_i, pos, axis=-1)
        g = jax.nn.softmax(top_s, axis=-1).astype(xb.dtype)
        u = jnp.take(u_tab, experts, axis=0)
        v = jnp.take(v_tab, experts, axis=0)
        act = jax.nn.gelu(jnp.einsum('td,thkd->thk', xb, u)) * g
        return jnp.einsum('thk,thkd->td', act, v)

    return lax.map(block, blocks).reshape(B, L, D)

def second_inputs(seed: int = 0) -> dict:
    key = jax.random.key(seed)
    ks = jax.random.split(key, 26)

    def nrm(k, shape, scale):
        return jax.random.normal(k, shape, jnp.float32) * scale

    decay_base = jnp.linspace(HYENA_MIN_DECAY, HYENA_MAX_DECAY, 2 * HYENA_WIDTH, dtype=jnp.float32)
    return {
        "x": nrm(ks[0], (BATCH, SEQ, D_MODEL), 1.0),
        "norm_mix_g": 1.0 + nrm(ks[1], (DEPTH, D_MODEL), 0.02),
        "w_in": nrm(ks[2], (DEPTH, D_MODEL, IN_COLS_2), D_MODEL ** -0.5),
        "hgrn_lb_logits": nrm(ks[3], (DEPTH + 1, HGRN_KEY_WIDTH), 0.1),
        "hgrn_norm_g": 1.0 + nrm(ks[4], (DEPTH, HGRN_DV), 0.02),
        "hyena_conv_w": nrm(ks[5], (DEPTH, HYENA_SHORT, 3 * HYENA_WIDTH), HYENA_SHORT ** -0.5),
        "hyena_conv_b": nrm(ks[6], (DEPTH, 3 * HYENA_WIDTH), 0.02),
        "filt_w1": nrm(ks[7], (DEPTH, HYENA_EMB, HYENA_FILTER_HIDDEN), HYENA_EMB ** -0.5),
        "filt_b1": nrm(ks[8], (DEPTH, HYENA_FILTER_HIDDEN), 0.1),
        "filt_freq1": 1.0 + nrm(ks[9], (DEPTH, HYENA_FILTER_HIDDEN), 0.02),
        "filt_w2": nrm(ks[10], (DEPTH, HYENA_FILTER_HIDDEN, HYENA_FILTER_HIDDEN), HYENA_FILTER_HIDDEN ** -0.5),
        "filt_b2": nrm(ks[11], (DEPTH, HYENA_FILTER_HIDDEN), 0.1),
        "filt_freq2": 1.0 + nrm(ks[12], (DEPTH, HYENA_FILTER_HIDDEN), 0.02),
        "filt_w3": nrm(ks[13], (DEPTH, HYENA_FILTER_HIDDEN, 2 * HYENA_WIDTH), 0.02 * HYENA_FILTER_HIDDEN ** -0.5),
        "filt_decay": decay_base[None, :] + nrm(ks[14], (DEPTH, 2 * HYENA_WIDTH), 0.1),
        "hyena_bias": nrm(ks[15], (DEPTH, HYENA_WIDTH), 0.1),
        "w_branch_a": nrm(ks[16], (DEPTH, HGRN_WIDTH, D_MODEL), HGRN_WIDTH ** -0.5),
        "w_branch_b": nrm(ks[17], (DEPTH, HYENA_WIDTH, D_MODEL), HYENA_WIDTH ** -0.5),
        "w_out": nrm(ks[18], (DEPTH, D_MODEL, D_MODEL), D_MODEL ** -0.5),
        "norm_ffn_g": 1.0 + nrm(ks[19], (DEPTH, D_MODEL), 0.02),
        "peer_w_q": nrm(ks[20], (DEPTH, D_MODEL, PEER_HEADS * PEER_QDIM), D_MODEL ** -0.5),
        "peer_subkeys": nrm(ks[21], (DEPTH, PEER_HEADS, 2, PEER_NKEYS, PEER_QDIM // 2), (PEER_QDIM // 2) ** -0.5),
        "peer_u": nrm(ks[22], (DEPTH, PEER_EXPERTS_2, D_MODEL), D_MODEL ** -0.5),
        "peer_v": nrm(ks[23], (DEPTH, PEER_EXPERTS_2, D_MODEL), 0.2),
        "norm_final_g": 1.0 + nrm(ks[24], (D_MODEL,), 0.02),
    }

def second_block(x, norm_mix_g, w_in, hgrn_lb_logits, hgrn_norm_g, hyena_conv_w, hyena_conv_b,
              filt_w1, filt_b1, filt_freq1, filt_w2, filt_b2, filt_freq2, filt_w3, filt_decay,
              hyena_bias, w_branch_a, w_branch_b, w_out, norm_ffn_g, peer_w_q, peer_subkeys,
              peer_u, peer_v, norm_final_g):
    lb_table = jnp.cumsum(jax.nn.softmax(hgrn_lb_logits.astype(jnp.float32), axis=0), axis=0)
    h = x
    for layer in range(DEPTH):
        h = h + hybrid_mixer(rmsnorm(h, norm_mix_g[layer]), w_in[layer], lb_table[layer],
                             hgrn_norm_g[layer], hyena_conv_w[layer], hyena_conv_b[layer],
                             filt_w1[layer], filt_b1[layer], filt_freq1[layer],
                             filt_w2[layer], filt_b2[layer], filt_freq2[layer],
                             filt_w3[layer], filt_decay[layer], hyena_bias[layer],
                             w_branch_a[layer], w_branch_b[layer], w_out[layer])
        h = h + peer_ffn_2(rmsnorm(h, norm_ffn_g[layer]), peer_w_q[layer], peer_subkeys[layer],
                         peer_u[layer], peer_v[layer])
    return rmsnorm(h, norm_final_g)


def setup_inputs(seed=0):
    out = dict(first_inputs(seed))
    for name, value in second_inputs(seed + 1).items():
        if name != "x":
            out[name + "_2"] = value
    return out


def reference(
    x, mem, rel_bias, norm_mix, w_in, gla_gate_w2, gla_gate_b, gla_out_norm, cmp_pos_k,
    cmp_pos_v, cmp_k_w1, cmp_k_w2, cmp_v_w1, cmp_v_w2, w_out, norm_xattn, norm_mem, xa_wq,
    xa_wk, xa_wv, xa_wo, norm_ffn, peer_wq, peer_subkeys, peer_down, peer_up, norm_final,
    norm_mix_g_2, w_in_2, hgrn_lb_logits_2, hgrn_norm_g_2, hyena_conv_w_2, hyena_conv_b_2,
    filt_w1_2, filt_b1_2, filt_freq1_2, filt_w2_2, filt_b2_2, filt_freq2_2, filt_w3_2,
    filt_decay_2, hyena_bias_2, w_branch_a_2, w_branch_b_2, w_out_2, norm_ffn_g_2, peer_w_q_2,
    peer_subkeys_2, peer_u_2, peer_v_2, norm_final_g_2,
):
    x = first_block(
        x, mem, rel_bias, norm_mix, w_in, gla_gate_w2, gla_gate_b, gla_out_norm, cmp_pos_k,
        cmp_pos_v, cmp_k_w1, cmp_k_w2, cmp_v_w1, cmp_v_w2, w_out, norm_xattn, norm_mem, xa_wq,
        xa_wk, xa_wv, xa_wo, norm_ffn, peer_wq, peer_subkeys, peer_down, peer_up, norm_final,
    )
    return second_block(
        x, norm_mix_g_2, w_in_2, hgrn_lb_logits_2, hgrn_norm_g_2, hyena_conv_w_2,
        hyena_conv_b_2, filt_w1_2, filt_b1_2, filt_freq1_2, filt_w2_2, filt_b2_2, filt_freq2_2,
        filt_w3_2, filt_decay_2, hyena_bias_2, w_branch_a_2, w_branch_b_2, w_out_2,
        norm_ffn_g_2, peer_w_q_2, peer_subkeys_2, peer_u_2, peer_v_2, norm_final_g_2,
    )


_drawn_inputs = setup_inputs


def setup_inputs(seed=0):
    import zlib

    import numpy as np

    out = dict(_drawn_inputs(seed))
    spreads = {}
    factors = {'cmp_pos_k': 3.948,
     'norm_xattn': 5.137,
     'norm_mem': 4.408,
     'norm_mix_g_2': 4.223,
     'hgrn_lb_logits_2': 7.907,
     'hgrn_norm_g_2': 21.767,
     'hyena_conv_b_2': 27.736,
     'filt_b1_2': 7.199,
     'filt_freq1_2': 8.0,
     'filt_b2_2': 5.998,
     'filt_freq2_2': 27.942,
     'filt_decay_2': 4.368,
     'norm_ffn_g_2': 31.128,
     'norm_final_g_2': 22.975,
     'norm_ffn': 4.978}
    for name, (base, spread) in spreads.items():
        noise = np.random.default_rng([zlib.crc32(name.encode()), seed]).standard_normal(out[name].shape)
        drawn = base * np.exp(spread * noise) if base else spread * noise
        out[name] = jnp.asarray(drawn.astype(out[name].dtype))
    for name, factor in factors.items():
        out[name] = (out[name] * factor).astype(out[name].dtype)
    return out
```

```python
from contextlib import ExitStack

import concourse.bass as bass
from concourse import mybir
import numpy as np

T, D, P = 256, 1024, 128
NT, KD = T // P, D // P
EPS = 1e-6
NEG_INF = -1e30
GLA_H, GLA_DK, GLA_RANK = 4, 64, 16
GLA_TAU = 16.0
NSA_H, NSA_G, NSA_DH = 8, 2, 64
HPG = NSA_H // NSA_G
CMP_BLOCK, CMP_STRIDE, CMP_HIDDEN = 32, 16, 128
N_CMP = (T - CMP_BLOCK) // CMP_STRIDE + 1
BUCKETS, MAX_DIST = 32, 2048
XA_H, XA_DH = 4, D // 4
PEER_H, NKEYS, TOPK = 8, 128, 16
HG_H = 8
BANDS = 16
EMB = 1 + 2 * BANDS
FILT_H = 64
LEVELS = [64, 32, 16, 8, 4, 2, 1]

F32 = mybir.dt.float32
U32 = mybir.dt.uint32
ALU = mybir.AluOpType
ACT = mybir.ActivationFunctionType
AX = mybir.AxisListType.X

GAINS = {}
_at = 0
for _name, _width in [("norm_mix", 8), ("norm_xattn", 8), ("norm_mem", 8), ("norm_ffn", 8), ("norm_final", 8),
                      ("gla_gate_b", 2), ("gla_out_norm", 1), ("norm_mix_g_2", 8), ("lb", 16), ("hgrn_norm_g_2", 1),
                      ("conv_w", 72), ("conv_b", 24), ("hyena_bias_2", 8), ("norm_ffn_g_2", 8), ("norm_final_g_2", 8)]:
    GAINS[_name] = (_at, _at + _width)
    _at += _width
N_GAINS = _at


class Queue:

    def __init__(self, sem, one_at_a_time):
        self.items, self.sem, self.count, self.seen = [], sem, 0, {}
        self.one_at_a_time = one_at_a_time

    def wait(self, marks):
        for sem, value in marks:
            if value > self.seen.get(sem.name, 0):
                self.seen[sem.name] = value
                self.items.append([lambda e, sem=sem, value=value: e.wait_ge(sem, value), None, 0])

    def do(self, build, after=()):
        if self.one_at_a_time and self.count:
            self.wait([(self.sem, self.count)])
        self.wait(after)
        self.tail = [build, None, 0]
        self.items.append(self.tail)
        if self.one_at_a_time:
            return self.last

    @property
    def last(self):
        if self.tail[1] is None:
            self.count += 1
            self.tail[1], self.tail[2] = self.sem, 1
        return (self.sem, self.count)

    def play(self, engine):
        for build, sem, by in self.items:
            ins = build(engine)
            if sem is not None:
                ins.then_inc(sem, by)


def tt(q, out, a, b, op, after=()):
    return q.do(lambda e: e.tensor_tensor(out, a, b, op), after)


def ts(q, out, a, s1, op0, s2=None, op1=None, after=()):
    if op1 is None:
        return q.do(lambda e: e.tensor_scalar(out, a, s1, None, op0), after)
    return q.do(lambda e: e.tensor_scalar(out, a, s1, s2, op0, op1), after)


def stt(q, out, a, s, b, op0, op1, after=()):
    return q.do(lambda e: e.scalar_tensor_tensor(out=out, in0=a, scalar=s, in1=b, op0=op0, op1=op1), after)


def copy(q, out, a, after=()):
    return q.do(lambda e: e.tensor_copy(out, a), after)


def fill(q, out, value, after=()):
    return q.do(lambda e: e.memset(out, value), after)


def reduce(q, out, a, op, after=()):
    return q.do(lambda e: e.tensor_reduce(out, a, AX, op), after)


def recip(q, out, a, after=()):
    return q.do(lambda e: e.reciprocal(out, a), after)


def act(q, out, a, func, scale=1.0, bias=0.0, after=()):
    return q.do(lambda e: e.activation(out, a, func, bias=bias, scale=scale), after)


def mm(q, out, lhsT, rhs, start=True, stop=True, after=()):
    return q.do(lambda e: e.matmul(out, lhsT, rhs, start=start, stop=stop), after)


def tr(q, out, a, ident, after=()):
    return q.do(lambda e: e.transpose(out, a, ident), after)


def over(ap, n, axis):
    shape = list(ap.shape)
    return ap.unsqueeze(axis).broadcast_to(shape[:axis] + [n] + shape[axis:])


def t5_bucket(dist):
    n = np.maximum(dist, 0)
    exact = BUCKETS // 2
    ratio = np.log(np.maximum(n, 1).astype(np.float32) / np.float32(exact)) / np.float32(np.log(MAX_DIST / exact))
    large = np.minimum(exact + (ratio * (BUCKETS - exact)).astype(np.int32), BUCKETS - 1)
    return np.where(n < exact, n, large)


def constants():
    f = np.float32
    c = {}
    c["ident"] = np.eye(P, dtype=f)
    s, t = np.meshgrid(np.arange(P), np.arange(P), indexing="ij")
    masks = []
    for causal in (True, False):
        for m in LEVELS:
            same = s // (2 * m) == t // (2 * m)
            s2, t2 = s // m % 2, t // m % 2
            masks.append(same & ((s2 == 0) & (t2 == 1) if causal else s2 != t2))
    c["masks"] = np.stack([x.astype(f) for x in masks], 1)
    c["reset"] = np.tile((np.arange(T) % P != 0).astype(f), (P, 1))
    dist = np.arange(2 * T) - (T - 1)
    c["bucket_of_dist"] = (t5_bucket(dist)[None, :] == np.arange(BUCKETS)[:, None]).astype(f)
    c["some_block"] = (np.arange(P) >= CMP_BLOCK - 1).astype(f)[:, None]
    c["iota"] = np.tile(np.arange(P, dtype=f), (P, 1))
    j, s = np.meshgrid(np.arange(T), np.arange(T), indexing="ij")
    angle = np.pi * (((2 * j + 1) * s) % (4 * T)) / (2 * T)
    for name, m in (("cos", np.cos(angle)), ("sin", np.sin(angle))):
        c[name + "_js"] = m.astype(f).reshape(NT, P, T).transpose(1, 0, 2)
        c[name + "_sj"] = m.T.astype(f).reshape(NT, P, T).transpose(1, 0, 2)
    pos = np.arange(T, dtype=f)
    tt_ = (pos / f(T - 1)).astype(f)
    bands = np.linspace(1e-4, BANDS - 1, BANDS, dtype=f)
    ang = (f(2.0 * np.pi / T) * pos[:, None] * bands[None, :]).astype(f)
    c["filter_z"] = np.concatenate([tt_[:, None], np.cos(ang), -np.sin(ang)], 1).T.astype(f)
    c["minus_t"] = (-tt_).reshape(NT, P).T
    c["not_first"] = (pos > 0).astype(f).reshape(NT, P).T
    return {k: np.ascontiguousarray(v) for k, v in c.items()}


class Core:

    SLOTS = 10

    def __init__(self, nc, ctx, dram):
        self.nc, self.ctx, self.dram = nc, ctx, dram
        self.V = Queue(self.sem("vector_done"), True)
        self.S = Queue(self.sem("scalar_done"), True)
        self.G = Queue(self.sem("gpsimd_done"), True)
        self.PE = Queue(self.sem("tensor_done"), False)
        self.DMA = Queue(self.sem("sync_done"), False)
        self.psum = ctx.enter_context(nc.psum_tensor("psum", [P, 4096], F32))
        self.bank_read = [[] for _ in range(8)]
        self.ring = self.sb("weight_ring", [P, self.SLOTS, 1024])
        self.ring_sem = [self.sem(f"slot_loaded_{i}") for i in range(self.SLOTS)]
        self.slot_read = [[] for _ in range(self.SLOTS)]
        self.units = 0
        self.n_small = 0
        self.next_bank = 0

    def sem(self, name):
        return self.ctx.enter_context(self.nc.semaphore(name))

    def sb(self, name, shape, ctx=None):
        return (ctx or self.ctx).enter_context(self.nc.sbuf_tensor(name, shape, F32))

    def bank(self, b, n=1):
        return self.psum[:, 512 * b:512 * (b + n)]

    def load(self, out, src, after=()):
        sem = self.sem(f"loaded_{self.n_small}")
        self.n_small += 1
        self.DMA.wait(after)
        self.DMA.items.append([lambda e: e.dma_start(out, src), sem, 16])
        return (sem, 16)

    def unit(self, src):
        slot, turn = self.units % self.SLOTS, self.units // self.SLOTS
        self.units += 1
        self.DMA.wait(self.slot_read[slot])
        out = self.ring[:, slot, :]
        self.DMA.items.append([lambda e: e.dma_start(out, src), self.ring_sem[slot], 16])
        return slot, (self.ring_sem[slot], 16 * (turn + 1))

    def barrier(self):
        marks = [q.last for q in (self.V, self.S, self.G, self.PE)]
        for q in (self.V, self.S, self.G, self.PE, self.DMA):
            q.wait(marks)

    def take_bank(self):
        b = self.next_bank
        self.next_bank = (b + 1) % 8
        return b

    def channels(self, src, acts, evac, after=(), cols=P):
        slot, came = self.unit(src)
        w = self.ring[:, slot, :].rearrange("p (k c) -> p k c", k=KD)
        b = self.take_bank()
        out = self.bank(b)[:, 0:T]
        self.PE.wait([came] + self.bank_read[b] + list(after))
        for k in range(KD):
            mm(self.PE, out, w[:, k, :], acts[:, k, :], k == 0, k == KD - 1)
        self.slot_read[slot] = [self.PE.last]
        self.bank_read[b] = [evac(out, self.PE.last)]

    def tokens(self, src, acts, evac, after=()):
        slot, came = self.unit(src)
        w = self.ring[:, slot, :].rearrange("p (k c) -> p k c", k=KD)
        b = self.take_bank()
        out = self.bank(b)[:, 0:NT * P].rearrange("p (i c) -> p i c", i=NT)
        self.PE.wait([came] + self.bank_read[b] + list(after))
        for i in range(NT):
            for k in range(KD):
                mm(self.PE, out[:, i, :], acts[:, k, P * i:P * (i + 1)], w[:, k, :], k == 0, k == KD - 1)
        self.slot_read[slot] = [self.PE.last]
        self.bank_read[b] = [evac(out, self.PE.last)]

    def rstd(self, total_bank, n, tmp, after):
        out = self.bank(total_bank)[:, 0:T]
        m = ts(self.V, tmp, out, 1.0 / n, ALU.mult, EPS, ALU.add, after=after)
        self.bank_read[total_bank] = [m]
        m = act(self.S, tmp, tmp, ACT.Sqrt, after=[m])
        return recip(self.V, tmp, tmp, after=[m])

    def rmsnorm(self, x, gain, out, work, tmp, after=()):
        m = act(self.S, work[:, :, :], x[:, :, :], ACT.Square, after=list(after) + [self.V.last])
        b = self.take_bank()
        self.PE.wait([m] + self.bank_read[b])
        for k in range(KD):
            mm(self.PE, self.bank(b)[:, 0:T], self.ones[:, :], work[:, k, :], k == 0, k == KD - 1)
        self.rstd(b, D, tmp[:, :], [self.PE.last])
        for k in range(KD):
            m = stt(self.V, out[:, k, :], x[:, k, :], gain[:, k:k + 1], tmp[:, :], ALU.mult, ALU.mult,
                    after=list(after))
        return m

    def softmax(self, s, e, mx, z, heads, n, coef=None):
        reduce(self.V, mx, s, ALU.max)
        m = tt(self.V, s, s, over(mx, n, 2), ALU.subtract)
        m = act(self.S, e, s, ACT.Exp, after=[m])
        reduce(self.V, z, e, ALU.add, after=[m])
        m = recip(self.V, z, z)
        if coef is not None:
            m = tt(self.V, z, z, coef, ALU.mult)
        return tt(self.G, e, e, over(z, n, 2), ALU.mult, after=[m])


def halves(ap, m):
    if len(ap.shape) == 3:
        ap = ap.rearrange("p a t -> p (a t)")
    return ap.rearrange("p (b h m) -> p b h m", h=2, m=m)


def gla(c, ctx, q, k, gate, v, gr, out_gain, o, started):
    V, S, G, PE = c.V, c.S, c.G, c.PE
    b = c.sb("gla_b", [P, 2, T], ctx)
    e = c.sb("gla_e", [P, 2, T], ctx)
    qq = c.sb("gla_qq", [P, 2, 2, T], ctx)
    kk = c.sb("gla_kk", [P, 2, 2, T], ctx)
    at = c.sb("gla_scores", [P, 2, 2, NT, P], ctx)
    across = c.sb("gla_scores_across", [P, 2, 2, P], ctx)
    fill(G, at[:, :, :, :, :], 0.0)
    for j in range(2):
        V.do(lambda e_, j=j: e_.tensor_tensor_scan(b[:, j, :], c.reset[:, :], gate[:, j, :], 0.0, ALU.mult, ALU.add),
             after=started)
    read = [[], []]
    merged = G.last
    for n, m in enumerate([P] + LEVELS + [0]):
        u = n % 2
        if m:
            bb, ee = halves(b[:, :, :], m), halves(e[:, :, :], m)
            if m == P:
                a = tt(V, ee[:, :, 0, :], bb[:, :, 0, :], over(bb[:, :, 0, m - 1], m, 2), ALU.subtract)
                a = copy(V, ee[:, :, 1, :], bb[:, :, 1, :])
            else:
                ref = bb[:, :, 0, m - 1]
                a = tt(V, ee[:, :, 0, :], bb[:, :, 0, :], over(ref, m, 2), ALU.subtract)
                a = tt(V, ee[:, :, 1, :], bb[:, :, 1, :], over(ref, m, 2), ALU.subtract)
            a = act(S, e[:, :, :], e[:, :, :], ACT.Abs, after=[a])
            a = act(S, e[:, :, :], e[:, :, :], ACT.Exp, scale=-1.0)
            tt(V, qq[:, u, :, :], q[:, :, :], e[:, :, :], ALU.mult, after=[a] + read[u])
            a = tt(V, kk[:, u, :, :], k[:, :, :], e[:, :, :], ALU.mult)
            ql, kl = qq[:, u, :, :], kk[:, u, :, :]
            PE.wait([a])
        else:
            ql, kl = q, k
        pair = 2 * (n % 4)
        PE.wait(c.bank_read[pair] + c.bank_read[pair + 1])
        for r in range(2):
            rows = slice(64 * r, 64 * r + 64)
            for j in range(2):
                if m == P:
                    mm(PE, c.bank(pair + r)[:, P * j:P * j + P], kl[rows, j, 0:P], ql[rows, j, P:T])
                else:
                    for i in range(NT):
                        tile = slice(P * i, P * i + P)
                        col = P * (2 * j + i)
                        mm(PE, c.bank(pair + r)[:, col:col + P], kl[rows, j, tile], ql[rows, j, tile])
        read[u] = [PE.last]
        src = c.bank(pair, 2).rearrange("p (r x) -> p r x", r=2)
        if m == P:
            a = copy(V, across[:, :, :, :].rearrange("p r j t -> p r (j t)"), src[:, :, 0:2 * P], after=[PE.last])
        else:
            mask = c.masks[:, n - 1, :] if m else c.ident[:, :]
            a = V.do(lambda e_, mask=mask, pair=pair: e_.copy_predicated(
                at[:, :, :, :, :].rearrange("p r j i t -> p (r j i) t"), over(mask.bitcast(U32), 8, 1),
                c.bank(pair, 2).rearrange("p (x t) -> p x t", t=P)), after=[PE.last, merged])
        c.bank_read[pair] = c.bank_read[pair + 1] = [a]
    sq = c.sb("gla_sq", [P, GLA_H, T], ctx)
    tmp = c.sb("gla_tmp", [P, T], ctx)
    act(S, gr[:, :, :], gr[:, :, :], ACT.Silu)
    for h in range(GLA_H):
        j, r = h // 2, h % 2
        bk = c.take_bank()
        PE.wait([a] + c.bank_read[bk])
        vh = v[:, :, P * h:P * h + P]
        mm(PE, c.bank(bk)[:, 0:P], vh[:, 0, :], at[:, r, j, 0, :])
        mm(PE, c.bank(bk)[:, P:T], vh[:, 0, :], across[:, r, j, :], True, False)
        mm(PE, c.bank(bk)[:, P:T], vh[:, 1, :], at[:, r, j, 1, :], False, True)
        c.bank_read[bk] = [act(S, o[:, h, :], c.bank(bk)[:, 0:T], ACT.Copy, after=[PE.last])]
    head_norm(c, o, GLA_H, sq, tmp, out_gain, gr)


def head_norm(c, o, heads, sq, tmp, gain, gated):
    m = act(c.S, sq[:, :, :], o[:, :, :], ACT.Square)
    for h in range(heads):
        bk = c.take_bank()
        mm(c.PE, c.bank(bk)[:, 0:T], c.ones[:, :], sq[:, h, :], after=[m] + c.bank_read[bk])
        c.rstd(bk, P, tmp[:, :], [c.PE.last])
        stt(c.V, o[:, h, :], o[:, h, :], gain, tmp[:, :], ALU.mult, ALU.mult)
        tt(c.V, o[:, h, :], o[:, h, :], gated[:, h, :], ALU.mult)


def compress(c, ctx, name, kv, kv_done, pos_src, w1_src):
    V, S, PE = c.V, c.S, c.PE
    w1 = c.sb(name + "_w1", [P, CMP_BLOCK, CMP_HIDDEN], ctx)
    pos = c.sb(name + "_pos", [P, CMP_BLOCK], ctx)
    blocks = c.sb(name + "_blocks", [P, CMP_BLOCK, N_CMP], ctx)
    hid = c.sb(name + "_hid", [P, NSA_G, N_CMP], ctx)
    w1_came = [c.load(w1[64 * g:64 * g + 64, :, :], w1_src) for g in range(NSA_G)]
    pos_came = [c.load(pos[64 * g:64 * g + 64, :], pos_src) for g in range(NSA_G)]
    width = CMP_STRIDE * N_CMP
    for half in range(CMP_BLOCK // CMP_STRIDE):
        src = kv[:, CMP_STRIDE * half:CMP_STRIDE * half + width].rearrange("p (n r) -> p r n", r=CMP_STRIDE)
        r = slice(CMP_STRIDE * half, CMP_STRIDE * (half + 1))
        m = tt(V, blocks[:, r, :], src, over(pos[:, r], N_CMP, 2), ALU.add, after=pos_came + [kv_done])
    for g in range(NSA_G):
        bk = c.take_bank()
        rows = slice(64 * g, 64 * g + 64)
        PE.wait([m] + w1_came + c.bank_read[bk])
        for r in range(CMP_BLOCK):
            mm(PE, c.bank(bk)[:, 0:N_CMP], w1[rows, r, :], blocks[rows, r, :], r == 0, r == CMP_BLOCK - 1)
        c.bank_read[bk] = [act(S, hid[:, g, :], c.bank(bk)[:, 0:N_CMP], ACT.Gelu_apprx_tanh, after=[PE.last])]
    return hid


def nsa(c, ctx, q, kv, vt, gates, o, projected):
    V, S, G, PE = c.V, c.S, c.G, c.PE
    table = c.sb("bias_table", [BUCKETS, NSA_H], ctx)
    onehot = c.sb("bias_onehot", [BUCKETS, 2 * T], ctx)
    by_dist = c.sb("bias_by_dist", [NSA_H, 2 * T], ctx)
    came = [c.load(table[:, :], c.dram["rel_bias"]), c.load(onehot[:, :], c.dram["bucket_of_dist"])]
    bk = c.take_bank()
    mm(PE, c.bank(bk)[0:NSA_H, :], table[:, :], onehot[:, :], after=came + c.bank_read[bk])
    c.bank_read[bk] = [copy(V, by_dist[:, :], c.bank(bk)[0:NSA_H, :], after=[PE.last])]
    m = fill(V, by_dist[:, 0:T - 1], NEG_INF)
    scratch = c.dram["bias_scratch"]
    stored = c.load(scratch, by_dist[:, :], after=[m])
    bias = [c.sb("bias_0", [P, NSA_H, P], ctx), c.sb("bias_1", [P, NSA_H, T], ctx)]
    came = [c.load(bias[0][:, :, :], bass.AP(scratch.tensor, T - P, [[1, P], [2 * T, NSA_H], [1, P]]), after=[stored]),
            c.load(bias[1][:, :, :], bass.AP(scratch.tensor, P, [[1, P], [2 * T, NSA_H], [1, T]]), after=[stored])]
    k_cmp = c.sb("k_cmp", [P, N_CMP], ctx)
    v_cmp = c.sb("v_cmp", [N_CMP, P], ctx)
    early = P // CMP_STRIDE - 1
    v_early = c.sb("v_cmp_early", [early, P], ctx)
    with ExitStack() as inner:
        hid_k = compress(c, inner, "cmp_k", kv["kc"], projected, c.dram["pos_k"], c.dram["cmp_k_w1"])
        hid_v = compress(c, inner, "cmp_v", kv["vc"], projected, c.dram["pos_v"], c.dram["cmp_v_w1"])
        w2 = c.sb("cmp_w2", [P, 2, NSA_DH], inner)
        w2_came = [c.load(w2[:, 0, :], c.dram["cmp_k_w2"]), c.load(w2[:, 1, :], c.dram["cmp_v_w2"])]
        bk = c.take_bank()
        PE.wait([S.last] + w2_came + c.bank_read[bk])
        for g in range(NSA_G):
            mm(PE, c.bank(bk)[64 * g:64 * g + 64, 0:N_CMP], w2[:, 0, :], hid_k[:, g, :])
        c.bank_read[bk] = [copy(V, k_cmp[:, :], c.bank(bk)[:, 0:N_CMP], after=[PE.last])]
        bk = c.take_bank()
        PE.wait(c.bank_read[bk])
        for g in range(NSA_G):
            mm(PE, c.bank(bk)[0:N_CMP, 64 * g:64 * g + 64], hid_v[:, g, :], w2[:, 1, :])
            mm(PE, c.bank(bk)[0:early, P + 64 * g:P + 64 * g + 64], hid_v[:, g, N_CMP - early:N_CMP], w2[:, 1, :])
        copy(V, v_cmp[:, :], c.bank(bk)[0:N_CMP, 0:P], after=[PE.last])
        c.bank_read[bk] = [copy(V, v_early[:, :], c.bank(bk)[0:early, P:2 * P])]
        c.barrier()

    sig = c.sb("gate_sigmoid", [P, NT, 3 * NSA_H], ctx)
    act(S, sig[:, :, :], gates[:, :, :], ACT.Sigmoid)
    sc = c.sb("cmp_s", [P, NSA_H, N_CMP], ctx)
    s = c.sb("nsa_s", [P, NSA_H, T], ctx)
    e = [c.sb("nsa_e0", [P, NSA_H, T], ctx), c.sb("nsa_e1", [P, NSA_H, T], ctx)]
    mx = c.sb("nsa_max", [P, NSA_H], ctx)
    z = c.sb("nsa_z", [P, 3, NSA_H], ctx)
    pt_cmp = c.sb("nsa_pt_cmp", [N_CMP, NSA_H, P], ctx)
    pt = c.sb("nsa_pt", [P, 2, NSA_H, NT, P], ctx)
    for i in range(NT):
        q_i = slice(P * i, P * i + P)
        n_keys = P * (i + 1)
        n_blocks = N_CMP if i else early
        bk = 0
        PE.wait([V.last] + c.bank_read[0] + c.bank_read[1])
        for g in range(NSA_G):
            rows = slice(64 * g, 64 * g + 64)
            for h in range(HPG):
                mm(PE, c.bank(g)[:, n_blocks * h:n_blocks * (h + 1)], q[rows, h, q_i],
                   k_cmp[rows, N_CMP - n_blocks:N_CMP])
        scv = sc[:, :, 0:n_blocks]
        for g in range(NSA_G):
            hs = slice(HPG * g, HPG * (g + 1))
            steps = bias[i][:, hs, :].rearrange("p h (n r) -> p h n r", r=CMP_STRIDE)[:, :, 0:n_blocks, 0]
            m = tt(V, scv[:, hs, :], c.bank(g)[:, 0:HPG * n_blocks].rearrange("p (h n) -> p h n", h=HPG), steps,
                   ALU.add, after=[PE.last] + came)
        c.bank_read[0] = c.bank_read[1] = [m]
        gate = sig[:, i, :].rearrange("p (h b) -> p b h", b=3)
        m = ts(V, mx[:, :], gate[:, 0, :], c.some_block[:, :], ALU.mult, after=[S.last]) if i == 0 else None
        coef = z[:, 1, :]
        m = copy(V, coef, mx[:, :]) if i == 0 else copy(V, coef, gate[:, 0, :], after=[S.last])
        ec = e[0][:, :, 0:n_blocks]
        m = c.softmax(scv, ec, mx[:, :], z[:, 0, :], NSA_H, n_blocks, coef)
        PE.wait([m] + c.bank_read[0] + c.bank_read[1])
        for h in range(NSA_H):
            tr(PE, c.bank(h // 4)[0:n_blocks, P * (h % 4):P * (h % 4) + P], ec[:, h, :], c.ident[:, :])
        for w in range(2):
            m = act(S, pt_cmp[0:n_blocks, 4 * w:4 * w + 4, :],
                    c.bank(w)[0:n_blocks, :].rearrange("p (h t) -> p h t", h=4), ACT.Copy, after=[PE.last])
            c.bank_read[w] = [m]
        sv = s[:, :, 0:n_keys]
        for w, name in enumerate(("ks", "kw")):
            PE.wait(c.bank_read[4] + c.bank_read[5] + c.bank_read[6] + c.bank_read[7])
            for g in range(NSA_G):
                rows = slice(64 * g, 64 * g + 64)
                area = c.bank(4 + 2 * g, 2)
                for h in range(HPG):
                    mm(PE, area[:, n_keys * h:n_keys * (h + 1)], q[rows, h, q_i], kv[name][rows, T - n_keys:T])
            for g in range(NSA_G):
                hs = slice(HPG * g, HPG * (g + 1))
                area = c.bank(4 + 2 * g, 2)[:, 0:HPG * n_keys].rearrange("p (h n) -> p h n", h=HPG)
                m = tt(V, sv[:, hs, :], area, bias[i][:, hs, :], ALU.add, after=[PE.last] + came)
                c.bank_read[4 + 2 * g] = c.bank_read[5 + 2 * g] = [m]
            ev = e[w][:, :, 0:n_keys]
            m = c.softmax(sv, ev, mx[:, :], z[:, 0, :], NSA_H, n_keys, gate[:, 1 + w, :])
            for jj in range(i + 1):
                for half in range(2):
                    b0 = c.bank(2 + half)
                    PE.wait([m] + c.bank_read[2 + half])
                    for h in range(4):
                        tr(PE, b0[:, P * h:P * h + P], ev[:, 4 * half + h, P * jj:P * jj + P], c.ident[:, :])
                    c.bank_read[2 + half] = [act(S, pt[:, w, 4 * half:4 * half + 4, jj, :],
                                                 b0.rearrange("p (h t) -> p h t", h=4), ACT.Copy, after=[PE.last])]
        vc_i = v_cmp if i else v_early
        PE.wait([S.last] + c.bank_read[1])
        for h in range(HPG):
            for g in range(NSA_G):
                out = c.bank(1)[64 * g:64 * g + 64, P * h:P * h + P]
                cols = slice(64 * g, 64 * g + 64)
                mm(PE, out, vc_i[0:n_blocks, cols], pt_cmp[0:n_blocks, HPG * g + h, :], True, False)
                for w, name in enumerate(("vs", "vw")):
                    for jj in range(i + 1):
                        mm(PE, out, vt[name][:, NT - 1 - i + jj, cols], pt[:, w, HPG * g + h, jj, :], False,
                           w == 1 and jj == i)
        c.bank_read[1] = [copy(V, o[:, :, q_i], c.bank(1).rearrange("p (h t) -> p h t", h=HPG), after=[PE.last])]
        S.wait([PE.last])


def first_mixer(c, h, xn, work, tmp):
    V, S, G, PE = c.V, c.S, c.G, c.PE
    with ExitStack() as ctx:
        m = c.rmsnorm(h, c.gain("norm_mix"), xn, work, tmp, after=[c.h_came, c.gains_came])
        xr = work
        rev = copy(V, xr[:, :, :], xn[:, :, ::-1])
        gq = c.sb("gla_q", [P, 2, T], ctx)
        gk = c.sb("gla_k", [P, 2, T], ctx)
        gate = c.sb("gla_gate", [P, 2, T], ctx)
        gv = c.sb("gla_v", [P, NT, 512], ctx)
        gr = c.sb("gla_r", [P, 4, T], ctx)
        o = c.sb("mix_o", [P, 8, T], ctx)
        nq = c.sb("nsa_q", [P, HPG, T], ctx)
        kv = {n: c.sb("nsa_" + n, [P, T], ctx) for n in ("kc", "vc", "ks", "kw")}
        vt = {n: c.sb("nsa_" + n, [P, NT, P], ctx) for n in ("vs", "vw")}
        small_w = c.sb("small_w", [P, KD, 40], ctx)
        glr = c.sb("gla_lr", [GLA_RANK, T], ctx)
        gates = c.sb("nsa_gates", [P, NT, 24], ctx)
        w2 = c.sb("gate_w2", [GLA_RANK, T], ctx)
        small_came = c.load(small_w[:, :, :], c.dram["w_in_small"])
        w2_came = c.load(w2[:, :], c.dram["gla_gate_w2"])
        PE.wait([m])

        def keep(dst, scale=1.0):
            return lambda out, done: act(S, dst, out, ACT.Copy, scale=scale, after=[done])

        w = c.dram["w_in"]
        for j in range(2):
            c.channels(w[j], xn, keep(gq[:, j, :], GLA_DK ** -0.5))
        for j in range(2):
            c.channels(w[2 + j], xn, keep(gk[:, j, :]))
        for j in range(4):
            c.tokens(w[4 + j], xn, keep(gv[:, :, P * j:P * j + P]))
        for j in range(4):
            c.channels(w[8 + j], xn, keep(gr[:, j, :]))
        for j in range(4):
            c.channels(w[12 + j], xn, keep(nq[:, j, :], NSA_DH ** -0.5))
        for n, name in ((16, "kc"), (17, "vc"), (18, "ks"), (20, "kw")):
            c.channels(w[n], xr, keep(kv[name][:, :]), after=[rev])
        for n, name in ((19, "vs"), (21, "vw")):
            c.tokens(w[n], xr, keep(vt[name][:, :, :]))
        bk = c.take_bank()
        PE.wait([small_came] + c.bank_read[bk])
        for k in range(KD):
            mm(PE, c.bank(bk)[0:GLA_RANK, 0:T], small_w[:, k, 0:GLA_RANK], xn[:, k, :], k == 0, k == KD - 1)
        a = act(S, glr[:, :], c.bank(bk)[0:GLA_RANK, 0:T], ACT.Copy, after=[PE.last])
        c.bank_read[bk] = [a]
        bk = c.take_bank()
        PE.wait(c.bank_read[bk])
        for i in range(NT):
            for k in range(KD):
                mm(PE, c.bank(bk)[:, 24 * i:24 * i + 24], xn[:, k, P * i:P * i + P], small_w[:, k, 16:40],
                   k == 0, k == KD - 1)
        c.bank_read[bk] = [act(S, gates[:, :, :], c.bank(bk)[:, 0:48].rearrange("p (i c) -> p i c", i=NT), ACT.Copy,
                               after=[PE.last])]
        za = c.sb("gate_z", [P, 2, T], ctx)
        for j in range(2):
            bk = c.take_bank()
            mm(PE, c.bank(bk)[:, 0:T], w2[:, P * j:P * j + P], glr[:, :], after=[a, w2_came] + c.bank_read[bk])
            bcol = c.gain("gla_gate_b")[:, j:j + 1]
            c.bank_read[bk] = [ts(V, gate[:, j, :], c.bank(bk)[:, 0:T], bcol, ALU.add, after=[PE.last])]
        act(S, za[:, :, :], gate[:, :, :], ACT.Abs, after=[V.last])
        act(S, za[:, :, :], za[:, :, :], ACT.Exp, scale=-1.0)
        m = act(S, za[:, :, :], za[:, :, :], ACT.Ln, bias=1.0)
        ts(V, gate[:, :, :], gate[:, :, :], 0.0, ALU.min, after=[m])
        tt(V, gate[:, :, :], gate[:, :, :], za[:, :, :], ALU.subtract)
        m = ts(V, gate[:, :, :], gate[:, :, :], 1.0 / GLA_TAU, ALU.mult)
        with ExitStack() as inner:
            gla(c, inner, gq[:, :, :], gk[:, :, :], gate, gv, gr, c.gain("gla_out_norm"), o[:, 0:4, :], [m, S.last])
            c.dump("gla_o", o[:, 0:4, :])
            c.barrier()
        with ExitStack() as inner:
            nsa(c, inner, nq, kv, vt, gates, o[:, 4:8, :], S.last)
            c.dump("nsa_o", o[:, 4:8, :])
            for n in range(KD):
                c.channels(c.dram["w_out"][n], o, lambda out, done, n=n: tt(V, h[:, n, :], h[:, n, :], out, ALU.add,
                                                                         after=[done]), after=[V.last])
            c.barrier()


def cross_attention(c, h, xn, work, tmp):
    V, S, G, PE = c.V, c.S, c.G, c.PE
    with ExitStack() as ctx:
        mem = c.sb("mem", [P, KD, T], ctx)
        memn = c.sb("memn", [P, KD, T], ctx)
        mem_came = c.load(mem[:, :, :], c.dram["memT"])
        c.rmsnorm(mem, c.gain("norm_mem"), memn, work, tmp, after=[mem_came])
        m = c.rmsnorm(h, c.gain("norm_xattn"), xn, work, tmp, after=[PE.last])
        q = c.sb("xa_q", [P, KD, T], ctx)
        k = c.sb("xa_k", [P, KD, T], ctx)
        v = c.sb("xa_v", [P, NT, D], ctx)
        o = c.sb("xa_o", [P, KD, T], ctx)
        s = c.sb("xa_s", [P, XA_H, T], ctx)
        e = c.sb("xa_e", [P, XA_H, T], ctx)
        mx = c.sb("xa_max", [P, XA_H], ctx)
        z = c.sb("xa_z", [P, XA_H], ctx)
        pt = c.sb("xa_pt", [P, XA_H, NT, T], ctx)
        PE.wait([m])

        def keep(dst, scale=1.0):
            return lambda out, done: act(S, dst, out, ACT.Copy, scale=scale, after=[done])

        for n in range(KD):
            c.channels(c.dram["xa_wk"][n], memn, keep(k[:, n, :]))
        for n in range(KD):
            c.channels(c.dram["xa_wq"][n], xn, keep(q[:, n, :], XA_DH ** -0.5))
        for n in range(KD):
            c.tokens(c.dram["xa_wv"][n], memn, keep(v[:, :, P * n:P * n + P]))
        for i in range(NT):
            tile = slice(P * i, P * i + P)
            PE.wait([S.last] + c.bank_read[0] + c.bank_read[1])
            for hd in range(XA_H):
                for j in range(2):
                    mm(PE, c.bank(0, 2)[:, T * hd:T * hd + T], q[:, 2 * hd + j, tile], k[:, 2 * hd + j, :],
                       j == 0, j == 1)
            m = copy(V, s[:, :, :], c.bank(0, 2).rearrange("p (h m) -> p h m", h=XA_H), after=[PE.last, S.last])
            c.bank_read[0] = c.bank_read[1] = [m]
            m = c.softmax(s[:, :, :], e[:, :, :], mx[:, :], z[:, :], XA_H, T)
            for j in range(NT):
                PE.wait([m] + c.bank_read[2 + j])
                for hd in range(XA_H):
                    tr(PE, c.bank(2 + j)[:, P * hd:P * hd + P], e[:, hd, P * j:P * j + P], c.ident[:, :])
                c.bank_read[2 + j] = [act(S, pt[:, :, j, tile], c.bank(2 + j).rearrange("p (h t) -> p h t", h=XA_H),
                                          ACT.Copy, after=[PE.last])]
        for n in range(KD):
            bk = c.take_bank()
            PE.wait([S.last] + c.bank_read[bk])
            for j in range(NT):
                mm(PE, c.bank(bk)[:, 0:T], v[:, j, P * n:P * n + P], pt[:, n // 2, j, :], j == 0, j == NT - 1)
            c.bank_read[bk] = [copy(V, o[:, n, :], c.bank(bk)[:, 0:T], after=[PE.last])]
        for n in range(KD):
            c.channels(c.dram["xa_wo"][n], o, lambda out, done, n=n: tt(V, h[:, n, :], h[:, n, :], out, ALU.add,
                                                                      after=[done]), after=[V.last])
        c.barrier()


def top16(c, vals, idx, src, spare):
    V = c.V
    V.do(lambda e: e.max(out=vals[:, 0:8], in_=src))
    V.do(lambda e: e.max_index(out=idx[:, 0:8], in_max=vals[:, 0:8], in_values=src))
    V.do(lambda e: e.match_replace(out=spare, in_to_replace=vals[:, 0:8], in_values=src, imm_value=-3e38))
    V.do(lambda e: e.max(out=vals[:, 8:16], in_=spare))
    return V.do(lambda e: e.max_index(out=idx[:, 8:16], in_max=vals[:, 8:16], in_values=spare))


def peer(c, h, xn, work, tmp, name, gain, half_dim, wq, subkeys, down, up):
    V, S, G, PE = c.V, c.S, c.G, c.PE
    n_q = 2 * PEER_H * half_dim // P
    with ExitStack() as ctx:
        gates = c.sb(name + "_gates", [P, NKEYS, T], ctx)
        pairs = c.sb(name + "_pairs", [P, 3, T], ctx)
        with ExitStack() as inner:
            area = gates[:, :, :].rearrange("p a t -> p (a t)")
            at = [0]

            def cut(n):
                at[0] += n
                return area[:, at[0] - n:at[0]]

            q = cut(n_q * T).rearrange("p (k t) -> p k t", k=n_q)
            n_sk = n_q * P * (P // half_dim) // (P // half_dim)
            sk = cut(n_sk).rearrange("p (k n) -> p k n", k=n_q)
            scores = cut(2 * PEER_H * NKEYS).rearrange("p (h a n) -> p h a n", h=PEER_H, a=2)
            cand = cut(PEER_H * 256).rearrange("p (h a b) -> p h a b", h=PEER_H, a=TOPK)
            eq = cut(PEER_H * 256).rearrange("p (h k j) -> p h k j", h=PEER_H, k=TOPK)
            spare = cut(256)
            vals = cut(2 * PEER_H * TOPK).rearrange("p (h a k) -> p h a k", h=PEER_H, a=2)
            idx = cut(2 * PEER_H * TOPK).rearrange("p (h a k) -> p h a k", h=PEER_H, a=2).bitcast(U32)
            idxf = cut(2 * PEER_H * TOPK).rearrange("p (h a k) -> p h a k", h=PEER_H, a=2)
            top = cut(PEER_H * TOPK).rearrange("p (h k) -> p h k", h=PEER_H)
            pos = cut(PEER_H * TOPK).rearrange("p (h k) -> p h k", h=PEER_H).bitcast(U32)
            part = cut(PEER_H * TOPK).rearrange("p (h k) -> p h k", h=PEER_H).bitcast(U32)
            partf = cut(PEER_H * TOPK).rearrange("p (h k) -> p h k", h=PEER_H)
            res = cut(3 * PEER_H * TOPK).rearrange("p (x h k) -> p x h k", x=3, h=PEER_H)
            zs = cut(PEER_H)
            m = c.rmsnorm(h, gain, xn, work, tmp)
            PE.wait([m])
            sk_came = c.load(sk, subkeys, after=[m])
            for n in range(n_q):
                c.channels(wq[n], xn, lambda out, done, n=n: act(S, q[:, n, :], out, ACT.Copy, after=[done]))
            for i in range(NT):
                tile = slice(P * i, P * i + P)
                if half_dim == 64:
                    PE.wait([S.last, sk_came] + [x for b in range(4) for x in c.bank_read[b]])
                    for hd in range(PEER_H):
                        for a in range(2):
                            mm(PE, c.bank(2 * a, 2)[:, P * hd:P * hd + P], q[64 * a:64 * a + 64, hd, tile],
                               sk[64 * a:64 * a + 64, hd, :])
                    for a in range(2):
                        m = act(S, scores[:, :, a, :], c.bank(2 * a, 2).rearrange("p (h n) -> p h n", h=PEER_H),
                                ACT.Copy, after=[PE.last, V.last])
                else:
                    PE.wait([S.last, sk_came] + [x for b in range(4) for x in c.bank_read[b]])
                    for n in range(n_q):
                        mm(PE, c.bank(0, 4)[:, P * n:P * n + P], q[:, n, tile], sk[:, n, :])
                    m = act(S, scores, c.bank(0, 4).rearrange("p (h a n) -> p h a n", h=PEER_H, a=2), ACT.Copy,
                            after=[PE.last, V.last])
                for b in range(4):
                    c.bank_read[b] = [m]
                V.wait([m])
                for hd in range(PEER_H):
                    for a in range(2):
                        top16(c, vals[:, hd, a, :], idx[:, hd, a, :], scores[:, hd, a, :], spare[:, 0:NKEYS])
                copy(V, idxf, idx)
                tt(V, cand, over(vals[:, :, 0, :], TOPK, 3), over(vals[:, :, 1, :], TOPK, 2), ALU.add)
                for hd in range(PEER_H):
                    top16(c, top[:, hd, :], pos[:, hd, :], cand[:, hd, :, :].rearrange("p a b -> p (a b)"), spare)
                iota16 = over(over(c.iota[:, 0:TOPK], TOPK, 1), PEER_H, 1)
                for a in range(2):
                    if a == 0:
                        ts(V, part, pos, 4, ALU.logical_shift_right)
                    else:
                        ts(V, part, pos, 15, ALU.bitwise_and)
                    copy(V, partf, part)
                    tt(V, eq, over(partf, TOPK, 3), iota16, ALU.is_equal)
                    tt(V, eq, eq, over(idxf[:, :, a, :], TOPK, 2), ALU.mult)
                    reduce(V, res[:, a, :, :], eq, ALU.add)
                m = tt(V, res[:, 2, :, :], top, over(top[:, :, 0], TOPK, 2), ALU.subtract)
                m = act(S, res[:, 2, :, :], res[:, 2, :, :], ACT.Exp, after=[m])
                reduce(V, zs, res[:, 2, :, :], ALU.add, after=[m])
                recip(V, zs, zs)
                m = tt(V, res[:, 2, :, :], res[:, 2, :, :], over(zs, TOPK, 2), ALU.mult)
                bk = 4
                PE.wait([m] + c.bank_read[bk])
                for x in range(3):
                    tr(PE, c.bank(bk)[:, P * x:P * x + P], res[:, x, :, :].rearrange("p h k -> p (h k)"), c.ident[:, :])
                c.bank_read[bk] = [copy(V, pairs[:, :, tile], c.bank(bk)[:, 0:3 * P].rearrange("p (x t) -> p x t", x=3),
                                        after=[PE.last])]
            if c.stop == name + "_pairs":
                c.dump("pairs", pairs[:, :, :])
            c.barrier()

        N1 = 8
        onehots = work[:, :, :].rearrange("p k (i n) -> p i k n", i=2)
        first, second = onehots[:, 0, :, :], onehots[:, 1, :, :]
        used = [[] for _ in range(N1)]
        built = None
        for t in range(T):
            u = t % N1
            built = V.do(lambda e, u=u, t=t: e.tensor_scalar(first[:, u, :], c.iota[:, :], pairs[:, 0, t:t + 1],
                                                              pairs[:, 2, t:t + 1], ALU.is_equal, ALU.mult),
                         after=used[u])
            V.do(lambda e, u=u, t=t: e.tensor_scalar(second[:, u, :], c.iota[:, :], pairs[:, 1, t:t + 1], None,
                                                     ALU.is_equal))
            b = t // 4 % 4
            if t % 4 == 0:
                PE.wait(c.bank_read[b])
            mm(PE, c.bank(b)[:, P * (t % 4):P * (t % 4) + P], first[:, u, :], second[:, u, :], after=[V.last])
            used[u] = [PE.last]
            if t % 4 == 3:
                c.bank_read[b] = [act(S, gates[:, :, t - 3:t + 1], c.bank(b).rearrange("p (t i) -> p i t", t=4), ACT.Copy,
                                      after=[PE.last])]
        gates_done = S.last
        if c.stop == name + "_gates":
            c.dump("gates", gates[:, 0:16, :])
        NB = 3
        hid = c.sb(name + "_hid", [P, NB, T], ctx)
        coef = c.sb(name + "_coef", [P, NB, T], ctx)
        coef_read = [[] for _ in range(NB)]
        coef_made = [None] * NB

        def hidden(n):
            u, b = n % NB, 4 + n % 4
            slot, came = c.unit(down[n])
            w = c.ring[:, slot, :].rearrange("p (k e) -> p k e", k=KD)
            PE.wait([came] + c.bank_read[b])
            for k in range(KD):
                mm(PE, c.bank(b)[:, 0:T], w[:, k, :], xn[:, k, :], k == 0, k == KD - 1)
            c.slot_read[slot] = [PE.last]
            c.bank_read[b] = [act(S, hid[:, u, :], c.bank(b)[:, 0:T], ACT.Gelu_apprx_tanh,
                                  after=[PE.last] + ([coef_made[u]] if coef_made[u] else []))]
            coef_made[u] = tt(V, coef[:, u, :], hid[:, u, :], gates[:, n, :], ALU.mult,
                              after=[S.last, gates_done] + coef_read[u])

        def output(n):
            u = n % NB
            slot, came = c.unit(up[n])
            PE.wait([came, coef_made[u]])
            if n == 0:
                PE.wait([x for b in range(4) for x in c.bank_read[b]])
            for i in range(NT):
                for half in range(2):
                    mm(PE, c.bank(2 * i + half), coef[:, u, P * i:P * i + P],
                       c.ring[:, slot, 512 * half:512 * half + 512], n == 0, n == NKEYS - 1)
            c.slot_read[slot] = [PE.last]
            coef_read[u] = [PE.last]

        hidden(0)
        for n in range(NKEYS):
            if n + 1 < NKEYS:
                hidden(n + 1)
            output(n)
        y = [work[:, 4 * i:4 * i + 4, :].rearrange("p k t -> p (k t)") for i in range(NT)]
        done = PE.last
        for i in range(NT):
            for b in (2 * i, 2 * i + 1):
                m = copy(V, y[i][:, 512 * (b % 2):512 * (b % 2) + 512], c.bank(b), after=[done])
                c.bank_read[b] = [m]
        for k in range(KD):
            b = 4 + k % 4
            PE.wait([m] + c.bank_read[b])
            for i in range(NT):
                tr(PE, c.bank(b)[:, P * i:P * i + P], y[i][:, P * k:P * k + P], c.ident[:, :])
            c.bank_read[b] = [tt(V, h[:, k, :], h[:, k, :], c.bank(b)[:, 0:T], ALU.add, after=[PE.last])]
        c.barrier()


def hgrn(c, ctx, q, zf, zb, v, o):
    V, S, G, PE = c.V, c.S, c.G, c.PE
    lb = c.sb("hg_lb", [P, KD], ctx)
    one_minus = c.sb("hg_one_minus", [P, KD], ctx)
    t2 = c.sb("hg_t2", [P, 2, KD], ctx)
    lbl = c.gain("lb").rearrange("p (l k) -> p l k", l=2)
    tt(V, lb[:, :], lbl[:, 0, :], lbl[:, 1, :], ALU.max)
    m = tt(V, t2[:, :, :], lbl, over(lb[:, :], 2, 1), ALU.subtract)
    m = act(S, t2[:, :, :], t2[:, :, :], ACT.Exp, after=[m])
    tt(V, one_minus[:, :], t2[:, 0, :], t2[:, 1, :], ALU.add, after=[m])
    recip(V, one_minus[:, :], one_minus[:, :])
    tt(V, lb[:, :], t2[:, 0, :], one_minus[:, :], ALU.mult)
    ts(V, one_minus[:, :], lb[:, :], -1.0, ALU.mult, 1.0, ALU.add)
    kf = c.sb("hg_kf", [P, HG_H, T], ctx)
    kb = c.sb("hg_kb", [P, HG_H, T], ctx)
    for z, k in ((zf, kf), (zb, kb)):
        act(S, k[:, :, :], z[:, :, :], ACT.Sigmoid, scale=-1.0)
        m = act(S, z[:, :, :], z[:, :, :], ACT.Sigmoid)
        for hd in range(HG_H):
            ts(V, k[:, hd, :], k[:, hd, :], one_minus[:, hd:hd + 1], ALU.mult, after=[m])
            ts(V, z[:, hd, :], z[:, hd, :], one_minus[:, hd:hd + 1], ALU.mult, lb[:, hd:hd + 1], ALU.add)
        m = ts(V, z[:, :, :], z[:, :, :], 2.0 ** -62, ALU.max)
        act(S, z[:, :, :], z[:, :, :], ACT.Ln, after=[m])
    bf = c.sb("hg_bf", [P, HG_H, T], ctx)
    bb = c.sb("hg_bb", [P, HG_H, T], ctx)
    for hd in range(HG_H):
        V.do(lambda e, hd=hd: e.tensor_tensor_scan(bf[:, hd, :], c.reset[:, :], zf[:, hd, :], 0.0, ALU.mult, ALU.add),
             after=[S.last])
        V.do(lambda e, hd=hd: e.tensor_tensor_scan(bb[:, hd, ::-1], c.reset[:, :], zb[:, hd, ::-1], 0.0, ALU.mult,
                                                   ALU.add))
    eq, ek = zf, zb
    qq = c.sb("hg_qq", [P, HG_H, T], ctx)
    kk = c.sb("hg_kk", [P, HG_H, T], ctx)
    at = c.sb("hg_scores", [P, HG_H, NT, P], ctx)
    fwd = c.sb("hg_scores_fwd", [P, HG_H, P], ctx)
    bwd = c.sb("hg_scores_bwd", [P, HG_H, P], ctx)
    read = []
    m0 = None
    for n, m in enumerate([P] + LEVELS + [0]):
        if m:
            F, B, EQ, EK = halves(bf[:, :, :], m), halves(bb[:, :, :], m), halves(eq[:, :, :], m), halves(ek[:, :, :], m)
            rf, rb = over(F[:, :, 0, m - 1], m, 2), over(B[:, :, 1, 0], m, 2)
            if m == P:
                copy(V, EQ[:, :, 1, :], F[:, :, 1, :])
                a1 = copy(V, EQ[:, :, 0, :], B[:, :, 0, :])
            else:
                tt(V, EQ[:, :, 1, :], F[:, :, 1, :], rf, ALU.subtract)
                a1 = tt(V, EQ[:, :, 0, :], B[:, :, 0, :], rb, ALU.subtract)
            tt(G, EK[:, :, 0, :], rf, F[:, :, 0, :], ALU.subtract, after=[V.last])
            a2 = tt(G, EK[:, :, 1, :], rb, B[:, :, 1, :], ALU.subtract)
            e1 = act(S, eq[:, :, :], eq[:, :, :], ACT.Exp, after=[a1])
            e2 = act(S, ek[:, :, :], ek[:, :, :], ACT.Exp, after=[a2])
            tt(V, qq[:, :, :], q[:, :, :], eq[:, :, :], ALU.mult, after=[e1] + read)
            KF, KB, KK = halves(kf[:, :, :], m), halves(kb[:, :, :], m), halves(kk[:, :, :], m)
            tt(G, KK[:, :, 0, :], KF[:, :, 0, :], EK[:, :, 0, :], ALU.mult, after=[e2] + read)
            a = tt(G, KK[:, :, 1, :], KB[:, :, 1, :], EK[:, :, 1, :], ALU.mult)
            ql = qq
        else:
            a = tt(G, kk[:, :, :], kf[:, :, :], kb[:, :, :], ALU.add, after=read)
            ql = q
        b0 = 4 * (n % 2)
        PE.wait([V.last, a] + [x for b in range(b0, b0 + 4) for x in c.bank_read[b]])
        area = c.bank(b0, 4).rearrange("p (h i t) -> p h i t", h=HG_H, i=NT)
        for hd in range(HG_H):
            for i in range(NT):
                s_tile = slice(P * i, P * i + P)
                t_tile = slice(P * (1 - i), P * (1 - i) + P) if m == P else s_tile
                mm(PE, area[:, hd, i, :], kk[:, hd, s_tile], ql[:, hd, t_tile])
        read = [PE.last]
        if m == P:
            copy(V, fwd[:, :, :], area[:, :, 0, :], after=read)
            a = copy(V, bwd[:, :, :], area[:, :, 1, :])
            fill(V, at[:, :, :, :], 0.0)
        else:
            mask = c.masks[:, len(LEVELS) + n - 1, :] if m else c.ident[:, :]
            a = V.do(lambda e, mask=mask, b0=b0: e.copy_predicated(
                at[:, :, :, :].rearrange("p h i t -> p (h i) t"), over(mask.bitcast(U32), HG_H * NT, 1),
                c.bank(b0, 4).rearrange("p (x t) -> p x t", t=P)), after=read)
        for b in range(b0, b0 + 4):
            c.bank_read[b] = [a]
    for hd in range(HG_H):
        bk = c.take_bank()
        PE.wait([V.last] + c.bank_read[bk])
        v0, v1 = v[:, 0, P * hd:P * hd + P], v[:, 1, P * hd:P * hd + P]
        out = c.bank(bk)
        mm(PE, out[:, 0:P], v0, at[:, hd, 0, :], True, False)
        mm(PE, out[:, 0:P], v1, bwd[:, hd, :], False, True)
        mm(PE, out[:, P:T], v0, fwd[:, hd, :], True, False)
        mm(PE, out[:, P:T], v1, at[:, hd, 1, :], False, True)
        c.bank_read[bk] = [act(S, o[:, hd, :], out[:, 0:T], ACT.Copy, after=[PE.last])]


def filters(c, ctx, both):
    V, S, PE = c.V, c.S, c.PE
    z = c.sb("filt_z", [EMB, T], ctx)
    w1 = c.sb("filt_w1", [EMB, FILT_H], ctx)
    w2 = c.sb("filt_w2", [FILT_H, FILT_H], ctx)
    w3 = c.sb("filt_w3", [FILT_H, 2 * D], ctx)
    vec = c.sb("filt_vec", [FILT_H, 4], ctx)
    decay = c.sb("filt_decay", [P, 2 * D], ctx)
    window = c.sb("filt_window", [P, 2 * D], ctx)
    cols = c.sb("filt_cols", [P, 2 * NT], ctx)
    hid = c.sb("filt_hid", [FILT_H, T], ctx)
    turns = c.sb("filt_turns", [FILT_H, T], ctx)
    came = [c.load(z[:, :], c.dram["filter_z"]), c.load(w1[:, :], c.dram["filt_w1_2"]),
            c.load(w2[:, :], c.dram["filt_w2_2"]), c.load(w3[:, :], c.dram["filt_w3_2"]),
            c.load(vec[:, :], c.dram["filt_vec"]), c.load(decay[:, :], c.dram["filt_decay_2"].partition_broadcast(P)),
            c.load(cols[:, 0:NT], c.dram["minus_t"]), c.load(cols[:, NT:2 * NT], c.dram["not_first"])]
    ROUND = 1.5 * 2.0 ** 23
    TWO_PI = [6.28125, 0.0019350051879882812, 3.019916e-07]
    act(S, decay[:, :], decay[:, :], ACT.Abs, after=came)
    last = None
    for n, (w, x) in enumerate(((w1, z), (w2, hid))):
        bk = c.take_bank()
        mm(PE, c.bank(bk)[0:FILT_H, 0:T], w[:, :], x[:, :], after=came + c.bank_read[bk] + ([last] if last else []))
        m = ts(V, hid[:, :], c.bank(bk)[0:FILT_H, 0:T], vec[:, 2 * n:2 * n + 1], ALU.add,
               vec[:, 2 * n + 1:2 * n + 2], ALU.mult, after=[PE.last] + came)
        c.bank_read[bk] = [m]
        ts(V, turns[:, :], hid[:, :], 1.0 / (2.0 * np.pi), ALU.mult, ROUND, ALU.add)
        ts(V, turns[:, :], turns[:, :], ROUND, ALU.subtract)
        for part in TWO_PI:
            stt(V, hid[:, :], turns[:, :], -part, hid[:, :], ALU.mult, ALU.add)
        ts(V, hid[:, :], hid[:, :], 3.1415925, ALU.min)
        m = ts(V, hid[:, :], hid[:, :], -3.1415925, ALU.max)
        last = act(S, hid[:, :], hid[:, :], ACT.Sin, after=[m])
    for i in range(NT):
        wide = act(S, window[:, :], decay[:, :], ACT.Exp, scale=cols[:, i:i + 1], after=[V.last])
        PE.wait([last] + [x for b in range(4) for x in c.bank_read[b]])
        for b in range(4):
            mm(PE, c.bank(b), hid[:, P * i:P * i + P], w3[:, 512 * b:512 * b + 512])
        m = tt(V, window[:, :], window[:, :], c.bank(0, 4), ALU.mult, after=[wide, PE.last])
        for b in range(4):
            c.bank_read[b] = [m]
        ts(V, window[:, D:2 * D], window[:, D:2 * D], cols[:, NT + i:NT + i + 1], ALU.mult)
        tt(V, both[:, i, 0, :], window[:, 0:D], window[:, D:2 * D], ALU.add)
        tt(V, both[:, i, 1, :], window[:, 0:D], window[:, D:2 * D], ALU.subtract)


def hyena(c, ctx, xn, yb):
    V, S, G, PE = c.V, c.S, c.G, c.PE
    both = c.sb("filters", [P, NT, 2, D], ctx)
    with ExitStack() as inner:
        filters(c, inner, both)
        c.dump("filters", both[:, :, :, :])
        c.barrier()
    basis = {}
    came = []
    for name in ("cos_sj", "sin_sj", "cos_js", "sin_js"):
        basis[name] = c.sb(name, [P, NT, T], ctx)
        came.append(c.load(basis[name][:, :, :], c.dram[name]))
    x0 = c.sb("hy_x0", [P, KD, T], ctx)
    u = c.sb("hy_u", [P, KD, T], ctx)
    x = c.sb("hy_x", [P, T], ctx)
    ut = c.sb("hy_ut", [P, NT, D], ctx)
    fu = c.sb("hy_fu", [P, NT, 2, D], ctx)
    fk = c.sb("hy_fk", [P, NT, 2, D], ctx)
    conv_w = c.gain("conv_w").rearrange("p (j n) -> p j n", j=3)
    conv_b = c.gain("conv_b")

    def short_conv(n, dst):
        def evac(out, done):
            ts(V, dst, out, conv_w[:, 1, n:n + 1], ALU.mult, conv_b[:, n:n + 1], ALU.add, after=[done])
            stt(V, dst[:, 1:T], out[:, 0:T - 1], conv_w[:, 0, n:n + 1], dst[:, 1:T], ALU.mult, ALU.add)
            return stt(V, dst[:, 0:T - 1], out[:, 1:T], conv_w[:, 2, n:n + 1], dst[:, 0:T - 1], ALU.mult, ALU.add)
        return evac

    w = c.dram["w_in_2"]
    for n in range(KD):
        c.channels(w[40 + n], xn, short_conv(n, x0[:, n, :]))
        c.channels(w[48 + n], xn, short_conv(8 + n, u[:, n, :]))
        c.channels(w[56 + n], xn, short_conv(16 + n, x[:, :]))
        m = tt(V, u[:, n, :], u[:, n, :], x[:, :], ALU.mult)
        bk = c.take_bank()
        PE.wait([m] + c.bank_read[bk])
        for i in range(NT):
            tr(PE, c.bank(bk)[:, P * i:P * i + P], u[:, n, P * i:P * i + P], c.ident[:, :])
        c.bank_read[bk] = [act(S, ut[:, :, P * n:P * n + P], c.bank(bk)[:, 0:T].rearrange("p (i c) -> p i c", i=NT),
                               ACT.Copy, after=[PE.last])]
    PE.wait(came + [S.last])
    for j in range(NT):
        for a, name in enumerate(("cos_sj", "sin_sj")):
            for src, dst in ((lambda i: ut[:, i, :], fu), (lambda i, a=a: both[:, i, a, :], fk)):
                for half in range(2):
                    bk = c.take_bank()
                    PE.wait(c.bank_read[bk])
                    for i in range(NT):
                        mm(PE, c.bank(bk), basis[name][:, i, P * j:P * j + P], src(i)[:, 512 * half:512 * half + 512],
                           i == 0, i == NT - 1)
                    c.bank_read[bk] = [act(S, dst[:, j, a, 512 * half:512 * half + 512], c.bank(bk), ACT.Copy,
                                           after=[PE.last])]
    y = both
    t1, t2 = ut[:, 0, :], ut[:, 1, :]
    for j in range(NT):
        uc, us, kc, ks = fu[:, j, 0, :], fu[:, j, 1, :], fk[:, j, 0, :], fk[:, j, 1, :]
        tt(V, t1, uc, kc, ALU.mult, after=[S.last, PE.last])
        tt(V, t2, us, ks, ALU.mult)
        tt(V, y[:, j, 0, :], t1, t2, ALU.subtract)
        tt(V, t1, uc, ks, ALU.mult)
        tt(V, t2, us, kc, ALU.mult)
        m = tt(V, y[:, j, 1, :], t1, t2, ALU.add)
    for n in range(KD):
        bk = c.take_bank()
        PE.wait([m] + c.bank_read[bk])
        for step, (j, a) in enumerate(((0, 0), (0, 1), (1, 0), (1, 1))):
            mm(PE, c.bank(bk)[:, 0:T], y[:, j, a, P * n:P * n + P], basis[("cos_js", "sin_js")[a]][:, j, :],
               step == 0, step == 3)
        ts(V, u[:, n, :], u[:, n, :], c.gain("hyena_bias_2")[:, n:n + 1], ALU.mult, after=[PE.last])
        c.bank_read[bk] = [stt(V, u[:, n, :], c.bank(bk)[:, 0:T], 1.0 / T, u[:, n, :], ALU.mult, ALU.add)]
        tt(V, u[:, n, :], u[:, n, :], x0[:, n, :], ALU.mult)
    c.dump("hy", u[:, :, :])
    for n in range(KD):
        c.channels(c.dram["w_branch_b_2"][n], u, lambda out, done, n=n: act(S, yb[:, n, :], out, ACT.Copy,
                                                                         after=[done]), after=[V.last])


def second_mixer(c, h, xn, work, tmp):
    V, S, G, PE = c.V, c.S, c.G, c.PE
    with ExitStack() as ctx:
        m = c.rmsnorm(h, c.gain("norm_mix_g_2"), xn, work, tmp)
        PE.wait([m])
        ya = c.sb("ya", [P, KD, T], ctx)
        yb = c.sb("yb", [P, KD, T], ctx)
        w = c.dram["w_in_2"]

        def keep(dst, func=ACT.Copy):
            return lambda out, done: act(S, dst, out, func, after=[done])

        with ExitStack() as inner:
            q = c.sb("hg_q", [P, HG_H, T], inner)
            zf = c.sb("hg_zf", [P, HG_H, T], inner)
            zb = c.sb("hg_zb", [P, HG_H, T], inner)
            v = c.sb("hg_v", [P, NT, D], inner)
            o = yb
            for n in range(KD):
                c.channels(w[n], xn, keep(q[:, n, :], ACT.Silu))
            for n in range(KD):
                c.channels(w[8 + n], xn, keep(zf[:, n, :]))
            for n in range(KD):
                c.channels(w[16 + n], xn, keep(zb[:, n, :]))
            for n in range(KD):
                c.tokens(w[24 + n], xn, keep(v[:, :, P * n:P * n + P]))
            with ExitStack() as deep:
                hgrn(c, deep, q, zf, zb, v, o)
                c.dump("hgrn_o", o[:, :, :])
                c.barrier()
            og = q
            for n in range(KD):
                c.channels(w[32 + n], xn, keep(og[:, n, :], ACT.Silu))
            head_norm(c, o, HG_H, work, tmp, c.gain("hgrn_norm_g_2"), og)
            for n in range(KD):
                c.channels(c.dram["w_branch_a_2"][n], o, keep(ya[:, n, :]), after=[V.last])
            c.barrier()
        with ExitStack() as inner:
            hyena(c, inner, xn, yb)
            c.barrier()
        g = work
        for half, y in ((0, ya), (1, yb)):
            for n in range(KD):
                def evac(out, done, n=n, y=y):
                    m = act(S, g[:, n, :], out, ACT.Sigmoid, after=[done, V.last])
                    tt(V, y[:, n, :], y[:, n, :], g[:, n, :], ALU.mult, after=[m])
                    return m
                c.channels(w[64 + 8 * half + n], xn, evac)
        tt(V, ya[:, :, :], ya[:, :, :], yb[:, :, :], ALU.add)
        for n in range(KD):
            c.channels(c.dram["w_out_2"][n], ya, lambda out, done, n=n: tt(V, h[:, n, :], h[:, n, :], out, ALU.add,
                                                                        after=[done]), after=[V.last])
        c.barrier()


def program(nc, dram, out, stop=None, debug=None):
    with ExitStack() as ctx:
        c = Core(nc, ctx, dram)
        c.stop = stop
        V, S, G, PE = c.V, c.S, c.G, c.PE
        h = c.sb("h", [P, KD, T])
        xn = c.sb("xn", [P, KD, T])
        work = c.sb("work", [P, KD, T])
        tmp = c.sb("tmp", [P, T])
        c.gains = c.sb("gains", [P, N_GAINS])
        c.ident = c.sb("ident", [P, P])
        c.ones = c.sb("ones", [P, P])
        c.iota = c.sb("iota", [P, P])
        c.reset = c.sb("reset", [P, T])
        c.some_block = c.sb("some_block", [P, 1])
        c.gain = lambda name: c.gains[:, GAINS[name][0]:GAINS[name][1]]
        c.h_came = c.load(h[:, :, :], dram["xT"])
        c.gains_came = c.load(c.gains[:, :], dram["gains"])
        came = [c.gains_came] + [c.load(x[:, :], dram[n]) for x, n in (
            (c.ident, "ident"), (c.iota, "iota"), (c.reset, "reset"), (c.some_block, "some_block"))]
        fill(V, c.ones[:, :], 1.0)
        for q in (V, S, G, PE):
            q.wait(came)
        PE.wait([V.last])
        outs = []

        def dump(name, ap):
            if debug is None or name not in debug:
                return
            marks = [q.last for q in (V, S, G, PE)]
            outs.append(c.load(debug[name], ap, after=marks))
        c.dump = dump

        with ExitStack() as mctx:
            c.masks = c.sb("masks", [P, 2 * len(LEVELS), P], mctx)
            V.wait([c.load(c.masks[:, :, :], dram["masks"])])
            first_mixer(c, h, xn, work, tmp)
        c.dump("h1", h[:, :, :])
        if stop != "h1":
            cross_attention(c, h, xn, work, tmp)
            c.dump("h2", h[:, :, :])
        if stop not in ("h1", "h2"):
            peer(c, h, xn, work, tmp, "peer_1", c.gain("norm_ffn"), 64, dram["peer_wq"], dram["peer_subkeys"],
                 dram["peer_down"], dram["peer_up"])
            c.rmsnorm(h, c.gain("norm_final"), h, work, tmp)
            c.dump("h3", h[:, :, :])
        if stop not in ("h1", "h2", "h3"):
            c.barrier()
            with ExitStack() as mctx:
                c.masks = c.sb("masks_2", [P, 2 * len(LEVELS), P], mctx)
                V.wait([c.load(c.masks[:, :, :], dram["masks"], after=[V.last])])
                second_mixer(c, h, xn, work, tmp)
            c.dump("h4", h[:, :, :])
        if stop is None:
            peer(c, h, xn, work, tmp, "peer_2", c.gain("norm_ffn_g_2"), 128, dram["peer_w_q_2"],
                 dram["peer_subkeys_2"], dram["peer_u_2"], dram["peer_v_2"])
        m = c.rmsnorm(h, c.gain("norm_final_g_2"), xn, work, tmp)
        outs.append(c.load(out, xn[:, :, :], after=[m]))
        c.DMA.wait(outs)

        block = ctx.enter_context(nc.Block())

        @block.sync
        def _(engine):
            c.DMA.play(engine)

        @block.gpsimd
        def _(engine):
            G.play(engine)

        @block.scalar
        def _(engine):
            S.play(engine)

        @block.vector
        def _(engine):
            V.play(engine)

        @block.tensor
        def _(engine):
            PE.play(engine)


def lay_out(x):
    def blocks(w, cols=P):
        w = w.reshape(KD, P, -1, cols)
        return np.ascontiguousarray(w.transpose(2, 1, 0, 3)).reshape(w.shape[2], P, KD * cols)

    def channel(v):
        return v.reshape(-1, P).T

    def turned(a):
        return np.ascontiguousarray(a.reshape(T, KD, P).transpose(2, 1, 0))

    a = dict(constants())
    x = {k: np.asarray(v) for k, v in x.items()}
    a["xT"], a["memT"] = turned(x["x"][0]), turned(x["mem"][0])
    w = x["w_in"][0]
    nq = w[:, 1552:2064].reshape(D, NSA_G, HPG, NSA_DH).transpose(0, 2, 1, 3).reshape(D, 512)
    a["w_in"] = blocks(np.concatenate([w[:, 0:1536], nq, w[:, 2064:2832]], 1))
    a["w_in_small"] = np.ascontiguousarray(
        np.concatenate([w[:, 1536:1552], w[:, 2832:2856]], 1).reshape(KD, P, 40).transpose(1, 0, 2))
    wo = x["w_out"][0]
    nsa_rows = wo[512:].reshape(NSA_G, HPG, NSA_DH, D).transpose(1, 0, 2, 3).reshape(512, D)
    a["w_out"] = blocks(np.concatenate([wo[0:512], nsa_rows], 0))
    for name in ("xa_wq", "xa_wk", "xa_wv", "xa_wo", "peer_wq", "w_in_2", "w_branch_a_2", "w_branch_b_2", "w_out_2",
                 "peer_w_q_2"):
        a[name] = blocks(x[name][0])
    a["rel_bias"] = x["rel_bias"]
    a["gla_gate_w2"] = x["gla_gate_w2"][0]
    for n in ("k", "v"):
        a[f"pos_{n}"] = np.ascontiguousarray(x[f"cmp_pos_{n}"][0][::-1].T)
        w1 = x[f"cmp_{n}_w1"][0].reshape(CMP_BLOCK, NSA_DH, CMP_HIDDEN)
        a[f"cmp_{n}_w1"] = np.ascontiguousarray(w1[::-1].transpose(1, 0, 2))
        a[f"cmp_{n}_w2"] = x[f"cmp_{n}_w2"][0]
    sk = x["peer_subkeys"][0].transpose(1, 3, 0, 2)
    a["peer_subkeys"] = np.ascontiguousarray(sk.reshape(P, PEER_H, NKEYS))
    sk = x["peer_subkeys_2"][0].transpose(3, 0, 1, 2)
    a["peer_subkeys_2"] = np.ascontiguousarray(sk.reshape(P, 2 * PEER_H, NKEYS))
    for down, up in (("peer_down", "peer_up"), ("peer_u_2", "peer_v_2")):
        d = x[down][0].reshape(P, NKEYS, KD, P)
        a[down] = np.ascontiguousarray(d.transpose(1, 3, 2, 0)).reshape(NKEYS, P, KD * P)
        a[up] = np.ascontiguousarray(x[up][0].reshape(P, NKEYS, D).transpose(1, 0, 2))
    a["filt_w1_2"], a["filt_w2_2"], a["filt_w3_2"] = x["filt_w1_2"][0], x["filt_w2_2"][0], x["filt_w3_2"][0]
    a["filt_vec"] = np.stack([x[n][0] for n in ("filt_b1_2", "filt_freq1_2", "filt_b2_2", "filt_freq2_2")], 1)
    a["filt_decay_2"] = x["filt_decay_2"][0]
    cols = {"lb": np.concatenate([channel(v) for v in x["hgrn_lb_logits_2"]], 1),
            "conv_w": np.concatenate([channel(v) for v in x["hyena_conv_w_2"][0]], 1),
            "conv_b": channel(x["hyena_conv_b_2"][0])}
    for name in GAINS:
        if name not in cols:
            cols[name] = channel(x[name].reshape(-1))
    a["gains"] = np.concatenate([cols[name] for name in GAINS], 1)
    return {k: np.ascontiguousarray(v) for k, v in a.items()}


STOP = None
DEBUG = {}


def kernel(**inputs):
    import concourse.bacc as bacc
    from concourse.bass_utils import run_bass_kernel_spmd

    nc = bacc.Bacc("TRN2", target_bir_lowering=False, num_devices=1)
    arrays, dram = {}, {}
    for name, a in lay_out(inputs).items():
        arrays[f"in_{name}"] = a
        dram[name] = nc.dram_tensor(f"in_{name}", a.shape, mybir.dt.from_np(a.dtype), kind="ExternalInput").ap()
    dram["bias_scratch"] = nc.dram_tensor("bias_scratch", (NSA_H, 2 * T), F32, kind="Internal").ap()
    out = nc.dram_tensor("out_yT", (P, KD, T), F32, kind="ExternalOutput").ap()
    debug = {n: nc.dram_tensor(f"dbg_{n}", s, F32, kind="ExternalOutput").ap() for n, s in DEBUG.items()}
    program(nc, dram, out, STOP, debug)
    result = run_bass_kernel_spmd(nc, [arrays], core_ids=[0]).results[0]["out_yT"]
    return np.ascontiguousarray(result.transpose(2, 1, 0)).reshape(1, T, D)
```

```python
from contextlib import ExitStack

import concourse.bass as bass
from concourse import mybir
import numpy as np

T, D, P = 256, 1024, 128
NT, KD = T // P, D // P
EPS = 1e-6
NEG_INF = -1e30
GLA_H, GLA_DK, GLA_RANK = 4, 64, 16
GLA_TAU = 16.0
NSA_H, NSA_G, NSA_DH = 8, 2, 64
HPG = NSA_H // NSA_G
CMP_BLOCK, CMP_STRIDE, CMP_HIDDEN = 32, 16, 128
N_CMP = (T - CMP_BLOCK) // CMP_STRIDE + 1
BUCKETS, MAX_DIST = 32, 2048
XA_H, XA_DH = 4, D // 4
PEER_H, NKEYS, TOPK = 8, 128, 16
HG_H = 8
BANDS = 16
EMB = 1 + 2 * BANDS
FILT_H = 64
LEVELS = [64, 32, 16, 8, 4, 2, 1]

F32 = mybir.dt.float32
F32R = mybir.dt.float32r
U32 = mybir.dt.uint32
ALU = mybir.AluOpType
ACT = mybir.ActivationFunctionType
AX = mybir.AxisListType.X

GAINS = {}
_at = 0
for _name, _width in [("norm_mix", 8), ("norm_xattn", 8), ("norm_mem", 8), ("norm_ffn", 8), ("norm_final", 8),
                      ("gla_gate_b", 2), ("gla_out_norm", 1), ("norm_mix_g_2", 8), ("lb", 16), ("hgrn_norm_g_2", 1),
                      ("conv_w", 72), ("conv_b", 24), ("hyena_bias_2", 8), ("norm_ffn_g_2", 8), ("norm_final_g_2", 8)]:
    GAINS[_name] = (_at, _at + _width)
    _at += _width
N_GAINS = _at


class Queue:

    def __init__(self, sem, one_at_a_time):
        self.items, self.sem, self.count, self.seen = [], sem, 0, {}
        self.one_at_a_time = one_at_a_time

    def wait(self, marks):
        for sem, value in marks:
            if value > self.seen.get(sem.name, 0):
                self.seen[sem.name] = value
                self.items.append([lambda e, sem=sem, value=value: e.wait_ge(sem, value), None, 0])

    def do(self, build, after=()):
        if self.one_at_a_time and self.count:
            self.wait([(self.sem, self.count)])
        self.wait(after)
        self.tail = [build, None, 0]
        self.items.append(self.tail)
        if self.one_at_a_time:
            return self.last

    @property
    def last(self):
        if self.tail[1] is None:
            self.count += 1
            self.tail[1], self.tail[2] = self.sem, 1
        return (self.sem, self.count)

    def play(self, engine):
        for build, sem, by in self.items:
            ins = build(engine)
            if sem is not None:
                ins.then_inc(sem, by)


def tt(q, out, a, b, op, after=()):
    return q.do(lambda e: e.tensor_tensor(out, a, b, op), after)


def ts(q, out, a, s1, op0, s2=None, op1=None, after=()):
    if op1 is None:
        return q.do(lambda e: e.tensor_scalar(out, a, s1, None, op0), after)
    return q.do(lambda e: e.tensor_scalar(out, a, s1, s2, op0, op1), after)


def stt(q, out, a, s, b, op0, op1, after=()):
    return q.do(lambda e: e.scalar_tensor_tensor(out=out, in0=a, scalar=s, in1=b, op0=op0, op1=op1), after)


def copy(q, out, a, after=()):
    return q.do(lambda e: e.tensor_copy(out, a), after)


def fill(q, out, value, after=()):
    return q.do(lambda e: e.memset(out, value), after)


def reduce(q, out, a, op, after=()):
    return q.do(lambda e: e.tensor_reduce(out, a, AX, op), after)


def recip(q, out, a, after=()):
    return q.do(lambda e: e.reciprocal(out, a), after)


def act(q, out, a, func, scale=1.0, bias=0.0, after=()):
    return q.do(lambda e: e.activation(out, a, func, bias=bias, scale=scale), after)


def mm(q, out, lhsT, rhs, start=True, stop=True, after=()):
    return q.do(lambda e: e.matmul(out, lhsT, rhs, start=start, stop=stop), after)


def tr(q, out, a, ident, after=()):
    return q.do(lambda e: e.transpose(out, a, ident), after)


def scan(q, out, reset, x, after=()):
    return q.do(lambda e: e.tensor_tensor_scan(out, reset, x, 0.0, ALU.mult, ALU.add), after)


def overwrite(q, out, mask, data, after=()):
    return q.do(lambda e: e.copy_predicated(out, mask.bitcast(U32), data), after)


def over(ap, n, axis):
    shape = list(ap.shape)
    return ap.unsqueeze(axis).broadcast_to(shape[:axis] + [n] + shape[axis:])


def t5_bucket(dist):
    n = np.maximum(dist, 0)
    exact = BUCKETS // 2
    ratio = np.log(np.maximum(n, 1).astype(np.float32) / np.float32(exact)) / np.float32(np.log(MAX_DIST / exact))
    large = np.minimum(exact + (ratio * (BUCKETS - exact)).astype(np.int32), BUCKETS - 1)
    return np.where(n < exact, n, large)


def constants():
    f = np.float32
    c = {}
    c["ident"] = np.eye(P, dtype=f)
    s, t = np.meshgrid(np.arange(P), np.arange(P), indexing="ij")
    masks = []
    for causal in (True, False):
        for m in LEVELS:
            same = s // (2 * m) == t // (2 * m)
            s2, t2 = s // m % 2, t // m % 2
            masks.append(same & ((s2 == 0) & (t2 == 1) if causal else s2 != t2))
    c["masks"] = np.stack([x.astype(f) for x in masks], 1)
    c["reset"] = np.tile((np.arange(T) % P != 0).astype(f), (P, 1))
    dist = np.arange(2 * T) - (T - 1)
    c["bucket_of_dist"] = (t5_bucket(dist)[None, :] == np.arange(BUCKETS)[:, None]).astype(f)
    c["some_block"] = (np.arange(P) >= CMP_BLOCK - 1).astype(f)[:, None]
    c["iota"] = np.tile(np.arange(P, dtype=f), (P, 1))
    j, s = np.meshgrid(np.arange(T), np.arange(T), indexing="ij")
    angle = np.pi * (((2 * j + 1) * s) % (4 * T)) / (2 * T)
    for name, m in (("cos", np.cos(angle)), ("sin", np.sin(angle))):
        c[name + "_js"] = m.astype(f).reshape(NT, P, T).transpose(1, 0, 2)
        c[name + "_sj"] = m.T.astype(f).reshape(NT, P, T).transpose(1, 0, 2)
    pos = np.arange(T, dtype=f)
    tt_ = (pos / f(T - 1)).astype(f)
    bands = np.linspace(1e-4, BANDS - 1, BANDS, dtype=f)
    ang = (f(2.0 * np.pi / T) * pos[:, None] * bands[None, :]).astype(f)
    c["filter_z"] = np.concatenate([tt_[:, None], np.cos(ang), -np.sin(ang)], 1).T.astype(f)
    c["minus_t"] = (-tt_).reshape(NT, P).T
    c["not_first"] = (pos > 0).astype(f).reshape(NT, P).T
    return {k: np.ascontiguousarray(v) for k, v in c.items()}


class Core:

    SLOTS = 3
    PARTS = 3
    AHEAD = 2

    def __init__(self, nc, ctx, dram):
        self.nc, self.ctx, self.dram = nc, ctx, dram
        self.V = Queue(self.sem("vector_done"), True)
        self.S = Queue(self.sem("scalar_done"), True)
        self.G = Queue(self.sem("gpsimd_done"), True)
        self.PE = Queue(self.sem("tensor_done"), False)
        self.DMA = Queue(self.sem("sync_done"), False)
        self.psum = ctx.enter_context(nc.psum_tensor("psum", [P, 4096], F32))
        self.bank_read = [[] for _ in range(8)]
        self.ring = self.sb("weight_ring", [P, self.SLOTS, 1024])
        self.parts = self.sb("weight_parts", [P, self.PARTS, 2, 1024], dtype=F32R)
        self.parts_read = [[] for _ in range(self.PARTS)]
        self.low_by = self.V
        self.jobs = []
        self.ring_sem = [self.sem(f"slot_loaded_{i}") for i in range(self.SLOTS)]
        self.slot_read = [[] for _ in range(self.SLOTS)]
        self.units = 0
        self.n_small = 0
        self.next_bank = 0

    def sem(self, name):
        return self.ctx.enter_context(self.nc.semaphore(name))

    def sb(self, name, shape, ctx=None, dtype=F32):
        return (ctx or self.ctx).enter_context(self.nc.sbuf_tensor(name, shape, dtype))

    def bank(self, b, n=1):
        return self.psum[:, 512 * b:512 * (b + n)]

    def load(self, out, src, after=()):
        sem = self.sem(f"loaded_{self.n_small}")
        self.n_small += 1
        self.DMA.wait(after)
        self.DMA.items.append([lambda e: e.dma_start(out, src), sem, 16])
        return (sem, 16)

    def split(self, x, high, low, after=(), by=None):
        m = act(self.S, high, x, ACT.Copy, after=after)
        return tt(by or self.V, low, x, high.bitcast(F32), ALU.subtract, after=[m] + list(after))

    def unit(self, src):
        slot, turn, u = self.units % self.SLOTS, self.units // self.SLOTS, self.units % self.PARTS
        self.units += 1
        self.DMA.wait(self.slot_read[slot])
        out = self.ring[:, slot, :]
        self.DMA.items.append([lambda e: e.dma_start(out, src), self.ring_sem[slot], 16])
        came = (self.ring_sem[slot], 16 * (turn + 1))
        m = self.split(out, self.parts[:, u, 0, :], self.parts[:, u, 1, :], [came] + self.parts_read[u],
                       self.low_by)
        self.slot_read[slot] = [m]
        return u, m

    def product(self, out, stationary, moving, first, last):
        (sh, sl), (mh, ml) = stationary, moving
        mm(self.PE, out, sh, mh, first, False)
        mm(self.PE, out, sh, ml, False, False)
        mm(self.PE, out, sl, mh, False, last)

    def barrier(self):
        self.flush()
        marks = [q.last for q in (self.V, self.S, self.G, self.PE)]
        for q in (self.V, self.S, self.G, self.PE, self.DMA):
            q.wait(marks)

    def take_bank(self):
        b = self.next_bank
        self.next_bank = (b + 1) % 8
        return b

    def submit(self, src, run):
        self.jobs.append((self.unit(src), run))
        if len(self.jobs) > self.AHEAD:
            self.work_off()

    def work_off(self):
        (u, m), run = self.jobs.pop(0)
        run(u, m)

    def flush(self):
        while self.jobs:
            self.work_off()

    def channels(self, src, acts, evac, after=()):
        after = list(after)

        def run(u, m):
            w = self.parts[:, u, :, :].rearrange("p x (k c) -> p x k c", k=KD)
            b = self.take_bank()
            out = self.bank(b)[:, 0:T]
            self.PE.wait([m] + self.bank_read[b] + after)
            for k in range(KD):
                self.product(out, (w[:, 0, k, :], w[:, 1, k, :]), (acts[0][:, k, :], acts[1][:, k, :]),
                             k == 0, k == KD - 1)
            self.parts_read[u] = [self.PE.last]
            self.bank_read[b] = [evac(out, self.PE.last)]

        self.submit(src, run)

    def tokens(self, src, acts, evac, after=()):
        after = list(after)

        def run(u, m):
            w = self.parts[:, u, :, :].rearrange("p x (k c) -> p x k c", k=KD)
            b = self.take_bank()
            out = self.bank(b)[:, 0:NT * P].rearrange("p (i c) -> p i c", i=NT)
            self.PE.wait([m] + self.bank_read[b] + after)
            for i in range(NT):
                tile = slice(P * i, P * i + P)
                for k in range(KD):
                    self.product(out[:, i, :], (acts[0][:, k, tile], acts[1][:, k, tile]),
                                 (w[:, 0, k, :], w[:, 1, k, :]), k == 0, k == KD - 1)
            self.parts_read[u] = [self.PE.last]
            self.bank_read[b] = [evac(out, self.PE.last)]

        self.submit(src, run)

    def rstd(self, total_bank, n, tmp, after):
        out = self.bank(total_bank)[:, 0:T]
        m = ts(self.V, tmp, out, 1.0 / n, ALU.mult, EPS, ALU.add, after=after)
        self.bank_read[total_bank] = [m]
        m = act(self.S, tmp, tmp, ACT.Sqrt, after=[m])
        return recip(self.V, tmp, tmp, after=[m])

    def split_norm(self, x, gain, parts, work, tmp, after=()):
        m = self.rmsnorm(x, gain, work, work, tmp, after)
        return self.split(work[:, :, :], parts[0][:, :, :], parts[1][:, :, :], [m] + list(after))

    def rmsnorm(self, x, gain, out, work, tmp, after=()):
        m = act(self.S, work[:, :, :], x[:, :, :], ACT.Square, after=list(after) + [self.V.last])
        b = self.take_bank()
        self.PE.wait([m] + self.bank_read[b])
        for k in range(KD):
            mm(self.PE, self.bank(b)[:, 0:T], self.ones[:, :], work[:, k, :], k == 0, k == KD - 1)
        self.rstd(b, D, tmp[:, :], [self.PE.last])
        for k in range(KD):
            m = stt(self.V, out[:, k, :], x[:, k, :], gain[:, k:k + 1], tmp[:, :], ALU.mult, ALU.mult,
                    after=list(after))
        return m

    def softmax(self, s, e, mx, z, heads, n, coef=None):
        reduce(self.V, mx, s, ALU.max)
        m = tt(self.V, s, s, over(mx, n, 2), ALU.subtract)
        m = act(self.S, e, s, ACT.Exp, after=[m])
        reduce(self.V, z, e, ALU.add, after=[m])
        m = recip(self.V, z, z)
        if coef is not None:
            m = tt(self.V, z, z, coef, ALU.mult)
        return tt(self.G, e, e, over(z, n, 2), ALU.mult, after=[m])


def halves(ap, m):
    if len(ap.shape) == 3:
        ap = ap.rearrange("p a t -> p (a t)")
    return ap.rearrange("p (b h m) -> p b h m", h=2, m=m)


def gla(c, ctx, q, k, gate, v, gr, out_gain, o, started):
    V, S, G, PE = c.V, c.S, c.G, c.PE
    b = c.sb("gla_b", [P, 2, T], ctx)
    e = c.sb("gla_e", [P, 2, T], ctx)
    qq = c.sb("gla_qq", [P, 2, 2, T], ctx)
    kk = c.sb("gla_kk", [P, 2, 2, T], ctx)
    at = c.sb("gla_scores", [P, 2, 2, NT, P], ctx)
    across = c.sb("gla_scores_across", [P, 2, 2, P], ctx)
    fill(G, at[:, :, :, :, :], 0.0)
    for j in range(2):
        scan(V, b[:, j, :], c.reset[:, :], gate[:, j, :], started)
    read = [[], []]
    merged = G.last
    for n, m in enumerate([P] + LEVELS + [0]):
        u = n % 2
        if m:
            bb, ee = halves(b[:, :, :], m), halves(e[:, :, :], m)
            if m == P:
                a = tt(V, ee[:, :, 0, :], bb[:, :, 0, :], over(bb[:, :, 0, m - 1], m, 2), ALU.subtract)
                a = copy(V, ee[:, :, 1, :], bb[:, :, 1, :])
            else:
                ref = bb[:, :, 0, m - 1]
                a = tt(V, ee[:, :, 0, :], bb[:, :, 0, :], over(ref, m, 2), ALU.subtract)
                a = tt(V, ee[:, :, 1, :], bb[:, :, 1, :], over(ref, m, 2), ALU.subtract)
            a = act(S, e[:, :, :], e[:, :, :], ACT.Abs, after=[a])
            a = act(S, e[:, :, :], e[:, :, :], ACT.Exp, scale=-1.0)
            tt(V, qq[:, u, :, :], q[:, :, :], e[:, :, :], ALU.mult, after=[a] + read[u])
            a = tt(V, kk[:, u, :, :], k[:, :, :], e[:, :, :], ALU.mult)
            ql, kl = qq[:, u, :, :], kk[:, u, :, :]
            PE.wait([a])
        else:
            ql, kl = q, k
        pair = 2 * (n % 4)
        PE.wait(c.bank_read[pair] + c.bank_read[pair + 1])
        for r in range(2):
            rows = slice(64 * r, 64 * r + 64)
            for j in range(2):
                if m == P:
                    mm(PE, c.bank(pair + r)[:, P * j:P * j + P], kl[rows, j, 0:P], ql[rows, j, P:T])
                else:
                    for i in range(NT):
                        tile = slice(P * i, P * i + P)
                        col = P * (2 * j + i)
                        mm(PE, c.bank(pair + r)[:, col:col + P], kl[rows, j, tile], ql[rows, j, tile])
        read[u] = [PE.last]
        src = c.bank(pair, 2).rearrange("p (r x) -> p r x", r=2)
        if m == P:
            a = copy(V, across[:, :, :, :].rearrange("p r j t -> p r (j t)"), src[:, :, 0:2 * P], after=[PE.last])
        else:
            mask = c.masks[:, n - 1, :] if m else c.ident[:, :]
            a = overwrite(V, at[:, :, :, :, :].rearrange("p r j i t -> p (r j i) t"), over(mask, 8, 1),
                          c.bank(pair, 2).rearrange("p (x t) -> p x t", t=P), [PE.last, merged])
        c.bank_read[pair] = c.bank_read[pair + 1] = [a]
    sq = c.sb("gla_sq", [P, GLA_H, T], ctx)
    tmp = c.sb("gla_tmp", [P, T], ctx)
    act(S, gr[:, :, :], gr[:, :, :], ACT.Silu)
    for h in range(GLA_H):
        j, r = h // 2, h % 2
        bk = c.take_bank()
        PE.wait([a] + c.bank_read[bk])
        vh = v[:, :, P * h:P * h + P]
        mm(PE, c.bank(bk)[:, 0:P], vh[:, 0, :], at[:, r, j, 0, :])
        mm(PE, c.bank(bk)[:, P:T], vh[:, 0, :], across[:, r, j, :], True, False)
        mm(PE, c.bank(bk)[:, P:T], vh[:, 1, :], at[:, r, j, 1, :], False, True)
        c.bank_read[bk] = [act(S, o[:, h, :], c.bank(bk)[:, 0:T], ACT.Copy, after=[PE.last])]
    head_norm(c, o, GLA_H, sq, tmp, out_gain, gr)


def head_norm(c, o, heads, sq, tmp, gain, gated):
    m = act(c.S, sq[:, :, :], o[:, :, :], ACT.Square)
    for h in range(heads):
        bk = c.take_bank()
        mm(c.PE, c.bank(bk)[:, 0:T], c.ones[:, :], sq[:, h, :], after=[m] + c.bank_read[bk])
        c.rstd(bk, P, tmp[:, :], [c.PE.last])
        stt(c.V, o[:, h, :], o[:, h, :], gain, tmp[:, :], ALU.mult, ALU.mult)
        tt(c.V, o[:, h, :], o[:, h, :], gated[:, h, :], ALU.mult)


def compress(c, ctx, name, kv, kv_done, pos_src, w1_src):
    V, S, PE = c.V, c.S, c.PE
    w1 = c.sb(name + "_w1", [P, CMP_BLOCK, CMP_HIDDEN], ctx)
    pos = c.sb(name + "_pos", [P, CMP_BLOCK], ctx)
    blocks = c.sb(name + "_blocks", [P, CMP_BLOCK, N_CMP], ctx)
    hid = c.sb(name + "_hid", [P, NSA_G, N_CMP], ctx)
    w1_came = [c.load(w1[64 * g:64 * g + 64, :, :], w1_src) for g in range(NSA_G)]
    pos_came = [c.load(pos[64 * g:64 * g + 64, :], pos_src) for g in range(NSA_G)]
    width = CMP_STRIDE * N_CMP
    for half in range(CMP_BLOCK // CMP_STRIDE):
        src = kv[:, CMP_STRIDE * half:CMP_STRIDE * half + width].rearrange("p (n r) -> p r n", r=CMP_STRIDE)
        r = slice(CMP_STRIDE * half, CMP_STRIDE * (half + 1))
        m = tt(V, blocks[:, r, :], src, over(pos[:, r], N_CMP, 2), ALU.add, after=pos_came + [kv_done])
    for g in range(NSA_G):
        bk = c.take_bank()
        rows = slice(64 * g, 64 * g + 64)
        PE.wait([m] + w1_came + c.bank_read[bk])
        for r in range(CMP_BLOCK):
            mm(PE, c.bank(bk)[:, 0:N_CMP], w1[rows, r, :], blocks[rows, r, :], r == 0, r == CMP_BLOCK - 1)
        c.bank_read[bk] = [act(S, hid[:, g, :], c.bank(bk)[:, 0:N_CMP], ACT.Gelu_apprx_tanh, after=[PE.last])]
    return hid


def nsa(c, ctx, q, kv, vt, gates, o, projected):
    V, S, G, PE = c.V, c.S, c.G, c.PE
    table = c.sb("bias_table", [BUCKETS, NSA_H], ctx)
    onehot = c.sb("bias_onehot", [BUCKETS, 2 * T], ctx)
    by_dist = c.sb("bias_by_dist", [NSA_H, 2 * T], ctx)
    came = [c.load(table[:, :], c.dram["rel_bias"]), c.load(onehot[:, :], c.dram["bucket_of_dist"])]
    bk = c.take_bank()
    mm(PE, c.bank(bk)[0:NSA_H, :], table[:, :], onehot[:, :], after=came + c.bank_read[bk])
    c.bank_read[bk] = [copy(V, by_dist[:, :], c.bank(bk)[0:NSA_H, :], after=[PE.last])]
    m = fill(V, by_dist[:, 0:T - 1], NEG_INF)
    scratch = c.dram["bias_scratch"]
    stored = c.load(scratch, by_dist[:, :], after=[m])
    bias = [c.sb("bias_0", [P, NSA_H, P], ctx), c.sb("bias_1", [P, NSA_H, T], ctx)]
    came = [c.load(bias[0][:, :, :], bass.AP(scratch.tensor, T - P, [[1, P], [2 * T, NSA_H], [1, P]]), after=[stored]),
            c.load(bias[1][:, :, :], bass.AP(scratch.tensor, P, [[1, P], [2 * T, NSA_H], [1, T]]), after=[stored])]
    k_cmp = c.sb("k_cmp", [P, N_CMP], ctx)
    v_cmp = c.sb("v_cmp", [N_CMP, P], ctx)
    early = P // CMP_STRIDE - 1
    v_early = c.sb("v_cmp_early", [early, P], ctx)
    with ExitStack() as inner:
        hid_k = compress(c, inner, "cmp_k", kv["kc"], projected, c.dram["pos_k"], c.dram["cmp_k_w1"])
        hid_v = compress(c, inner, "cmp_v", kv["vc"], projected, c.dram["pos_v"], c.dram["cmp_v_w1"])
        w2 = c.sb("cmp_w2", [P, 2, NSA_DH], inner)
        w2_came = [c.load(w2[:, 0, :], c.dram["cmp_k_w2"]), c.load(w2[:, 1, :], c.dram["cmp_v_w2"])]
        bk = c.take_bank()
        PE.wait([S.last] + w2_came + c.bank_read[bk])
        for g in range(NSA_G):
            mm(PE, c.bank(bk)[64 * g:64 * g + 64, 0:N_CMP], w2[:, 0, :], hid_k[:, g, :])
        c.bank_read[bk] = [copy(V, k_cmp[:, :], c.bank(bk)[:, 0:N_CMP], after=[PE.last])]
        bk = c.take_bank()
        PE.wait(c.bank_read[bk])
        for g in range(NSA_G):
            mm(PE, c.bank(bk)[0:N_CMP, 64 * g:64 * g + 64], hid_v[:, g, :], w2[:, 1, :])
            mm(PE, c.bank(bk)[0:early, P + 64 * g:P + 64 * g + 64], hid_v[:, g, N_CMP - early:N_CMP], w2[:, 1, :])
        copy(V, v_cmp[:, :], c.bank(bk)[0:N_CMP, 0:P], after=[PE.last])
        c.bank_read[bk] = [copy(V, v_early[:, :], c.bank(bk)[0:early, P:2 * P])]
        c.barrier()

    sig = c.sb("gate_sigmoid", [P, NT, 3 * NSA_H], ctx)
    act(S, sig[:, :, :], gates[:, :, :], ACT.Sigmoid)
    sc = c.sb("cmp_s", [P, NSA_H, N_CMP], ctx)
    s = c.sb("nsa_s", [P, NSA_H, T], ctx)
    e = [c.sb("nsa_e0", [P, NSA_H, T], ctx), c.sb("nsa_e1", [P, NSA_H, T], ctx)]
    mx = c.sb("nsa_max", [P, NSA_H], ctx)
    z = c.sb("nsa_z", [P, 3, NSA_H], ctx)
    pt_cmp = c.sb("nsa_pt_cmp", [N_CMP, NSA_H, P], ctx)
    pt = c.sb("nsa_pt", [P, 2, NSA_H, NT, P], ctx)
    for i in range(NT):
        q_i = slice(P * i, P * i + P)
        n_keys = P * (i + 1)
        n_blocks = N_CMP if i else early
        bk = 0
        PE.wait([V.last] + c.bank_read[0] + c.bank_read[1])
        for g in range(NSA_G):
            rows = slice(64 * g, 64 * g + 64)
            for h in range(HPG):
                mm(PE, c.bank(g)[:, n_blocks * h:n_blocks * (h + 1)], q[rows, h, q_i],
                   k_cmp[rows, N_CMP - n_blocks:N_CMP])
        scv = sc[:, :, 0:n_blocks]
        for g in range(NSA_G):
            hs = slice(HPG * g, HPG * (g + 1))
            steps = bias[i][:, hs, :].rearrange("p h (n r) -> p h n r", r=CMP_STRIDE)[:, :, 0:n_blocks, 0]
            m = tt(V, scv[:, hs, :], c.bank(g)[:, 0:HPG * n_blocks].rearrange("p (h n) -> p h n", h=HPG), steps,
                   ALU.add, after=[PE.last] + came)
        c.bank_read[0] = c.bank_read[1] = [m]
        gate = sig[:, i, :].rearrange("p (h b) -> p b h", b=3)
        m = ts(V, mx[:, :], gate[:, 0, :], c.some_block[:, :], ALU.mult, after=[S.last]) if i == 0 else None
        coef = z[:, 1, :]
        m = copy(V, coef, mx[:, :]) if i == 0 else copy(V, coef, gate[:, 0, :], after=[S.last])
        ec = e[0][:, :, 0:n_blocks]
        m = c.softmax(scv, ec, mx[:, :], z[:, 0, :], NSA_H, n_blocks, coef)
        PE.wait([m] + c.bank_read[0] + c.bank_read[1])
        for h in range(NSA_H):
            tr(PE, c.bank(h // 4)[0:n_blocks, P * (h % 4):P * (h % 4) + P], ec[:, h, :], c.ident[:, :])
        for w in range(2):
            m = act(S, pt_cmp[0:n_blocks, 4 * w:4 * w + 4, :],
                    c.bank(w)[0:n_blocks, :].rearrange("p (h t) -> p h t", h=4), ACT.Copy, after=[PE.last])
            c.bank_read[w] = [m]
        sv = s[:, :, 0:n_keys]
        for w, name in enumerate(("ks", "kw")):
            PE.wait(c.bank_read[4] + c.bank_read[5] + c.bank_read[6] + c.bank_read[7])
            for g in range(NSA_G):
                rows = slice(64 * g, 64 * g + 64)
                area = c.bank(4 + 2 * g, 2)
                for h in range(HPG):
                    mm(PE, area[:, n_keys * h:n_keys * (h + 1)], q[rows, h, q_i], kv[name][rows, T - n_keys:T])
            for g in range(NSA_G):
                hs = slice(HPG * g, HPG * (g + 1))
                area = c.bank(4 + 2 * g, 2)[:, 0:HPG * n_keys].rearrange("p (h n) -> p h n", h=HPG)
                m = tt(V, sv[:, hs, :], area, bias[i][:, hs, :], ALU.add, after=[PE.last] + came)
                c.bank_read[4 + 2 * g] = c.bank_read[5 + 2 * g] = [m]
            ev = e[w][:, :, 0:n_keys]
            m = c.softmax(sv, ev, mx[:, :], z[:, 0, :], NSA_H, n_keys, gate[:, 1 + w, :])
            for jj in range(i + 1):
                for half in range(2):
                    b0 = c.bank(2 + half)
                    PE.wait([m] + c.bank_read[2 + half])
                    for h in range(4):
                        tr(PE, b0[:, P * h:P * h + P], ev[:, 4 * half + h, P * jj:P * jj + P], c.ident[:, :])
                    c.bank_read[2 + half] = [act(S, pt[:, w, 4 * half:4 * half + 4, jj, :],
                                                 b0.rearrange("p (h t) -> p h t", h=4), ACT.Copy, after=[PE.last])]
        vc_i = v_cmp if i else v_early
        PE.wait([S.last] + c.bank_read[1])
        for h in range(HPG):
            for g in range(NSA_G):
                out = c.bank(1)[64 * g:64 * g + 64, P * h:P * h + P]
                cols = slice(64 * g, 64 * g + 64)
                mm(PE, out, vc_i[0:n_blocks, cols], pt_cmp[0:n_blocks, HPG * g + h, :], True, False)
                for w, name in enumerate(("vs", "vw")):
                    for jj in range(i + 1):
                        mm(PE, out, vt[name][:, NT - 1 - i + jj, cols], pt[:, w, HPG * g + h, jj, :], False,
                           w == 1 and jj == i)
        c.bank_read[1] = [copy(V, o[:, :, q_i], c.bank(1).rearrange("p (h t) -> p h t", h=HPG), after=[PE.last])]
        S.wait([PE.last])


def first_mixer(c, h, xn, work, tmp):
    V, S, G, PE = c.V, c.S, c.G, c.PE
    with ExitStack() as ctx:
        m = c.split_norm(h, c.gain("norm_mix"), xn, work, tmp, after=[c.h_came, c.gains_came])
        rev_ctx = ctx.enter_context(ExitStack())
        xr = [c.sb(f"xn_reversed_{x}", [P, KD, T], rev_ctx, F32R) for x in range(2)]
        for x in range(2):
            rev = copy(G, xr[x][:, :, :], xn[x][:, :, ::-1], after=[m])
        gq = c.sb("gla_q", [P, 2, T], ctx)
        gk = c.sb("gla_k", [P, 2, T], ctx)
        gate = c.sb("gla_gate", [P, 2, T], ctx)
        gv = c.sb("gla_v", [P, NT, 512], ctx)
        gr = c.sb("gla_r", [P, 4, T], ctx)
        o = c.sb("mix_o", [P, 8, T], ctx)
        nq = c.sb("nsa_q", [P, HPG, T], ctx)
        kv = {n: c.sb("nsa_" + n, [P, T], ctx) for n in ("kc", "vc", "ks", "kw")}
        vt = {n: c.sb("nsa_" + n, [P, NT, P], ctx) for n in ("vs", "vw")}
        small_w = c.sb("small_w", [P, KD, 40], ctx)
        glr = c.sb("gla_lr", [GLA_RANK, T], ctx)
        gates = c.sb("nsa_gates", [P, NT, 24], ctx)
        w2 = c.sb("gate_w2", [GLA_RANK, T], ctx)
        small_came = c.load(small_w[:, :, :], c.dram["w_in_small"])
        w2_came = c.load(w2[:, :], c.dram["gla_gate_w2"])
        PE.wait([m])

        def keep(dst, scale=1.0):
            return lambda out, done: act(S, dst, out, ACT.Copy, scale=scale, after=[done])

        w = c.dram["w_in"]
        for j in range(2):
            c.channels(w[j], xn, keep(gq[:, j, :], GLA_DK ** -0.5))
        for j in range(2):
            c.channels(w[2 + j], xn, keep(gk[:, j, :]))
        for j in range(4):
            c.tokens(w[4 + j], xn, keep(gv[:, :, P * j:P * j + P]))
        for j in range(4):
            c.channels(w[8 + j], xn, keep(gr[:, j, :]))
        for j in range(4):
            c.channels(w[12 + j], xn, keep(nq[:, j, :], NSA_DH ** -0.5))
        for n, name in ((16, "kc"), (17, "vc"), (18, "ks"), (20, "kw")):
            c.channels(w[n], xr, keep(kv[name][:, :]), after=[rev])
        for n, name in ((19, "vs"), (21, "vw")):
            c.tokens(w[n], xr, keep(vt[name][:, :, :]))
        c.flush()
        whole = work
        bk = c.take_bank()
        PE.wait([small_came] + c.bank_read[bk])
        for k in range(KD):
            mm(PE, c.bank(bk)[0:GLA_RANK, 0:T], small_w[:, k, 0:GLA_RANK], whole[:, k, :], k == 0, k == KD - 1)
        a = act(S, glr[:, :], c.bank(bk)[0:GLA_RANK, 0:T], ACT.Copy, after=[PE.last])
        c.bank_read[bk] = [a]
        bk = c.take_bank()
        PE.wait(c.bank_read[bk])
        for i in range(NT):
            for k in range(KD):
                mm(PE, c.bank(bk)[:, 24 * i:24 * i + 24], whole[:, k, P * i:P * i + P], small_w[:, k, 16:40],
                   k == 0, k == KD - 1)
        c.bank_read[bk] = [act(S, gates[:, :, :], c.bank(bk)[:, 0:48].rearrange("p (i c) -> p i c", i=NT), ACT.Copy,
                               after=[PE.last])]
        za = c.sb("gate_z", [P, 2, T], ctx)
        for j in range(2):
            bk = c.take_bank()
            mm(PE, c.bank(bk)[:, 0:T], w2[:, P * j:P * j + P], glr[:, :], after=[a, w2_came] + c.bank_read[bk])
            bcol = c.gain("gla_gate_b")[:, j:j + 1]
            c.bank_read[bk] = [ts(V, gate[:, j, :], c.bank(bk)[:, 0:T], bcol, ALU.add, after=[PE.last])]
        act(S, za[:, :, :], gate[:, :, :], ACT.Abs, after=[V.last])
        act(S, za[:, :, :], za[:, :, :], ACT.Exp, scale=-1.0)
        m = act(S, za[:, :, :], za[:, :, :], ACT.Ln, bias=1.0)
        ts(V, gate[:, :, :], gate[:, :, :], 0.0, ALU.min, after=[m])
        tt(V, gate[:, :, :], gate[:, :, :], za[:, :, :], ALU.subtract)
        m = ts(V, gate[:, :, :], gate[:, :, :], 1.0 / GLA_TAU, ALU.mult)
        with ExitStack() as inner:
            gla(c, inner, gq[:, :, :], gk[:, :, :], gate, gv, gr, c.gain("gla_out_norm"), o[:, 0:4, :], [m, S.last])
            c.dump("gla_o", o[:, 0:4, :])
            c.barrier()
        with ExitStack() as inner:
            nsa(c, inner, nq, kv, vt, gates, o[:, 4:8, :], S.last)
            c.dump("nsa_o", o[:, 4:8, :])
            m = c.split(o[:, :, :], xn[0][:, :, :], xn[1][:, :, :], [V.last])
            for n in range(KD):
                c.channels(c.dram["w_out"][n], xn, lambda out, done, n=n: tt(V, h[:, n, :], h[:, n, :], out, ALU.add,
                                                                         after=[done]), after=[V.last])
            c.barrier()


def cross_attention(c, h, xn, work, tmp):
    V, S, G, PE = c.V, c.S, c.G, c.PE
    with ExitStack() as ctx:
        mem = c.sb("mem", [P, KD, T], ctx)
        memn = [c.sb(f"memn_{x}", [P, KD, T], ctx, F32R) for x in range(2)]
        mem_came = c.load(mem[:, :, :], c.dram["memT"])
        m1 = c.split_norm(mem, c.gain("norm_mem"), memn, work, tmp, after=[mem_came])
        m = c.split_norm(h, c.gain("norm_xattn"), xn, work, tmp, after=[PE.last])
        q = c.sb("xa_q", [P, KD, T], ctx)
        k = c.sb("xa_k", [P, KD, T], ctx)
        v = c.sb("xa_v", [P, NT, D], ctx)
        o = c.sb("xa_o", [P, KD, T], ctx)
        s = c.sb("xa_s", [P, XA_H, T], ctx)
        e = c.sb("xa_e", [P, XA_H, T], ctx)
        mx = c.sb("xa_max", [P, XA_H], ctx)
        z = c.sb("xa_z", [P, XA_H], ctx)
        pt = c.sb("xa_pt", [P, XA_H, NT, T], ctx)
        PE.wait([m])

        def keep(dst, scale=1.0):
            return lambda out, done: act(S, dst, out, ACT.Copy, scale=scale, after=[done])

        for n in range(KD):
            c.channels(c.dram["xa_wk"][n], memn, keep(k[:, n, :]))
        for n in range(KD):
            c.channels(c.dram["xa_wq"][n], xn, keep(q[:, n, :], XA_DH ** -0.5))
        for n in range(KD):
            c.tokens(c.dram["xa_wv"][n], memn, keep(v[:, :, P * n:P * n + P]))
        c.flush()
        for i in range(NT):
            tile = slice(P * i, P * i + P)
            PE.wait([S.last] + c.bank_read[0] + c.bank_read[1])
            for hd in range(XA_H):
                for j in range(2):
                    mm(PE, c.bank(0, 2)[:, T * hd:T * hd + T], q[:, 2 * hd + j, tile], k[:, 2 * hd + j, :],
                       j == 0, j == 1)
            m = copy(V, s[:, :, :], c.bank(0, 2).rearrange("p (h m) -> p h m", h=XA_H), after=[PE.last, S.last])
            c.bank_read[0] = c.bank_read[1] = [m]
            m = c.softmax(s[:, :, :], e[:, :, :], mx[:, :], z[:, :], XA_H, T)
            for j in range(NT):
                PE.wait([m] + c.bank_read[2 + j])
                for hd in range(XA_H):
                    tr(PE, c.bank(2 + j)[:, P * hd:P * hd + P], e[:, hd, P * j:P * j + P], c.ident[:, :])
                c.bank_read[2 + j] = [act(S, pt[:, :, j, tile], c.bank(2 + j).rearrange("p (h t) -> p h t", h=XA_H),
                                          ACT.Copy, after=[PE.last])]
        for n in range(KD):
            bk = c.take_bank()
            PE.wait([S.last] + c.bank_read[bk])
            for j in range(NT):
                mm(PE, c.bank(bk)[:, 0:T], v[:, j, P * n:P * n + P], pt[:, n // 2, j, :], j == 0, j == NT - 1)
            c.bank_read[bk] = [copy(V, o[:, n, :], c.bank(bk)[:, 0:T], after=[PE.last])]
        c.split(o[:, :, :], xn[0][:, :, :], xn[1][:, :, :], [V.last])
        for n in range(KD):
            c.channels(c.dram["xa_wo"][n], xn, lambda out, done, n=n: tt(V, h[:, n, :], h[:, n, :], out, ALU.add,
                                                                      after=[done]), after=[V.last])
        c.barrier()


def top16(c, vals, idx, src, spare):
    V = c.V
    V.do(lambda e: e.max(out=vals[:, 0:8], in_=src))
    V.do(lambda e: e.max_index(out=idx[:, 0:8], in_max=vals[:, 0:8], in_values=src))
    V.do(lambda e: e.match_replace(out=spare, in_to_replace=vals[:, 0:8], in_values=src, imm_value=-3e38))
    V.do(lambda e: e.max(out=vals[:, 8:16], in_=spare))
    return V.do(lambda e: e.max_index(out=idx[:, 8:16], in_max=vals[:, 8:16], in_values=spare))


def routing(c, q, sk, area, half_dim, pairs, queries_done):
    V, S, PE = c.V, c.S, c.PE
    at = [0]

    def cut(*shape):
        n = int(np.prod(shape))
        at[0] += n
        names = "abcd"[:len(shape)]
        view = area[:, at[0] - n:at[0]]
        return view.rearrange(f"p ({' '.join(names)}) -> p {' '.join(names)}", **dict(zip(names, shape)))

    scores = cut(PEER_H, 2, NKEYS)
    cand = cut(PEER_H, TOPK, TOPK)
    eq = cut(PEER_H, TOPK, TOPK)
    spare = cut(2 * NKEYS)
    vals = cut(PEER_H, 2, TOPK)
    idx = cut(PEER_H, 2, TOPK).bitcast(U32)
    idxf = cut(PEER_H, 2, TOPK)
    top = cut(PEER_H, TOPK)
    pos = cut(PEER_H, TOPK).bitcast(U32)
    part = cut(PEER_H, TOPK).bitcast(U32)
    partf = cut(PEER_H, TOPK)
    res = cut(3, PEER_H, TOPK)
    zs = cut(PEER_H)
    iota16 = over(over(c.iota[:, 0:TOPK], TOPK, 1), PEER_H, 1)
    for i in range(NT):
        tile = slice(P * i, P * i + P)
        PE.wait(queries_done + [x for b in range(4) for x in c.bank_read[b]])
        if half_dim == 64:
            for hd in range(PEER_H):
                for a in range(2):
                    mm(PE, c.bank(2 * a, 2)[:, P * hd:P * hd + P], q[64 * a:64 * a + 64, hd, tile],
                       sk[64 * a:64 * a + 64, hd, :])
            for a in range(2):
                m = act(S, scores[:, :, a, :], c.bank(2 * a, 2).rearrange("p (h n) -> p h n", h=PEER_H), ACT.Copy,
                        after=[PE.last, V.last])
        else:
            for n in range(2 * PEER_H):
                mm(PE, c.bank(0, 4)[:, P * n:P * n + P], q[:, n, tile], sk[:, n, :])
            m = act(S, scores, c.bank(0, 4).rearrange("p (h a n) -> p h a n", h=PEER_H, a=2), ACT.Copy,
                    after=[PE.last, V.last])
        for b in range(4):
            c.bank_read[b] = [m]
        V.wait([m])
        for hd in range(PEER_H):
            for a in range(2):
                top16(c, vals[:, hd, a, :], idx[:, hd, a, :], scores[:, hd, a, :], spare[:, 0:NKEYS])
                yield
        copy(V, idxf, idx)
        tt(V, cand, over(vals[:, :, 0, :], TOPK, 3), over(vals[:, :, 1, :], TOPK, 2), ALU.add)
        yield
        for hd in range(PEER_H):
            top16(c, top[:, hd, :], pos[:, hd, :], cand[:, hd, :, :].rearrange("p a b -> p (a b)"), spare)
            yield
        for a in range(2):
            if a == 0:
                ts(V, part, pos, 4, ALU.logical_shift_right)
            else:
                ts(V, part, pos, 15, ALU.bitwise_and)
            copy(V, partf, part)
            tt(V, eq, over(partf, TOPK, 3), iota16, ALU.is_equal)
            yield
            tt(V, eq, eq, over(idxf[:, :, a, :], TOPK, 2), ALU.mult)
            reduce(V, res[:, a, :, :], eq, ALU.add)
            yield
        m = tt(V, res[:, 2, :, :], top, over(top[:, :, 0], TOPK, 2), ALU.subtract)
        m = act(S, res[:, 2, :, :], res[:, 2, :, :], ACT.Exp, after=[m])
        reduce(V, zs, res[:, 2, :, :], ALU.add, after=[m])
        recip(V, zs, zs)
        m = tt(V, res[:, 2, :, :], res[:, 2, :, :], over(zs, TOPK, 2), ALU.mult)
        yield
        PE.wait([m] + c.bank_read[0])
        for x in range(3):
            tr(PE, c.bank(0)[:, P * x:P * x + P], res[:, x, :, :].rearrange("p h k -> p (h k)"), c.ident[:, :])
        c.bank_read[0] = [copy(V, pairs[:, :, tile], c.bank(0)[:, 0:3 * P].rearrange("p (x t) -> p x t", x=3),
                               after=[PE.last])]
        yield


def peer(c, h, xn, work, tmp, name, gain, half_dim, wq, subkeys, down, up):
    V, S, G, PE = c.V, c.S, c.G, c.PE
    n_q = 2 * PEER_H * half_dim // P
    with ExitStack() as ctx:
        experts = c.sb(name + "_experts", [P, NKEYS, T], ctx)
        pairs = c.sb(name + "_pairs", [P, 3, T], ctx)
        first_kept = 64
        area = experts[:, first_kept:NKEYS, :].rearrange("p a t -> p (a t)")
        sk = area[:, 0:n_q * P].rearrange("p (k n) -> p k n", k=n_q)
        q = area[:, n_q * P:n_q * (P + T)].rearrange("p (k t) -> p k t", k=n_q)
        c.split_norm(h, gain, xn, work, tmp)
        sk_came = c.load(sk, subkeys)
        for n in range(n_q):
            c.channels(wq[n], xn, lambda out, done, n=n: act(S, q[:, n, :], out, ACT.Copy, after=[done]))
        c.flush()
        route = routing(c, q, sk, area[:, n_q * (P + T):], half_dim, pairs, [S.last, sk_came])
        routed = [False]

        def go_on(n):
            for _ in range(n):
                if not routed[0]:
                    routed[0] = next(route, "end") == "end"

        c.next_bank = 4
        c.low_by = G
        for n in range(NKEYS):
            if n == first_kept:
                while not routed[0]:
                    go_on(1)
                done_routing = [V.last, PE.last]
                c.low_by = V

            def gelu(out, done, n=n):
                if c.next_bank < 4:
                    c.next_bank = 4
                go_on(2)
                return act(S, experts[:, n, :], out, ACT.Gelu_apprx_tanh,
                           after=[done] + (done_routing if n >= first_kept else []))

            if n == first_kept:
                c.flush()
            c.channels(down[n], xn, gelu)
        c.flush()
        hidden_done = S.last

        GROUP = 4
        onehots = work[:, :, :].rearrange("p k (i n) -> p i k n", i=2)
        used = [[], []]
        for g in range(T // GROUP):
            u, toks = g % 2, slice(GROUP * g, GROUP * (g + 1))
            sl = slice(GROUP * u, GROUP * (u + 1))
            first, second = onehots[:, 0, sl, :], onehots[:, 1, sl, :]
            iota = over(c.iota[:, :], GROUP, 1)
            m = tt(V, first, iota, over(pairs[:, 0, toks], P, 2), ALU.is_equal, after=used[u])
            m = tt(G, first, first, over(pairs[:, 2, toks], P, 2), ALU.mult, after=[m])
            m2 = tt(V, second, iota, over(pairs[:, 1, toks], P, 2), ALU.is_equal)
            b = g % 8
            PE.wait([m, m2] + c.bank_read[b])
            for t in range(GROUP):
                mm(PE, c.bank(b)[:, P * t:P * t + P], first[:, t, :], second[:, t, :])
            used[u] = [PE.last]
            if g:
                gate_in(c, experts, g - 1, GROUP, before, hidden_done)
            before = PE.last
        gate_in(c, experts, g, GROUP, before, hidden_done)

        NB = 2
        coef = c.sb(name + "_coef", [P, NB, 2, T], ctx, F32R)
        coef_read = [[] for _ in range(NB)]
        c.PE.wait([x for b in range(4) for x in c.bank_read[b]])
        made = [None] * NKEYS

        def make_coef(n):
            u = n % NB
            made[n] = c.split(experts[:, n, :], coef[:, u, 0, :], coef[:, u, 1, :], coef_read[u] + [V.last])

        for n in range(NKEYS):
            def run(part, came, n=n):
                if n == NKEYS - 2:
                    make_coef(n + 1)
                u = n % NB
                PE.wait([came, made[n]])
                for i in range(NT):
                    tile = slice(P * i, P * i + P)
                    for half in range(2):
                        cols = slice(512 * half, 512 * half + 512)
                        c.product(c.bank(2 * i + half), (coef[:, u, 0, tile], coef[:, u, 1, tile]),
                                  (c.parts[:, part, 0, cols], c.parts[:, part, 1, cols]), n == 0, n == NKEYS - 1)
                c.parts_read[part] = coef_read[u] = [PE.last]
            if n == 0:
                make_coef(0)
            elif n >= c.AHEAD:
                make_coef(n - c.AHEAD + 1)
            c.submit(up[n], run)
        c.flush()
        y = [work[:, 4 * i:4 * i + 4, :].rearrange("p k t -> p (k t)") for i in range(NT)]
        done = PE.last
        for i in range(NT):
            for b in (2 * i, 2 * i + 1):
                m = copy(V, y[i][:, 512 * (b % 2):512 * (b % 2) + 512], c.bank(b), after=[done])
                c.bank_read[b] = [m]
        for k in range(KD):
            b = 4 + k % 4
            PE.wait([m] + c.bank_read[b])
            for i in range(NT):
                tr(PE, c.bank(b)[:, P * i:P * i + P], y[i][:, P * k:P * k + P], c.ident[:, :])
            c.bank_read[b] = [tt(V, h[:, k, :], h[:, k, :], c.bank(b)[:, 0:T], ALU.add, after=[PE.last])]
        c.barrier()


def gate_in(c, experts, g, group, done, hidden_done):
    dst = experts[:, :, group * g:group * (g + 1)]
    gates = c.bank(g % 8).rearrange("p (t i) -> p i t", t=group)
    c.bank_read[g % 8] = [tt(c.V, dst, dst, gates, ALU.mult, after=[done, hidden_done])]


def hgrn(c, ctx, q, zf, zb, v, o):
    V, S, G, PE = c.V, c.S, c.G, c.PE
    lb = c.sb("hg_lb", [P, KD], ctx)
    one_minus = c.sb("hg_one_minus", [P, KD], ctx)
    t2 = c.sb("hg_t2", [P, 2, KD], ctx)
    lbl = c.gain("lb").rearrange("p (l k) -> p l k", l=2)
    tt(V, lb[:, :], lbl[:, 0, :], lbl[:, 1, :], ALU.max)
    m = tt(V, t2[:, :, :], lbl, over(lb[:, :], 2, 1), ALU.subtract)
    m = act(S, t2[:, :, :], t2[:, :, :], ACT.Exp, after=[m])
    tt(V, one_minus[:, :], t2[:, 0, :], t2[:, 1, :], ALU.add, after=[m])
    recip(V, one_minus[:, :], one_minus[:, :])
    tt(V, lb[:, :], t2[:, 0, :], one_minus[:, :], ALU.mult)
    ts(V, one_minus[:, :], lb[:, :], -1.0, ALU.mult, 1.0, ALU.add)
    kf = c.sb("hg_kf", [P, HG_H, T], ctx)
    kb = c.sb("hg_kb", [P, HG_H, T], ctx)
    for z, k in ((zf, kf), (zb, kb)):
        act(S, k[:, :, :], z[:, :, :], ACT.Sigmoid, scale=-1.0)
        m = act(S, z[:, :, :], z[:, :, :], ACT.Sigmoid)
        for hd in range(HG_H):
            ts(V, k[:, hd, :], k[:, hd, :], one_minus[:, hd:hd + 1], ALU.mult, after=[m])
            ts(V, z[:, hd, :], z[:, hd, :], one_minus[:, hd:hd + 1], ALU.mult, lb[:, hd:hd + 1], ALU.add)
        m = ts(V, z[:, :, :], z[:, :, :], 2.0 ** -62, ALU.max)
        act(S, z[:, :, :], z[:, :, :], ACT.Ln, after=[m])
    bf = c.sb("hg_bf", [P, HG_H, T], ctx)
    bb = c.sb("hg_bb", [P, HG_H, T], ctx)
    for hd in range(HG_H):
        scan(V, bf[:, hd, :], c.reset[:, :], zf[:, hd, :], [S.last])
        scan(V, bb[:, hd, ::-1], c.reset[:, :], zb[:, hd, ::-1])
    eq, ek = zf, zb
    qq = c.sb("hg_qq", [P, HG_H, T], ctx)
    kk = c.sb("hg_kk", [P, HG_H, T], ctx)
    at = c.sb("hg_scores", [P, HG_H, NT, P], ctx)
    fwd = c.sb("hg_scores_fwd", [P, HG_H, P], ctx)
    bwd = c.sb("hg_scores_bwd", [P, HG_H, P], ctx)
    read = []
    m0 = None
    for n, m in enumerate([P] + LEVELS + [0]):
        if m:
            F, B, EQ, EK = halves(bf[:, :, :], m), halves(bb[:, :, :], m), halves(eq[:, :, :], m), halves(ek[:, :, :], m)
            rf, rb = over(F[:, :, 0, m - 1], m, 2), over(B[:, :, 1, 0], m, 2)
            if m == P:
                copy(V, EQ[:, :, 1, :], F[:, :, 1, :])
                a1 = copy(V, EQ[:, :, 0, :], B[:, :, 0, :])
            else:
                tt(V, EQ[:, :, 1, :], F[:, :, 1, :], rf, ALU.subtract)
                a1 = tt(V, EQ[:, :, 0, :], B[:, :, 0, :], rb, ALU.subtract)
            tt(G, EK[:, :, 0, :], rf, F[:, :, 0, :], ALU.subtract, after=[V.last])
            a2 = tt(G, EK[:, :, 1, :], rb, B[:, :, 1, :], ALU.subtract)
            e1 = act(S, eq[:, :, :], eq[:, :, :], ACT.Exp, after=[a1])
            e2 = act(S, ek[:, :, :], ek[:, :, :], ACT.Exp, after=[a2])
            tt(V, qq[:, :, :], q[:, :, :], eq[:, :, :], ALU.mult, after=[e1] + read)
            KF, KB, KK = halves(kf[:, :, :], m), halves(kb[:, :, :], m), halves(kk[:, :, :], m)
            tt(G, KK[:, :, 0, :], KF[:, :, 0, :], EK[:, :, 0, :], ALU.mult, after=[e2] + read)
            a = tt(G, KK[:, :, 1, :], KB[:, :, 1, :], EK[:, :, 1, :], ALU.mult)
            ql = qq
        else:
            a = tt(G, kk[:, :, :], kf[:, :, :], kb[:, :, :], ALU.add, after=read)
            ql = q
        b0 = 4 * (n % 2)
        PE.wait([V.last, a] + [x for b in range(b0, b0 + 4) for x in c.bank_read[b]])
        area = c.bank(b0, 4).rearrange("p (h i t) -> p h i t", h=HG_H, i=NT)
        for hd in range(HG_H):
            for i in range(NT):
                s_tile = slice(P * i, P * i + P)
                t_tile = slice(P * (1 - i), P * (1 - i) + P) if m == P else s_tile
                mm(PE, area[:, hd, i, :], kk[:, hd, s_tile], ql[:, hd, t_tile])
        read = [PE.last]
        if m == P:
            copy(V, fwd[:, :, :], area[:, :, 0, :], after=read)
            a = copy(V, bwd[:, :, :], area[:, :, 1, :])
            fill(V, at[:, :, :, :], 0.0)
        else:
            mask = c.masks[:, len(LEVELS) + n - 1, :] if m else c.ident[:, :]
            a = overwrite(V, at[:, :, :, :].rearrange("p h i t -> p (h i) t"), over(mask, HG_H * NT, 1),
                          c.bank(b0, 4).rearrange("p (x t) -> p x t", t=P), read)
        for b in range(b0, b0 + 4):
            c.bank_read[b] = [a]
    for hd in range(HG_H):
        bk = c.take_bank()
        PE.wait([V.last] + c.bank_read[bk])
        v0, v1 = v[:, 0, P * hd:P * hd + P], v[:, 1, P * hd:P * hd + P]
        out = c.bank(bk)
        mm(PE, out[:, 0:P], v0, at[:, hd, 0, :], True, False)
        mm(PE, out[:, 0:P], v1, bwd[:, hd, :], False, True)
        mm(PE, out[:, P:T], v0, fwd[:, hd, :], True, False)
        mm(PE, out[:, P:T], v1, at[:, hd, 1, :], False, True)
        c.bank_read[bk] = [act(S, o[:, hd, :], out[:, 0:T], ACT.Copy, after=[PE.last])]


def filters(c, ctx, both):
    V, S, PE = c.V, c.S, c.PE
    z = c.sb("filt_z", [EMB, T], ctx)
    w1 = c.sb("filt_w1", [EMB, FILT_H], ctx)
    w2 = c.sb("filt_w2", [FILT_H, FILT_H], ctx)
    w3 = c.sb("filt_w3", [FILT_H, 2 * D], ctx)
    vec = c.sb("filt_vec", [FILT_H, 4], ctx)
    decay = c.sb("filt_decay", [P, 2 * D], ctx)
    window = c.sb("filt_window", [P, 2 * D], ctx)
    cols = c.sb("filt_cols", [P, 2 * NT], ctx)
    hid = c.sb("filt_hid", [FILT_H, T], ctx)
    turns = c.sb("filt_turns", [FILT_H, T], ctx)
    came = [c.load(z[:, :], c.dram["filter_z"]), c.load(w1[:, :], c.dram["filt_w1_2"]),
            c.load(w2[:, :], c.dram["filt_w2_2"]), c.load(w3[:, :], c.dram["filt_w3_2"]),
            c.load(vec[:, :], c.dram["filt_vec"]), c.load(decay[:, :], c.dram["filt_decay_2"].partition_broadcast(P)),
            c.load(cols[:, 0:NT], c.dram["minus_t"]), c.load(cols[:, NT:2 * NT], c.dram["not_first"])]
    ROUND = 1.5 * 2.0 ** 23
    TWO_PI = [6.28125, 0.0019350051879882812, 3.019916e-07]
    act(S, decay[:, :], decay[:, :], ACT.Abs, after=came)
    last = None
    for n, (w, x) in enumerate(((w1, z), (w2, hid))):
        bk = c.take_bank()
        mm(PE, c.bank(bk)[0:FILT_H, 0:T], w[:, :], x[:, :], after=came + c.bank_read[bk] + ([last] if last else []))
        m = ts(V, hid[:, :], c.bank(bk)[0:FILT_H, 0:T], vec[:, 2 * n:2 * n + 1], ALU.add,
               vec[:, 2 * n + 1:2 * n + 2], ALU.mult, after=[PE.last] + came)
        c.bank_read[bk] = [m]
        ts(V, turns[:, :], hid[:, :], 1.0 / (2.0 * np.pi), ALU.mult, ROUND, ALU.add)
        ts(V, turns[:, :], turns[:, :], ROUND, ALU.subtract)
        for part in TWO_PI:
            stt(V, hid[:, :], turns[:, :], -part, hid[:, :], ALU.mult, ALU.add)
        ts(V, hid[:, :], hid[:, :], 3.1415925, ALU.min)
        m = ts(V, hid[:, :], hid[:, :], -3.1415925, ALU.max)
        last = act(S, hid[:, :], hid[:, :], ACT.Sin, after=[m])
    for i in range(NT):
        wide = act(S, window[:, :], decay[:, :], ACT.Exp, scale=cols[:, i:i + 1], after=[V.last])
        PE.wait([last] + [x for b in range(4) for x in c.bank_read[b]])
        for b in range(4):
            mm(PE, c.bank(b), hid[:, P * i:P * i + P], w3[:, 512 * b:512 * b + 512])
        m = tt(V, window[:, :], window[:, :], c.bank(0, 4), ALU.mult, after=[wide, PE.last])
        for b in range(4):
            c.bank_read[b] = [m]
        ts(V, window[:, D:2 * D], window[:, D:2 * D], cols[:, NT + i:NT + i + 1], ALU.mult)
        tt(V, both[:, i, 0, :], window[:, 0:D], window[:, D:2 * D], ALU.add)
        tt(V, both[:, i, 1, :], window[:, 0:D], window[:, D:2 * D], ALU.subtract)


def hyena(c, ctx, xn, yb):
    V, S, G, PE = c.V, c.S, c.G, c.PE
    both = c.sb("filters", [P, NT, 2, D], ctx)
    with ExitStack() as inner:
        filters(c, inner, both)
        c.dump("filters", both[:, :, :, :])
        c.barrier()
    basis = {}
    came = []
    for name in ("cos_sj", "sin_sj", "cos_js", "sin_js"):
        basis[name] = c.sb(name, [P, NT, T], ctx)
        came.append(c.load(basis[name][:, :, :], c.dram[name]))
    x0 = c.sb("hy_x0", [P, KD, T], ctx)
    u = c.sb("hy_u", [P, KD, T], ctx)
    x = c.sb("hy_x", [P, T], ctx)
    ut = c.sb("hy_ut", [P, NT, D], ctx)
    fu = c.sb("hy_fu", [P, NT, 2, D], ctx)
    fk = c.sb("hy_fk", [P, NT, 2, D], ctx)
    conv_w = c.gain("conv_w").rearrange("p (j n) -> p j n", j=3)
    conv_b = c.gain("conv_b")

    def short_conv(n, dst):
        def evac(out, done):
            ts(V, dst, out, conv_w[:, 1, n:n + 1], ALU.mult, conv_b[:, n:n + 1], ALU.add, after=[done])
            stt(V, dst[:, 1:T], out[:, 0:T - 1], conv_w[:, 0, n:n + 1], dst[:, 1:T], ALU.mult, ALU.add)
            return stt(V, dst[:, 0:T - 1], out[:, 1:T], conv_w[:, 2, n:n + 1], dst[:, 0:T - 1], ALU.mult, ALU.add)
        return evac

    w = c.dram["w_in_2"]
    for n in range(KD):
        c.channels(w[40 + n], xn, short_conv(n, x0[:, n, :]))
        c.channels(w[48 + n], xn, short_conv(8 + n, u[:, n, :]))


        def times_x1(out, done, n=n):
            m = short_conv(16 + n, x[:, :])(out, done)
            tt(V, u[:, n, :], u[:, n, :], x[:, :], ALU.mult)
            return m

        c.channels(w[56 + n], xn, times_x1)
    c.flush()
    for n in range(KD):
        bk = c.take_bank()
        PE.wait([V.last] + c.bank_read[bk])
        for i in range(NT):
            tr(PE, c.bank(bk)[:, P * i:P * i + P], u[:, n, P * i:P * i + P], c.ident[:, :])
        c.bank_read[bk] = [act(S, ut[:, :, P * n:P * n + P], c.bank(bk)[:, 0:T].rearrange("p (i c) -> p i c", i=NT),
                               ACT.Copy, after=[PE.last])]
    PE.wait(came + [S.last])
    for j in range(NT):
        for a, name in enumerate(("cos_sj", "sin_sj")):
            for src, dst in ((lambda i: ut[:, i, :], fu), (lambda i, a=a: both[:, i, a, :], fk)):
                for half in range(2):
                    bk = c.take_bank()
                    PE.wait(c.bank_read[bk])
                    for i in range(NT):
                        mm(PE, c.bank(bk), basis[name][:, i, P * j:P * j + P], src(i)[:, 512 * half:512 * half + 512],
                           i == 0, i == NT - 1)
                    c.bank_read[bk] = [act(S, dst[:, j, a, 512 * half:512 * half + 512], c.bank(bk), ACT.Copy,
                                           after=[PE.last])]
    y = both
    t1, t2 = ut[:, 0, :], ut[:, 1, :]
    for j in range(NT):
        uc, us, kc, ks = fu[:, j, 0, :], fu[:, j, 1, :], fk[:, j, 0, :], fk[:, j, 1, :]
        tt(V, t1, uc, kc, ALU.mult, after=[S.last, PE.last])
        tt(V, t2, us, ks, ALU.mult)
        tt(V, y[:, j, 0, :], t1, t2, ALU.subtract)
        tt(V, t1, uc, ks, ALU.mult)
        tt(V, t2, us, kc, ALU.mult)
        m = tt(V, y[:, j, 1, :], t1, t2, ALU.add)
    for n in range(KD):
        bk = c.take_bank()
        PE.wait([m] + c.bank_read[bk])
        for step, (j, a) in enumerate(((0, 0), (0, 1), (1, 0), (1, 1))):
            mm(PE, c.bank(bk)[:, 0:T], y[:, j, a, P * n:P * n + P], basis[("cos_js", "sin_js")[a]][:, j, :],
               step == 0, step == 3)
        ts(V, u[:, n, :], u[:, n, :], c.gain("hyena_bias_2")[:, n:n + 1], ALU.mult, after=[PE.last])
        c.bank_read[bk] = [stt(V, u[:, n, :], c.bank(bk)[:, 0:T], 1.0 / T, u[:, n, :], ALU.mult, ALU.add)]
        tt(V, u[:, n, :], u[:, n, :], x0[:, n, :], ALU.mult)
    c.dump("hy", u[:, :, :])
    up = [c.sb(f"hy_u_{x}", [P, KD, T], ctx, F32R) for x in range(2)]
    c.split(u[:, :, :], up[0][:, :, :], up[1][:, :, :], [V.last])
    for n in range(KD):
        c.channels(c.dram["w_branch_b_2"][n], up, lambda out, done, n=n: act(S, yb[:, n, :], out, ACT.Copy,
                                                                         after=[done]), after=[V.last])


def second_mixer(c, h, xn, work, tmp):
    V, S, G, PE = c.V, c.S, c.G, c.PE
    with ExitStack() as ctx:
        m = c.split_norm(h, c.gain("norm_mix_g_2"), xn, work, tmp)
        PE.wait([m])
        ya = c.sb("ya", [P, KD, T], ctx)
        yb = c.sb("yb", [P, KD, T], ctx)
        w = c.dram["w_in_2"]

        def keep(dst, func=ACT.Copy):
            return lambda out, done: act(S, dst, out, func, after=[done])

        with ExitStack() as inner:
            q = c.sb("hg_q", [P, HG_H, T], inner)
            zf = c.sb("hg_zf", [P, HG_H, T], inner)
            zb = c.sb("hg_zb", [P, HG_H, T], inner)
            v = c.sb("hg_v", [P, NT, D], inner)
            o = yb
            for n in range(KD):
                c.channels(w[n], xn, keep(q[:, n, :], ACT.Silu))
            for n in range(KD):
                c.channels(w[8 + n], xn, keep(zf[:, n, :]))
            for n in range(KD):
                c.channels(w[16 + n], xn, keep(zb[:, n, :]))
            for n in range(KD):
                c.tokens(w[24 + n], xn, keep(v[:, :, P * n:P * n + P]))
            c.flush()
            with ExitStack() as deep:
                hgrn(c, deep, q, zf, zb, v, o)
                c.dump("hgrn_o", o[:, :, :])
                c.barrier()
            og = q
            for n in range(KD):
                c.channels(w[32 + n], xn, keep(og[:, n, :], ACT.Silu))
            c.flush()
            head_norm(c, o, HG_H, work, tmp, c.gain("hgrn_norm_g_2"), og)
            op = [c.sb(f"hg_o_{x}", [P, KD, T], inner, F32R) for x in range(2)]
            c.split(o[:, :, :], op[0][:, :, :], op[1][:, :, :], [V.last])
            for n in range(KD):
                c.channels(c.dram["w_branch_a_2"][n], op, keep(ya[:, n, :]))
            c.barrier()
        with ExitStack() as inner:
            hyena(c, inner, xn, yb)
            c.barrier()
        g = work
        for half, y in ((0, ya), (1, yb)):
            for n in range(KD):
                def evac(out, done, n=n, y=y):
                    m = act(S, g[:, n, :], out, ACT.Sigmoid, after=[done, V.last])
                    tt(V, y[:, n, :], y[:, n, :], g[:, n, :], ALU.mult, after=[m])
                    return m
                c.channels(w[64 + 8 * half + n], xn, evac)
        c.flush()
        m = tt(V, ya[:, :, :], ya[:, :, :], yb[:, :, :], ALU.add)
        c.split(ya[:, :, :], xn[0][:, :, :], xn[1][:, :, :], [m, PE.last])
        for n in range(KD):
            c.channels(c.dram["w_out_2"][n], xn, lambda out, done, n=n: tt(V, h[:, n, :], h[:, n, :], out, ALU.add,
                                                                        after=[done]), after=[V.last])
        c.barrier()


def program(nc, dram, out, stop=None, debug=None):
    with ExitStack() as ctx:
        c = Core(nc, ctx, dram)
        c.stop = stop
        V, S, G, PE = c.V, c.S, c.G, c.PE
        h = c.sb("h", [P, KD, T])
        xn = [c.sb(f"acts_{x}", [P, KD, T], dtype=F32R) for x in ("high", "low")]
        work = c.sb("work", [P, KD, T])
        tmp = c.sb("tmp", [P, T])
        c.gains = c.sb("gains", [P, N_GAINS])
        c.ident = c.sb("ident", [P, P])
        c.ones = c.sb("ones", [P, P])
        c.iota = c.sb("iota", [P, P])
        c.some_block = c.sb("some_block", [P, 1])
        c.gain = lambda name: c.gains[:, GAINS[name][0]:GAINS[name][1]]
        c.h_came = c.load(h[:, :, :], dram["xT"])
        c.gains_came = c.load(c.gains[:, :], dram["gains"])
        came = [c.gains_came] + [c.load(x[:, :], dram[n]) for x, n in (
            (c.ident, "ident"), (c.iota, "iota"), (c.some_block, "some_block"))]
        fill(V, c.ones[:, :], 1.0)
        for q in (V, S, G, PE):
            q.wait(came)
        PE.wait([V.last])
        outs = []

        def dump(name, ap):
            if debug is None or name not in debug:
                return
            marks = [q.last for q in (V, S, G, PE)]
            outs.append(c.load(debug[name], ap, after=marks))
        c.dump = dump

        with ExitStack() as mctx:
            c.masks = c.sb("masks", [P, 2 * len(LEVELS), P], mctx)
            c.reset = c.sb("reset", [P, T], mctx)
            V.wait([c.load(c.masks[:, :, :], dram["masks"]), c.load(c.reset[:, :], dram["reset"])])
            first_mixer(c, h, xn, work, tmp)
        c.dump("h1", h[:, :, :])
        if stop != "h1":
            cross_attention(c, h, xn, work, tmp)
            c.dump("h2", h[:, :, :])
        if stop not in ("h1", "h2"):
            peer(c, h, xn, work, tmp, "peer_1", c.gain("norm_ffn"), 64, dram["peer_wq"], dram["peer_subkeys"],
                 dram["peer_down"], dram["peer_up"])
            c.rmsnorm(h, c.gain("norm_final"), h, work, tmp)
            c.dump("h3", h[:, :, :])
        if stop not in ("h1", "h2", "h3"):
            c.barrier()
            with ExitStack() as mctx:
                c.masks = c.sb("masks_2", [P, 2 * len(LEVELS), P], mctx)
                c.reset = c.sb("reset_2", [P, T], mctx)
                V.wait([c.load(c.masks[:, :, :], dram["masks"]), c.load(c.reset[:, :], dram["reset"])])
                second_mixer(c, h, xn, work, tmp)
            c.dump("h4", h[:, :, :])
        if stop is None:
            peer(c, h, xn, work, tmp, "peer_2", c.gain("norm_ffn_g_2"), 128, dram["peer_w_q_2"],
                 dram["peer_subkeys_2"], dram["peer_u_2"], dram["peer_v_2"])
        m = c.rmsnorm(h, c.gain("norm_final_g_2"), work, work, tmp)
        outs.append(c.load(out, work[:, :, :], after=[m]))
        c.DMA.wait(outs)

        block = ctx.enter_context(nc.Block())

        @block.sync
        def _(engine):
            c.DMA.play(engine)

        @block.gpsimd
        def _(engine):
            G.play(engine)

        @block.scalar
        def _(engine):
            S.play(engine)

        @block.vector
        def _(engine):
            V.play(engine)

        @block.tensor
        def _(engine):
            PE.play(engine)


def lay_out(x):
    def blocks(w, cols=P):
        w = w.reshape(KD, P, -1, cols)
        return np.ascontiguousarray(w.transpose(2, 1, 0, 3)).reshape(w.shape[2], P, KD * cols)

    def channel(v):
        return v.reshape(-1, P).T

    def turned(a):
        return np.ascontiguousarray(a.reshape(T, KD, P).transpose(2, 1, 0))

    a = dict(constants())
    x = {k: np.asarray(v) for k, v in x.items()}
    a["xT"], a["memT"] = turned(x["x"][0]), turned(x["mem"][0])
    w = x["w_in"][0]
    nq = w[:, 1552:2064].reshape(D, NSA_G, HPG, NSA_DH).transpose(0, 2, 1, 3).reshape(D, 512)
    a["w_in"] = blocks(np.concatenate([w[:, 0:1536], nq, w[:, 2064:2832]], 1))
    a["w_in_small"] = np.ascontiguousarray(
        np.concatenate([w[:, 1536:1552], w[:, 2832:2856]], 1).reshape(KD, P, 40).transpose(1, 0, 2))
    wo = x["w_out"][0]
    nsa_rows = wo[512:].reshape(NSA_G, HPG, NSA_DH, D).transpose(1, 0, 2, 3).reshape(512, D)
    a["w_out"] = blocks(np.concatenate([wo[0:512], nsa_rows], 0))
    for name in ("xa_wq", "xa_wk", "xa_wv", "xa_wo", "peer_wq", "w_in_2", "w_branch_a_2", "w_branch_b_2", "w_out_2",
                 "peer_w_q_2"):
        a[name] = blocks(x[name][0])
    a["rel_bias"] = x["rel_bias"]
    a["gla_gate_w2"] = x["gla_gate_w2"][0]
    for n in ("k", "v"):
        a[f"pos_{n}"] = np.ascontiguousarray(x[f"cmp_pos_{n}"][0][::-1].T)
        w1 = x[f"cmp_{n}_w1"][0].reshape(CMP_BLOCK, NSA_DH, CMP_HIDDEN)
        a[f"cmp_{n}_w1"] = np.ascontiguousarray(w1[::-1].transpose(1, 0, 2))
        a[f"cmp_{n}_w2"] = x[f"cmp_{n}_w2"][0]
    sk = x["peer_subkeys"][0].transpose(1, 3, 0, 2)
    a["peer_subkeys"] = np.ascontiguousarray(sk.reshape(P, PEER_H, NKEYS))
    sk = x["peer_subkeys_2"][0].transpose(3, 0, 1, 2)
    a["peer_subkeys_2"] = np.ascontiguousarray(sk.reshape(P, 2 * PEER_H, NKEYS))
    for down, up in (("peer_down", "peer_up"), ("peer_u_2", "peer_v_2")):
        d = x[down][0].reshape(P, NKEYS, KD, P)
        a[down] = np.ascontiguousarray(d.transpose(1, 3, 2, 0)).reshape(NKEYS, P, KD * P)
        a[up] = np.ascontiguousarray(x[up][0].reshape(P, NKEYS, D).transpose(1, 0, 2))
    a["filt_w1_2"], a["filt_w2_2"], a["filt_w3_2"] = x["filt_w1_2"][0], x["filt_w2_2"][0], x["filt_w3_2"][0]
    a["filt_vec"] = np.stack([x[n][0] for n in ("filt_b1_2", "filt_freq1_2", "filt_b2_2", "filt_freq2_2")], 1)
    a["filt_decay_2"] = x["filt_decay_2"][0]
    cols = {"lb": np.concatenate([channel(v) for v in x["hgrn_lb_logits_2"]], 1),
            "conv_w": np.concatenate([channel(v) for v in x["hyena_conv_w_2"][0]], 1),
            "conv_b": channel(x["hyena_conv_b_2"][0])}
    for name in GAINS:
        if name not in cols:
            cols[name] = channel(x[name].reshape(-1))
    a["gains"] = np.concatenate([cols[name] for name in GAINS], 1)
    return {k: np.ascontiguousarray(v) for k, v in a.items()}


STOP = None
DEBUG = {}


def kernel(**inputs):
    import concourse.bacc as bacc
    from concourse.bass_utils import run_bass_kernel_spmd

    nc = bacc.Bacc("TRN2", target_bir_lowering=False, num_devices=1)
    arrays, dram = {}, {}
    for name, a in lay_out(inputs).items():
        arrays[f"in_{name}"] = a
        dram[name] = nc.dram_tensor(f"in_{name}", a.shape, mybir.dt.from_np(a.dtype), kind="ExternalInput").ap()
    dram["bias_scratch"] = nc.dram_tensor("bias_scratch", (NSA_H, 2 * T), F32, kind="Internal").ap()
    out = nc.dram_tensor("out_yT", (P, KD, T), F32, kind="ExternalOutput").ap()
    debug = {n: nc.dram_tensor(f"dbg_{n}", s, F32, kind="ExternalOutput").ap() for n, s in DEBUG.items()}
    program(nc, dram, out, STOP, debug)
    result = run_bass_kernel_spmd(nc, [arrays], core_ids=[0]).results[0]["out_yT"]
    return np.ascontiguousarray(result.transpose(2, 1, 0)).reshape(1, T, D)
```

```python
from contextlib import ExitStack

import concourse.bass as bass
from concourse import mybir
import numpy as np

T, D, P = 256, 1024, 128
NT, KD = T // P, D // P
EPS = 1e-6
NEG_INF = -1e30
GLA_H, GLA_DK, GLA_RANK = 4, 64, 16
GLA_TAU = 16.0
NSA_H, NSA_G, NSA_DH = 8, 2, 64
HPG = NSA_H // NSA_G
CMP_BLOCK, CMP_STRIDE, CMP_HIDDEN = 32, 16, 128
N_CMP = (T - CMP_BLOCK) // CMP_STRIDE + 1
BUCKETS, MAX_DIST = 32, 2048
XA_H, XA_DH = 4, D // 4
PEER_H, NKEYS, TOPK = 8, 128, 16
HG_H = 8
BANDS = 16
EMB = 1 + 2 * BANDS
FILT_H = 64
LEVELS = [64, 32, 16, 8, 4, 2, 1]

F32 = mybir.dt.float32
F32R = mybir.dt.float32r
U32 = mybir.dt.uint32
ALU = mybir.AluOpType
ACT = mybir.ActivationFunctionType
AX = mybir.AxisListType.X

GAINS = {}
_at = 0
for _name, _width in [("norm_mix", 8), ("norm_xattn", 8), ("norm_mem", 8), ("norm_ffn", 8), ("norm_final", 8),
                      ("gla_gate_b", 2), ("gla_out_norm", 1), ("norm_mix_g_2", 8), ("lb", 16), ("hgrn_norm_g_2", 1),
                      ("conv_w", 72), ("conv_b", 24), ("hyena_bias_2", 8), ("norm_ffn_g_2", 8), ("norm_final_g_2", 8)]:
    GAINS[_name] = (_at, _at + _width)
    _at += _width
N_GAINS = _at


class Queue:

    def __init__(self, sem, one_at_a_time):
        self.items, self.sem, self.count, self.seen, self.tail = [], sem, 0, {}, None
        self.one_at_a_time = one_at_a_time

    def wait(self, marks):
        for sem, value in marks:
            if value > self.seen.get(sem.name, 0):
                self.seen[sem.name] = value
                self.items.append([lambda e, sem=sem, value=value: e.wait_ge(sem, value), None, 0])

    def do(self, build, after=()):
        if self.one_at_a_time and self.tail:
            self.wait([self.last])
        self.wait(after)
        return self.go(build)

    def go(self, build):
        self.tail = [build, None, 0]
        self.items.append(self.tail)
        if self.one_at_a_time:
            return self.last

    @property
    def last(self):
        if self.tail[1] is None:
            self.count += 1
            self.tail[1], self.tail[2] = self.sem, 1
        return (self.sem, self.count)

    def play(self, engine):
        for build, sem, by in self.items:
            ins = build(engine)
            if sem is not None:
                ins.then_inc(sem, by)


def tt(q, out, a, b, op, after=()):
    return q.do(lambda e: e.tensor_tensor(out, a, b, op), after)


def ts(q, out, a, s1, op0, s2=None, op1=None, after=()):
    if op1 is None:
        return q.do(lambda e: e.tensor_scalar(out, a, s1, None, op0), after)
    return q.do(lambda e: e.tensor_scalar(out, a, s1, s2, op0, op1), after)


def stt(q, out, a, s, b, op0, op1, after=()):
    return q.do(lambda e: e.scalar_tensor_tensor(out=out, in0=a, scalar=s, in1=b, op0=op0, op1=op1), after)


def copy(q, out, a, after=()):
    return q.do(lambda e: e.tensor_copy(out, a), after)


def fill(q, out, value, after=()):
    return q.do(lambda e: e.memset(out, value), after)


def reduce(q, out, a, op, after=()):
    return q.do(lambda e: e.tensor_reduce(out, a, AX, op), after)


def recip(q, out, a, after=()):
    return q.do(lambda e: e.reciprocal(out, a), after)


def act(q, out, a, func, scale=1.0, bias=0.0, after=()):
    return q.do(lambda e: e.activation(out, a, func, bias=bias, scale=scale), after)


def mm(q, out, lhsT, rhs, start=True, stop=True, after=()):
    return q.do(lambda e: e.matmul(out, lhsT, rhs, start=start, stop=stop), after)


def tr(q, out, a, ident, after=()):
    return q.do(lambda e: e.transpose(out, a, ident), after)


def scan(q, out, reset, x, after=()):
    return q.do(lambda e: e.tensor_tensor_scan(out, reset, x, 0.0, ALU.mult, ALU.add), after)


def onehot(q, out, iota, index, factor):
    return q.go(lambda e: e.tensor_scalar(out, iota, index, factor, ALU.is_equal, ALU.mult))


def overwrite(q, out, mask, data, after=()):
    return q.do(lambda e: e.copy_predicated(out, mask.bitcast(U32), data), after)


def over(ap, n, axis):
    shape = list(ap.shape)
    return ap.unsqueeze(axis).broadcast_to(shape[:axis] + [n] + shape[axis:])


def t5_bucket(dist):
    n = np.maximum(dist, 0)
    exact = BUCKETS // 2
    ratio = np.log(np.maximum(n, 1).astype(np.float32) / np.float32(exact)) / np.float32(np.log(MAX_DIST / exact))
    large = np.minimum(exact + (ratio * (BUCKETS - exact)).astype(np.int32), BUCKETS - 1)
    return np.where(n < exact, n, large)


def constants():
    f = np.float32
    c = {}
    c["ident"] = np.eye(P, dtype=f)
    s, t = np.meshgrid(np.arange(P), np.arange(P), indexing="ij")
    masks = []
    for causal in (True, False):
        for m in LEVELS:
            same = s // (2 * m) == t // (2 * m)
            s2, t2 = s // m % 2, t // m % 2
            masks.append(same & ((s2 == 0) & (t2 == 1) if causal else s2 != t2))
    c["masks"] = np.stack([x.astype(f) for x in masks], 1)
    c["reset"] = np.tile((np.arange(T) % P != 0).astype(f), (P, 1))
    dist = np.arange(2 * T) - (T - 1)
    c["bucket_of_dist"] = (t5_bucket(dist)[None, :] == np.arange(BUCKETS)[:, None]).astype(f)
    c["some_block"] = (np.arange(P) >= CMP_BLOCK - 1).astype(f)[:, None]
    c["iota"] = np.tile(np.arange(P, dtype=f), (P, 1))
    j, s = np.meshgrid(np.arange(T), np.arange(T), indexing="ij")
    angle = np.pi * (((2 * j + 1) * s) % (4 * T)) / (2 * T)
    for name, m in (("cos", np.cos(angle)), ("sin", np.sin(angle))):
        c[name + "_js"] = m.astype(f).reshape(NT, P, T).transpose(1, 0, 2)
        c[name + "_sj"] = m.T.astype(f).reshape(NT, P, T).transpose(1, 0, 2)
    pos = np.arange(T, dtype=f)
    tt_ = (pos / f(T - 1)).astype(f)
    bands = np.linspace(1e-4, BANDS - 1, BANDS, dtype=f)
    ang = (f(2.0 * np.pi / T) * pos[:, None] * bands[None, :]).astype(f)
    c["filter_z"] = np.concatenate([tt_[:, None], np.cos(ang), -np.sin(ang)], 1).T.astype(f)
    c["minus_t"] = (-tt_).reshape(NT, P).T
    c["not_first"] = (pos > 0).astype(f).reshape(NT, P).T
    return {k: np.ascontiguousarray(v) for k, v in c.items()}


class Parts:

    def __init__(self, high, low):
        self.high, self.low, self.marks = high, low, [None] * KD

    def chunk(self, k):
        return self.high[:, k, :], self.low[:, k, :]


def pipeline(makers, width):
    makers, active = list(makers), {}
    for slot in range(min(width, len(makers))):
        active[slot] = makers.pop(0)(slot)
    while active:
        for slot in list(active):
            if next(active[slot], "end") == "end":
                if makers:
                    active[slot] = makers.pop(0)(slot)
                else:
                    del active[slot]
            yield


def together(main, filler, every):
    for n, _ in enumerate(main):
        if n % every == 0:
            next(filler, None)


class Core:

    SLOTS = 3
    PARTS = 3
    AHEAD = 2

    def __init__(self, nc, ctx, dram):
        self.nc, self.ctx, self.dram = nc, ctx, dram
        self.V = Queue(self.sem("vector_done"), True)
        self.S = Queue(self.sem("scalar_done"), True)
        self.G = Queue(self.sem("gpsimd_done"), True)
        self.PE = Queue(self.sem("tensor_done"), False)
        self.DMA = Queue(self.sem("sync_done"), False)
        self.psum = ctx.enter_context(nc.psum_tensor("psum", [P, 4096], F32))
        self.bank_read = [[] for _ in range(8)]
        self.ring = self.sb("weight_ring", [P, self.SLOTS, 1024])
        self.parts = self.sb("weight_parts", [P, self.PARTS, 2, 1024], dtype=F32R)
        self.parts_read = [[] for _ in range(self.PARTS)]
        self.low_by = self.V
        self.jobs = []
        self.prepared = []
        self.fence = []
        self.ring_sem = [self.sem(f"slot_loaded_{i}") for i in range(self.SLOTS)]
        self.slot_read = [[] for _ in range(self.SLOTS)]
        self.units = self.splits = 0

        self.n_small = 0
        self.rotation = list(range(7))

    def sem(self, name):
        return self.ctx.enter_context(self.nc.semaphore(name))

    def sb(self, name, shape, ctx=None, dtype=F32):
        return (ctx or self.ctx).enter_context(self.nc.sbuf_tensor(name, shape, dtype))

    def bank(self, b, n=1):
        return self.psum[:, 512 * b:512 * (b + n)]

    def load(self, out, src, after=()):
        sem = self.sem(f"loaded_{self.n_small}")
        self.n_small += 1
        self.DMA.wait(self.fence + list(after))
        self.DMA.items.append([lambda e: e.dma_start(out, src), sem, 16])
        return (sem, 16)

    def raw_unit(self, src):
        slot, turn = self.units % self.SLOTS, self.units // self.SLOTS
        self.units += 1
        self.DMA.wait(self.slot_read[slot])
        out = self.ring[:, slot, :]
        self.DMA.items.append([lambda e: e.dma_start(out, src), self.ring_sem[slot], 16])
        return slot, (self.ring_sem[slot], 16 * (turn + 1))

    def split(self, x, high, low, after=(), by=None):
        m = act(self.S, high, x, ACT.Copy, after=after)
        return tt(by or self.V, low, x, high.bitcast(F32), ALU.subtract, after=[m] + list(after))

    def unit(self, src):
        u = self.splits % self.PARTS
        self.splits += 1
        slot, came = self.raw_unit(src)
        out = self.ring[:, slot, :]
        m = self.split(out, self.parts[:, u, 0, :], self.parts[:, u, 1, :], [came] + self.parts_read[u],
                       self.low_by)
        self.slot_read[slot] = [m]
        return u, m

    def product(self, out, stationary, moving, first, last):
        (sh, sl), (mh, ml) = stationary, moving
        mm(self.PE, out, sh, mh, first, False)
        mm(self.PE, out, sh, ml, False, False)
        mm(self.PE, out, sl, mh, False, last)

    def barrier(self):
        self.flush()
        self.fence = [q.last for q in (self.V, self.S, self.G, self.PE)]
        for q in (self.V, self.S, self.G, self.PE):
            q.wait(self.fence)

    def take_bank(self):
        self.rotation.append(self.rotation.pop(0))
        return self.rotation[-1]

    def submit(self, src, run):
        self.jobs.append((self.prepared.pop(0) if self.prepared else self.unit(src), run))
        if len(self.jobs) > self.AHEAD:
            self.work_off()

    def work_off(self):
        (u, m), run = self.jobs.pop(0)
        run(u, m)

    def flush(self, *following):
        for src in following:
            self.prepared.append(self.unit(src))
            if self.jobs:
                self.work_off()
        while self.jobs:
            self.work_off()

    def channels(self, src, acts, evac):
        def run(u, m):
            w = self.parts[:, u, :, :].rearrange("p x (k c) -> p x k c", k=KD)
            b = self.take_bank()
            out = self.bank(b)[:, 0:T]
            self.PE.wait([m] + self.bank_read[b])
            for k in range(KD):
                self.PE.wait([acts.marks[k]])
                self.product(out, (w[:, 0, k, :], w[:, 1, k, :]), acts.chunk(k), k == 0, k == KD - 1)
            self.parts_read[u] = [self.PE.last]
            self.bank_read[b] = [evac(out, self.PE.last)]

        self.submit(src, run)

    def tokens(self, srcs, acts, cols, evac):
        banks = []
        n_units = srcs.shape[0]
        n_k = KD // n_units

        def run(u, m, n):
            w = self.parts[:, u, :, :].rearrange("p x (k c) -> p x k c", k=n_k)
            if n == 0:
                banks.extend(self.take_bank() for _ in range(NT))
                self.PE.wait([x for b in banks for x in self.bank_read[b]])
            self.PE.wait([m])
            for i in range(NT):
                tile = slice(P * i, P * i + P)
                for kk in range(n_k):
                    k = n_k * n + kk
                    self.PE.wait([acts.marks[k]])
                    self.product(self.bank(banks[i])[:, 0:cols], (acts.high[:, k, tile], acts.low[:, k, tile]),
                                 (w[:, 0, kk, :], w[:, 1, kk, :]), k == 0, k == KD - 1)
            self.parts_read[u] = [self.PE.last]
            if n == n_units - 1:
                done = self.PE.last
                for i in range(NT):
                    self.bank_read[banks[i]] = [evac(i, self.bank(banks[i])[:, 0:cols], done)]

        for n in range(n_units):
            self.submit(srcs[n], lambda u, m, n=n: run(u, m, n))
            yield

    def rstd(self, total_bank, n, tmp, after):
        out = self.bank(total_bank)[:, 0:T]
        m = ts(self.V, tmp, out, 1.0 / n, ALU.mult, EPS, ALU.add, after=after)
        self.bank_read[total_bank] = [m]
        m = act(self.S, tmp, tmp, ACT.Sqrt, after=[m])
        return recip(self.V, tmp, tmp, after=[m])

    def split_chunk(self, x, parts, k, after=()):
        parts.marks[k] = self.split(x, parts.high[:, k, :], parts.low[:, k, :], after)

    def norm_add(self, x, work, k, made):
        m = tt(self.G, work[:, k, :], x[:, k, :], x[:, k, :], ALU.mult, after=made)
        if k:
            self.norm_sum(work, k - 1)
        self.squared = m

    def norm_sum(self, work, k):
        self.PE.wait([self.squared] + (self.bank_read[7] if k == 0 else []))
        mm(self.PE, self.bank(7)[:, 0:T], self.ones[:, :], work[:, k, :], k == 0, k == KD - 1)

    def norm_finish(self, x, gain, out, work, tmp, parts=None, after=(), each=None, summed=False):
        if not summed:
            self.norm_sum(work, KD - 1)
        self.rstd(7, D, tmp[:, :], [self.PE.last])
        for k in range(KD):
            m = stt(self.V, out[:, k, :], x[:, k, :], gain[:, k:k + 1], tmp[:, :], ALU.mult, ALU.mult)
            if parts is not None:
                self.split_chunk(out[:, k, :], parts, k, [m] + list(after))
            if each is not None:
                each(k, m)
        return m



    def add_to_h(self, h, work, n, what, done):
        m = tt(self.V, h[:, n, :], h[:, n, :], what, ALU.add, after=[done])
        self.norm_add(h, work, n, [m])
        return m


def halves(ap, m):
    if len(ap.shape) == 3:
        ap = ap.rearrange("p a t -> p (a t)")
    return ap.rearrange("p (b h m) -> p b h m", h=2, m=m)


def gla(c, ctx, q, k, gate, v, gr, out_gain, o, started, finish_gates):
    V, S, G, PE = c.V, c.S, c.G, c.PE
    b = c.sb("gla_b", [P, 2, T], ctx)
    e = c.sb("gla_e", [P, 2, 2, T], ctx)
    qq = c.sb("gla_qq", [P, 2, 2, T], ctx)
    kk = c.sb("gla_kk", [P, 2, 2, T], ctx)
    at = c.sb("gla_scores", [P, 2, 2, NT, P], ctx)
    across = c.sb("gla_scores_across", [P, 2, 2, P], ctx)
    cleared = fill(G, at[:, :, :, :, :], 0.0)
    for j in range(2):
        scan(V, b[:, j, :], c.reset[:, :], gate[:, j, :], started)
    read = [[], []]

    def level(n, m, u):
        eu = e[:, u, :, :]
        if m:
            bb, ee = halves(b[:, :, :], m), halves(eu, m)
            if m == P:
                tt(V, ee[:, :, 0, :], bb[:, :, 0, :], over(bb[:, :, 0, m - 1], m, 2), ALU.subtract)
                a = copy(V, ee[:, :, 1, :], bb[:, :, 1, :])
            else:
                ref = bb[:, :, 0, m - 1]
                tt(V, ee[:, :, 0, :], bb[:, :, 0, :], over(ref, m, 2), ALU.subtract)
                a = tt(V, ee[:, :, 1, :], bb[:, :, 1, :], over(ref, m, 2), ALU.subtract)
            yield
            act(S, eu, eu, ACT.Abs, after=[a])
            a = act(S, eu, eu, ACT.Exp, scale=-1.0)
            yield
            tt(V, qq[:, u, :, :], q, eu, ALU.mult, after=[a] + read[u])
            a = tt(V, kk[:, u, :, :], k, eu, ALU.mult)
            ql, kl = qq[:, u, :, :], kk[:, u, :, :]
            yield
        else:
            a = started[0]
            ql, kl = q, k
        pair = 2 * u
        PE.wait([a] + list(started) + c.bank_read[pair] + c.bank_read[pair + 1])
        for r in range(2):
            rows = slice(64 * r, 64 * r + 64)
            for j in range(2):
                if m == P:
                    mm(PE, c.bank(pair + r)[:, P * j:P * j + P], kl[rows, j, 0:P], ql[rows, j, P:T])
                else:
                    for i in range(NT):
                        tile = slice(P * i, P * i + P)
                        col = P * (2 * j + i)
                        mm(PE, c.bank(pair + r)[:, col:col + P], kl[rows, j, tile], ql[rows, j, tile])
        done = PE.last
        read[u] = [done]
        yield
        src = c.bank(pair, 2).rearrange("p (r x) -> p r x", r=2)
        if m == P:
            a = copy(V, across[:, :, :, :].rearrange("p r j t -> p r (j t)"), src[:, :, 0:2 * P], after=[done])
        else:
            mask = c.masks[:, n - 1, :] if m else c.ident[:, :]
            a = overwrite(V, at[:, :, :, :, :].rearrange("p r j i t -> p (r j i) t"), over(mask, 8, 1),
                          c.bank(pair, 2).rearrange("p (x t) -> p x t", t=P), [done, cleared])
        c.bank_read[pair] = c.bank_read[pair + 1] = [a]
        yield

    yield from pipeline([lambda u, n=n, m=m: level(n, m, u) for n, m in enumerate([P] + LEVELS + [0])], 2)
    sq = c.sb("gla_sq", [P, GLA_H, T], ctx)
    tmp = c.sb("gla_tmp", [P, 2, T], ctx)
    finished = V.last
    gated_done = finish_gates()

    def head(h, u):
        j, r = h // 2, h % 2
        PE.wait([finished] + c.bank_read[u])
        vh = v[:, :, P * h:P * h + P]
        mm(PE, c.bank(u)[:, 0:P], vh[:, 0, :], at[:, r, j, 0, :])
        mm(PE, c.bank(u)[:, P:T], vh[:, 0, :], across[:, r, j, :], True, False)
        mm(PE, c.bank(u)[:, P:T], vh[:, 1, :], at[:, r, j, 1, :], False, True)
        yield
        c.bank_read[u] = [act(S, o[:, h, :], c.bank(u)[:, 0:T], ACT.Copy, after=[PE.last])]
        yield from head_norm(c, o, h, u, sq, tmp, out_gain, gr, gated_done)

    yield from pipeline([lambda u, h=h: head(h, u) for h in range(GLA_H)], 2)


def head_norm(c, o, h, u, sq, tmp, gain, gated, gated_done):
    m = act(c.S, sq[:, h, :], o[:, h, :], ACT.Square)
    yield
    mm(c.PE, c.bank(u)[:, 0:T], c.ones[:, :], sq[:, h, :], after=[m] + c.bank_read[u])
    done = c.PE.last
    yield
    m = ts(c.V, tmp[:, u, :], c.bank(u)[:, 0:T], 1.0 / P, ALU.mult, EPS, ALU.add, after=[done])
    c.bank_read[u] = [m]
    tt(c.V, o[:, h, :], o[:, h, :], gated[:, h, :], ALU.mult, after=[m, gated_done])
    yield
    m = act(c.S, tmp[:, u, :], tmp[:, u, :], ACT.Sqrt, after=[m])
    yield
    recip(c.V, tmp[:, u, :], tmp[:, u, :], after=[m])
    stt(c.V, o[:, h, :], o[:, h, :], gain, tmp[:, u, :], ALU.mult, ALU.mult)
    yield


def compress(c, ctx, name, kv, hid, projected, pos_src, w1_srcs):
    V, S, PE = c.V, c.S, c.PE
    pos = c.sb(name + "_pos", [P, CMP_BLOCK], ctx)
    blocks = c.sb(name + "_blocks", [P, CMP_BLOCK, N_CMP], ctx)
    pos_came = [c.load(pos[64 * g:64 * g + 64, :], pos_src) for g in range(NSA_G)]
    width = CMP_STRIDE * N_CMP
    for half in range(CMP_BLOCK // CMP_STRIDE):
        src = kv[:, CMP_STRIDE * half:CMP_STRIDE * half + width].rearrange("p (n r) -> p r n", r=CMP_STRIDE)
        r = slice(CMP_STRIDE * half, CMP_STRIDE * (half + 1))
        m = tt(V, blocks[:, r, :], src, over(pos[:, r], N_CMP, 2), ALU.add, after=pos_came + [projected])
    banks = [c.take_bank() for _ in range(NSA_G)]
    PE.wait([m] + [x for b in banks for x in c.bank_read[b]])
    per_unit = 1024 // CMP_HIDDEN
    for n in range(w1_srcs.shape[0]):
        slot, came = c.raw_unit(w1_srcs[n])
        w1 = c.ring[:, slot, :].rearrange("p (r c) -> p r c", r=per_unit)
        PE.wait([came])
        for g in range(NSA_G):
            rows = slice(64 * g, 64 * g + 64)
            for rr in range(per_unit):
                r = per_unit * n + rr
                mm(PE, c.bank(banks[g])[:, 0:N_CMP], w1[rows, rr, :], blocks[rows, r, :], r == 0, r == CMP_BLOCK - 1)
        c.slot_read[slot] = [PE.last]
        yield
    for g in range(NSA_G):
        c.bank_read[banks[g]] = [act(S, hid[:, g, :], c.bank(banks[g])[:, 0:N_CMP], ACT.Gelu_apprx_tanh,
                                     after=[PE.last])]
    yield


def nsa(c, ctx, q, kv, vt, gates, o, projected):
    V, S, G, PE = c.V, c.S, c.G, c.PE
    table = c.sb("bias_table", [BUCKETS, NSA_H], ctx)
    onehot = c.sb("bias_onehot", [BUCKETS, 2 * T], ctx)
    by_dist = c.sb("bias_by_dist", [NSA_H, 2 * T], ctx)
    came = [c.load(table[:, :], c.dram["rel_bias"]), c.load(onehot[:, :], c.dram["bucket_of_dist"])]
    bk = c.take_bank()
    mm(PE, c.bank(bk)[0:NSA_H, :], table[:, :], onehot[:, :], after=came + c.bank_read[bk])
    c.bank_read[bk] = [copy(V, by_dist[:, :], c.bank(bk)[0:NSA_H, :], after=[PE.last])]
    m = fill(V, by_dist[:, 0:T - 1], NEG_INF)
    scratch = c.dram["bias_scratch"]
    stored = c.load(scratch, by_dist[:, :], after=[m])
    bias = [c.sb("bias_0", [P, NSA_H, P], ctx), c.sb("bias_1", [P, NSA_H, T], ctx)]
    came = [c.load(bias[0][:, :, :], bass.AP(scratch.tensor, T - P, [[1, P], [2 * T, NSA_H], [1, P]]), after=[stored]),
            c.load(bias[1][:, :, :], bass.AP(scratch.tensor, P, [[1, P], [2 * T, NSA_H], [1, T]]), after=[stored])]
    k_cmp = c.sb("k_cmp", [P, N_CMP], ctx)
    v_cmp = c.sb("v_cmp", [N_CMP, P], ctx)
    early = P // CMP_STRIDE - 1
    v_early = c.sb("v_cmp_early", [early, P], ctx)
    hid_k, hid_v = (c.sb(f"cmp_hid_{x}", [P, NSA_G, N_CMP], ctx) for x in "kv")
    with ExitStack() as brief:
        yield from compress(c, brief, "cmp_k", kv["kc"], hid_k, projected, c.dram["pos_k"], c.dram["cmp_k_w1"])
        yield from compress(c, brief, "cmp_v", kv["vc"], hid_v, projected, c.dram["pos_v"], c.dram["cmp_v_w1"])
    w2 = c.sb("cmp_w2", [P, 2, NSA_DH], ctx)
    w2_came = [c.load(w2[:, 0, :], c.dram["cmp_k_w2"]), c.load(w2[:, 1, :], c.dram["cmp_v_w2"])]
    bk = c.take_bank()
    PE.wait([S.last] + w2_came + c.bank_read[bk])
    for g in range(NSA_G):
        mm(PE, c.bank(bk)[64 * g:64 * g + 64, 0:N_CMP], w2[:, 0, :], hid_k[:, g, :])
    c.bank_read[bk] = [copy(V, k_cmp[:, :], c.bank(bk)[:, 0:N_CMP], after=[PE.last])]
    bk = c.take_bank()
    PE.wait(c.bank_read[bk])
    for g in range(NSA_G):
        mm(PE, c.bank(bk)[0:N_CMP, 64 * g:64 * g + 64], hid_v[:, g, :], w2[:, 1, :])
        mm(PE, c.bank(bk)[0:early, P + 64 * g:P + 64 * g + 64], hid_v[:, g, N_CMP - early:N_CMP], w2[:, 1, :])
    copy(V, v_cmp[:, :], c.bank(bk)[0:N_CMP, 0:P], after=[PE.last])
    c.bank_read[bk] = [copy(V, v_early[:, :], c.bank(bk)[0:early, P:2 * P])]
    compressed = V.last
    yield

    WIDTH = 2
    sig = c.sb("gate_sigmoid", [P, NT, 3 * NSA_H], ctx)
    cmp_coef = c.sb("nsa_cmp_coef", [P, NT, NSA_H], ctx)
    s = c.sb("nsa_s", [P, WIDTH, HPG, T], ctx)
    mx = c.sb("nsa_max", [P, WIDTH, NSA_H], ctx)
    z = c.sb("nsa_z", [P, WIDTH, NSA_H], ctx)
    pt_cmp = c.sb("nsa_pt_cmp", [N_CMP, NT, NSA_H, P], ctx)
    pts = [c.sb(f"nsa_pt_{i}", [P, 2, NSA_H, i + 1, P], ctx) for i in range(NT)]
    m = act(S, sig[:, :, :], gates[:, :, :], ACT.Sigmoid)
    by_branch = sig[:, :, :].rearrange("p i (h b) -> p i b h", b=3)
    ts(V, cmp_coef[:, 0, :], by_branch[:, 0, 0, :], c.some_block[:, :], ALU.mult, after=[m])
    copy(V, cmp_coef[:, 1, :], by_branch[:, 1, 0, :])
    yield

    def soft(area, u, heads, n, coef):
        mxu, zu = mx[:, u, 0:heads], z[:, u, 0:heads]
        reduce(V, mxu, area, ALU.max)
        m = tt(V, area, area, over(mxu, n, 2), ALU.subtract)
        yield
        m = act(S, area, area, ACT.Exp, after=[m])
        yield
        reduce(V, zu, area, ALU.add, after=[m])
        recip(V, zu, zu)
        m = tt(V, zu, zu, coef, ALU.mult)
        yield
        tt(G, area, area, over(zu, n, 2), ALU.mult, after=[m])
        yield

    def cmp_chain(i, u):
        q_i, n_blocks, b0 = slice(P * i, P * i + P), N_CMP if i else early, 2 * u
        PE.wait([compressed] + c.bank_read[b0] + c.bank_read[b0 + 1])
        for g in range(NSA_G):
            rows = slice(64 * g, 64 * g + 64)
            for h in range(HPG):
                mm(PE, c.bank(b0 + g)[:, n_blocks * h:n_blocks * (h + 1)], q[rows, h, q_i],
                   k_cmp[rows, N_CMP - n_blocks:N_CMP])
        done = PE.last
        yield
        area = s[:, u, :, :].rearrange("p h n -> p (h n)")[:, 0:NSA_H * n_blocks].rearrange("p (h n) -> p h n", h=NSA_H)
        for g in range(NSA_G):
            hs = slice(HPG * g, HPG * (g + 1))
            steps = bias[i][:, hs, :].rearrange("p h (n r) -> p h n r", r=CMP_STRIDE)[:, :, 0:n_blocks, 0]
            m = tt(V, area[:, hs, :], c.bank(b0 + g)[:, 0:HPG * n_blocks].rearrange("p (h n) -> p h n", h=HPG), steps,
                   ALU.add, after=[done] + came)
            c.bank_read[b0 + g] = [m]
        yield from soft(area, u, NSA_H, n_blocks, cmp_coef[:, i, :])
        PE.wait([G.last] + c.bank_read[b0] + c.bank_read[b0 + 1])
        for h in range(NSA_H):
            tr(PE, c.bank(b0 + h // 4)[0:n_blocks, P * (h % 4):P * (h % 4) + P], area[:, h, :], c.ident[:, :])
        done = PE.last
        yield
        for w in range(2):
            c.bank_read[b0 + w] = [act(S, pt_cmp[0:n_blocks, i, 4 * w:4 * w + 4, :],
                                       c.bank(b0 + w)[0:n_blocks, :].rearrange("p (h t) -> p h t", h=4), ACT.Copy,
                                       after=[done])]
        yield

    def full_chain(w, i, g, u):
        q_i, n_keys, b0 = slice(P * i, P * i + P), P * (i + 1), 2 * u
        name, rows, hs = ("ks", "kw")[w], slice(64 * g, 64 * g + 64), slice(HPG * g, HPG * (g + 1))
        PE.wait([projected] + c.bank_read[b0] + c.bank_read[b0 + 1])
        for h in range(HPG):
            mm(PE, c.bank(b0, 2)[:, n_keys * h:n_keys * (h + 1)], q[rows, h, q_i], kv[name][rows, T - n_keys:T])
        done = PE.last
        yield
        area = s[:, u, :, 0:n_keys]
        m = tt(V, area, c.bank(b0, 2)[:, 0:HPG * n_keys].rearrange("p (h n) -> p h n", h=HPG), bias[i][:, hs, :],
               ALU.add, after=[done] + came)
        c.bank_read[b0] = c.bank_read[b0 + 1] = [m]
        yield from soft(area, u, HPG, n_keys, by_branch[:, i, 1 + w, hs])
        PE.wait([G.last])
        for jj in range(i + 1):
            PE.wait(c.bank_read[b0 + jj])
            for h in range(HPG):
                tr(PE, c.bank(b0 + jj)[:, P * h:P * h + P], area[:, h, P * jj:P * jj + P], c.ident[:, :])
        done = PE.last
        yield
        for jj in range(i + 1):
            c.bank_read[b0 + jj] = [act(S, pts[i][:, w, hs, jj, :], c.bank(b0 + jj).rearrange("p (h t) -> p h t", h=4),
                                        ACT.Copy, after=[done])]
        yield

    def counted(i, chain):
        yield from chain
        ended[i] += 1

    def outputs(i, u):
        assert ended[i] == len(chains[i])
        n_blocks, vc_i = (N_CMP, v_cmp) if i else (early, v_early)
        bk = 2 * u
        PE.wait([S.last] + c.bank_read[bk])
        for h in range(HPG):
            for g in range(NSA_G):
                out = c.bank(bk)[64 * g:64 * g + 64, P * h:P * h + P]
                cols = slice(64 * g, 64 * g + 64)
                mm(PE, out, vc_i[0:n_blocks, cols], pt_cmp[0:n_blocks, i, HPG * g + h, :], True, False)
                for w in range(2):
                    for jj in range(i + 1):
                        mm(PE, out, vt[:, NT - 1 - i + jj, P * w + 64 * g:P * w + 64 * g + 64],
                           pts[i][:, w, HPG * g + h, jj, :], False, w == 1 and jj == i)
            yield
        c.bank_read[bk] = [copy(V, o[:, :, P * i:P * i + P], c.bank(bk).rearrange("p (h t) -> p h t", h=HPG),
                                after=[PE.last])]
        yield

    ended, chains = [0] * NT, []
    for i in range(NT):
        chains.append([lambda u, i=i: counted(i, cmp_chain(i, u))])
        for w in range(2):
            for g in range(NSA_G):
                chains[i].append(lambda u, i=i, w=w, g=g: counted(i, full_chain(w, i, g, u)))
    first, second = chains
    yield from pipeline(first + second[:2] + [lambda u: outputs(0, u)] + second[2:], WIDTH)
    yield from outputs(1, 0)


def first_mixer(c, h, xn, work, tmp, mem_kv):
    V, S, G, PE = c.V, c.S, c.G, c.PE
    with ExitStack() as ctx:
        for k in range(KD):
            c.norm_add(h, work, k, [c.h_came])
        c.flush(c.dram["w_in"][0], c.dram["w_in"][1])
        c.norm_finish(h, c.gain("norm_mix"), work, work, tmp, xn, after=[c.gains_came])
        gq = c.sb("gla_q", [P, 2, T], ctx)
        gk = c.sb("gla_k", [P, 2, T], ctx)
        gate = c.sb("gla_gate", [P, 2, T], ctx)
        gv = c.sb("gla_v", [P, NT, 512], ctx)
        gr = c.sb("gla_r", [P, 4, T], ctx)
        o = c.sb("mix_o", [P, 8, T], ctx)
        nq = c.sb("nsa_q", [P, HPG, T], ctx)
        kv = {n: c.sb("nsa_" + n, [P, T], ctx) for n in ("kc", "vc", "ks", "kw")}
        vt = c.sb("nsa_vt", [P, NT, 2 * P], ctx)
        gates = c.sb("nsa_gates", [P, NT, 24], ctx)
        xr = Parts(*(c.sb(f"xn_reversed_{x}", [P, KD, T], ctx, F32R) for x in range(2)))

        def keep(dst, scale=1.0, func=ACT.Copy):
            return lambda out, done: act(S, dst, out, func, scale=scale, after=[done])

        w = c.dram["w_in"]
        with ExitStack() as inner:
            small_w = c.sb("small_w", [P, KD, 40], inner)
            glr = c.sb("gla_lr", [GLA_RANK, T], inner)
            w2 = c.sb("gate_w2", [GLA_RANK, T], inner)
            za = c.sb("gate_z", [P, 2, T], inner)
            for j in range(2):
                c.channels(w[j], xn, keep(gq[:, j, :], GLA_DK ** -0.5))
            small_came = c.load(small_w[:, :, :], c.dram["w_in_small"])
            w2_came = c.load(w2[:, :], c.dram["gla_gate_w2"])
            for j in range(2):
                c.channels(w[2 + j], xn, keep(gk[:, j, :]))
            for k in range(KD):
                copy(G, xr.high[:, k, :], xn.high[:, k, ::-1], after=[xn.marks[k]])
                xr.marks[k] = copy(G, xr.low[:, k, :], xn.low[:, k, ::-1])
            whole = work
            bk = c.take_bank()
            PE.wait([small_came, V.last] + c.bank_read[bk])
            for k in range(KD):
                mm(PE, c.bank(bk)[0:GLA_RANK, 0:T], small_w[:, k, 0:GLA_RANK], whole[:, k, :], k == 0, k == KD - 1)
            a = act(S, glr[:, :], c.bank(bk)[0:GLA_RANK, 0:T], ACT.Copy, after=[PE.last])
            c.bank_read[bk] = [a]
            bk = c.take_bank()
            PE.wait(c.bank_read[bk])
            for i in range(NT):
                for k in range(KD):
                    mm(PE, c.bank(bk)[:, 24 * i:24 * i + 24], whole[:, k, P * i:P * i + P], small_w[:, k, 16:40],
                       k == 0, k == KD - 1)
            c.bank_read[bk] = [act(S, gates[:, :, :], c.bank(bk)[:, 0:48].rearrange("p (i c) -> p i c", i=NT),
                                   ACT.Copy, after=[PE.last])]
            for j in range(2):
                bk = c.take_bank()
                mm(PE, c.bank(bk)[:, 0:T], w2[:, P * j:P * j + P], glr[:, :], after=[a, w2_came] + c.bank_read[bk])
                bcol = c.gain("gla_gate_b")[:, j:j + 1]
                c.bank_read[bk] = [ts(V, gate[:, j, :], c.bank(bk)[:, 0:T], bcol, ALU.add, after=[PE.last])]
            gv_units = c.tokens(c.dram["w_in_gv"], xn, 512, lambda i, out, done: act(S, gv[:, i, :], out, ACT.Copy,
                                                                                    after=[done]))
            for _ in gv_units:
                pass
            act(S, za[:, :, :], gate[:, :, :], ACT.Abs, after=[V.last])
            act(S, za[:, :, :], za[:, :, :], ACT.Exp, scale=-1.0)
            m = act(S, za[:, :, :], za[:, :, :], ACT.Ln, bias=1.0)
            ts(V, gate[:, :, :], gate[:, :, :], 0.0, ALU.min, after=[m])
            tt(V, gate[:, :, :], gate[:, :, :], za[:, :, :], ALU.subtract)
            m = ts(V, gate[:, :, :], gate[:, :, :], 1.0 / GLA_TAU, ALU.mult)
            c.flush(w[4], w[5])
            small_done = [V.last, S.last, PE.last]

        k_mem, v_mem = mem_kv
        mem = v_mem

        def projections():
            for j in range(4):
                c.channels(w[4 + j], xn, keep(gr[:, j, :], func=ACT.Silu))
                yield
            for j in range(4):
                c.channels(w[8 + j], xn, keep(nq[:, j, :], NSA_DH ** -0.5))
                yield
            for n, name in ((12, "kc"), (13, "vc"), (14, "ks"), (15, "kw")):
                c.channels(w[n], xr, keep(kv[name][:, :]))
                yield
            yield from c.tokens(c.dram["w_in_v"], xr, 2 * P, lambda i, out, done: act(S, vt[:, i, :], out, ACT.Copy,
                                                                                     after=[done]))

        def memory():
            read = [PE.last]
            whole_mem = mem[:, :, :].rearrange("p i (k t) -> p (i k) t", k=KD // NT)
            mem_came = c.load(whole_mem, c.dram["memT"], after=small_done)
            for k in range(KD):
                c.norm_add(whole_mem, work, k, [mem_came] + small_done)
                yield
            memn = Parts(xr.high, xr.low)
            c.norm_finish(whole_mem, c.gain("norm_mem"), work, work, tmp, memn, after=read)
            normed = [V.last]
            yield
            for n in range(KD):
                c.channels(c.dram["xa_wk"][n], memn, keep(k_mem[:, n, :]))
                yield
            for half in range(2):
                cols = slice(512 * half, 512 * half + 512)
                yield from c.tokens(c.dram["xa_wv"][half], memn, 512,
                                    lambda i, out, done, cols=cols: act(S, v_mem[:, i, cols], out, ACT.Copy,
                                                                        after=[done] + normed))

        c.rotation = [4, 5, 6]
        filler = projections()
        with ExitStack() as inner:
            def finish_gates():
                for _ in filler:
                    pass
                c.flush(c.dram["xa_wk"][0], c.dram["xa_wk"][1])
                return S.last

            together(gla(c, inner, gq[:, :, :], gk[:, :, :], gate, gv, gr, c.gain("gla_out_norm"), o[:, 0:4, :],
                         [m, S.last], finish_gates), filler, 3)
            for _ in filler:
                pass
            c.barrier()
        with ExitStack() as inner:
            gla_done = [V.last, PE.last]
            for k in range(4):
                c.split_chunk(o[:, k, :], xn, k, gla_done)
            filler = memory()
            together(nsa(c, inner, nq, kv, vt, gates, o[:, 4:8, :], S.last), filler, 3)
            for _ in filler:
                pass
            c.flush(c.dram["w_out"][0], c.dram["w_out"][1])
            made = [V.last, PE.last]
            for k in range(4, KD):
                c.split_chunk(o[:, k, :], xn, k, made)
            for n in range(KD):
                c.channels(c.dram["w_out"][n], xn, lambda out, done, n=n: c.add_to_h(h, work, n, out, done))
            c.flush(c.dram["xa_wq"][0], c.dram["xa_wq"][1])
            c.barrier()
            c.rotation = list(range(7))


def cross_attention(c, h, xn, work, tmp, mem_kv, following):
    V, S, G, PE = c.V, c.S, c.G, c.PE
    k, v = mem_kv
    with ExitStack() as ctx:
        q = c.sb("xa_q", [P, KD, T], ctx)

        WIDTH = 3
        s = c.sb("xa_s", [P, WIDTH, 2, T], ctx)
        mx = c.sb("xa_max", [P, WIDTH, 2], ctx)
        z = c.sb("xa_z", [P, WIDTH, 2], ctx)
        pt = c.sb("xa_pt", [P, XA_H, NT, T], ctx)
        c.norm_finish(h, c.gain("norm_xattn"), work, work, tmp, xn)
        for n in range(KD):
            c.channels(c.dram["xa_wq"][n], xn,
                       lambda out, done, n=n: act(S, q[:, n, :], out, ACT.Copy, scale=XA_DH ** -0.5, after=[done]))
        c.flush(c.dram["xa_wo"][0], c.dram["xa_wo"][1])
        queries = S.last

        def chain(i, two, u):
            tile, b = slice(P * i, P * i + P), 2 * u
            PE.wait([queries] + c.bank_read[b])
            for x in range(2):
                for j in range(2):
                    mm(PE, c.bank(b)[:, T * x:T * x + T], q[:, 2 * (2 * two + x) + j, tile],
                       k[:, 2 * (2 * two + x) + j, :], j == 0, j == 1)
            done = PE.last
            yield
            area, src = s[:, u, :, :], c.bank(b).rearrange("p (h m) -> p h m", h=2)
            reduce(V, mx[:, u, :], src, ALU.max, after=[done])
            m = tt(V, area, src, over(mx[:, u, :], T, 2), ALU.subtract)
            c.bank_read[b] = [m]
            yield
            m = act(S, area, area, ACT.Exp, after=[m])
            yield
            reduce(V, z[:, u, :], area, ALU.add, after=[m])
            m = recip(V, z[:, u, :], z[:, u, :])
            yield
            m = tt(G, area, area, over(z[:, u, :], T, 2), ALU.mult, after=[m])
            yield
            PE.wait([m] + c.bank_read[b])
            for j in range(NT):
                for x in range(2):
                    tr(PE, c.bank(b)[:, P * (2 * j + x):P * (2 * j + x) + P], area[:, x, P * j:P * j + P], c.ident[:, :])
            done = PE.last
            yield
            m = act(S, pt[:, 2 * two:2 * two + 2, :, tile],
                    c.bank(b).rearrange("p (j h t) -> p h j t", j=NT, h=2), ACT.Copy, after=[done])
            c.bank_read[b] = [m]
            yield

        for _ in pipeline([lambda u, i=i, two=two: chain(i, two, u) for two in range(2) for i in range(NT)], WIDTH):
            pass
        for n in range(KD):
            bk = c.take_bank()
            PE.wait([S.last] + c.bank_read[bk])
            for j in range(NT):
                mm(PE, c.bank(bk)[:, 0:T], v[:, j, P * n:P * n + P], pt[:, n // 2, j, :], j == 0, j == NT - 1)
            c.split_chunk(c.bank(bk)[:, 0:T], xn, n, [PE.last])
            c.bank_read[bk] = [xn.marks[n]]
        for n in range(KD):
            c.channels(c.dram["xa_wo"][n], xn, lambda out, done, n=n: c.add_to_h(h, work, n, out, done))
        c.flush(*following)
        c.barrier()


def top16(c, vals, idx, src, spare):
    V = c.V
    V.do(lambda e: e.max(out=vals[:, 0:8], in_=src))
    V.do(lambda e: e.max_index(out=idx[:, 0:8], in_max=vals[:, 0:8], in_values=src))
    V.do(lambda e: e.match_replace(out=spare, in_to_replace=vals[:, 0:8], in_values=src, imm_value=-3e38))
    V.do(lambda e: e.max(out=vals[:, 8:16], in_=spare))
    return V.do(lambda e: e.max_index(out=idx[:, 8:16], in_max=vals[:, 8:16], in_values=spare))


def routing(c, q, sk, area, half_dim, pairs, queries_done):
    V, S, PE = c.V, c.S, c.PE
    at = [0]

    def cut(*shape):
        n = int(np.prod(shape))
        at[0] += n
        names = "abcd"[:len(shape)]
        view = area[:, at[0] - n:at[0]]
        return view.rearrange(f"p ({' '.join(names)}) -> p {' '.join(names)}", **dict(zip(names, shape)))

    scores = cut(PEER_H, 2, NKEYS)
    cand = cut(PEER_H, TOPK, TOPK)
    eq = cut(PEER_H, TOPK, TOPK)
    spare = cut(2 * NKEYS)
    vals = cut(PEER_H, 2, TOPK)
    idx = cut(PEER_H, 2, TOPK).bitcast(U32)
    idxf = cut(PEER_H, 2, TOPK)
    top = cut(PEER_H, TOPK)
    pos = cut(PEER_H, TOPK).bitcast(U32)
    part = cut(PEER_H, TOPK).bitcast(U32)
    partf = cut(PEER_H, TOPK)
    res = cut(3, PEER_H, TOPK)
    zs = cut(PEER_H)
    iota16 = over(over(c.iota[:, 0:TOPK], TOPK, 1), PEER_H, 1)
    for i in range(NT):
        tile = slice(P * i, P * i + P)
        PE.wait(queries_done + [x for b in range(4) for x in c.bank_read[b]])
        if half_dim == 64:
            for hd in range(PEER_H):
                for a in range(2):
                    mm(PE, c.bank(2 * a, 2)[:, P * hd:P * hd + P], q[64 * a:64 * a + 64, hd, tile],
                       sk[64 * a:64 * a + 64, hd, :])
            for a in range(2):
                m = act(S, scores[:, :, a, :], c.bank(2 * a, 2).rearrange("p (h n) -> p h n", h=PEER_H), ACT.Copy,
                        after=[PE.last, V.last])
        else:
            for n in range(2 * PEER_H):
                mm(PE, c.bank(0, 4)[:, P * n:P * n + P], q[:, n, tile], sk[:, n, :])
            m = act(S, scores, c.bank(0, 4).rearrange("p (h a n) -> p h a n", h=PEER_H, a=2), ACT.Copy,
                    after=[PE.last, V.last])
        for b in range(4):
            c.bank_read[b] = [m]
        V.wait([m])
        for hd in range(PEER_H):
            for a in range(2):
                top16(c, vals[:, hd, a, :], idx[:, hd, a, :], scores[:, hd, a, :], spare[:, 0:NKEYS])
                yield
        copy(V, idxf, idx)
        tt(V, cand, over(vals[:, :, 0, :], TOPK, 3), over(vals[:, :, 1, :], TOPK, 2), ALU.add)
        yield
        for hd in range(PEER_H):
            top16(c, top[:, hd, :], pos[:, hd, :], cand[:, hd, :, :].rearrange("p a b -> p (a b)"), spare)
            yield
        for a in range(2):
            if a == 0:
                ts(V, part, pos, 4, ALU.logical_shift_right)
            else:
                ts(V, part, pos, 15, ALU.bitwise_and)
            copy(V, partf, part)
            tt(V, eq, over(partf, TOPK, 3), iota16, ALU.is_equal)
            yield
            tt(V, eq, eq, over(idxf[:, :, a, :], TOPK, 2), ALU.mult)
            reduce(V, res[:, a, :, :], eq, ALU.add)
            yield
        m = tt(V, res[:, 2, :, :], top, over(top[:, :, 0], TOPK, 2), ALU.subtract)
        m = act(S, res[:, 2, :, :], res[:, 2, :, :], ACT.Exp, after=[m])
        reduce(V, zs, res[:, 2, :, :], ALU.add, after=[m])
        recip(V, zs, zs)
        m = tt(V, res[:, 2, :, :], res[:, 2, :, :], over(zs, TOPK, 2), ALU.mult)
        yield
        PE.wait([m] + c.bank_read[0])
        for x in range(3):
            tr(PE, c.bank(0)[:, P * x:P * x + P], res[:, x, :, :].rearrange("p h k -> p (h k)"), c.ident[:, :])
        c.bank_read[0] = [copy(V, pairs[:, :, tile], c.bank(0)[:, 0:3 * P].rearrange("p (x t) -> p x t", x=3),
                               after=[PE.last])]
        yield


def peer(c, h, xn, work, tmp, name, gain, half_dim, wq, subkeys, down, up, following=()):
    V, S, G, PE = c.V, c.S, c.G, c.PE
    n_q = 2 * PEER_H * half_dim // P
    with ExitStack() as ctx:
        experts = c.sb(name + "_experts", [P, NKEYS, T], ctx)
        pairs = c.sb(name + "_pairs", [P, 3, T], ctx)
        first_kept = 72
        area = experts[:, first_kept:NKEYS, :].rearrange("p a t -> p (a t)")
        sk = area[:, 0:n_q * P].rearrange("p (k n) -> p k n", k=n_q)
        q = area[:, n_q * P:n_q * (P + T)].rearrange("p (k t) -> p k t", k=n_q)
        c.norm_finish(h, gain, work, work, tmp, xn)
        sk_came = c.load(sk, subkeys)
        for n in range(n_q):
            c.channels(wq[n], xn, lambda out, done, n=n: act(S, q[:, n, :], out, ACT.Copy, after=[done]))
        c.flush(down[0], down[1])
        route = routing(c, q, sk, area[:, n_q * (P + T):], half_dim, pairs, [S.last, sk_came])
        routed = [False]

        def go_on(n):
            for _ in range(n):
                if not routed[0]:
                    routed[0] = next(route, "end") == "end"

        c.rotation = [4, 5, 6]
        c.low_by = G
        for n in range(NKEYS):
            if n == first_kept:
                while not routed[0]:
                    go_on(1)
                done_routing = [V.last, PE.last]
                c.low_by = V

            def gelu(out, done, n=n):
                go_on(1)
                return act(S, experts[:, n, :], out, ACT.Gelu_apprx_tanh,
                           after=[done] + (done_routing if n >= first_kept else []))

            if n == first_kept:
                c.flush()
            c.channels(down[n], xn, gelu)
        c.flush(up[0], up[1])
        hidden_done = S.last

        GROUP = 4
        onehots = work[:, :, :].rearrange("p k (i n) -> p i k n", i=2)
        with ExitStack() as inner:
            gates = c.sb(name + "_gates", [P, 2, P * GROUP], inner)
            used, gated = [[], []], [[], []]
            iota = c.bank(7)[:, 0:P]
            copy(V, iota, c.iota[:, :], after=c.bank_read[7])
            for g in range(T // GROUP):
                u, b = g % 2, g % 7
                i1, i2, gate = (pairs[:, x, GROUP * g:GROUP * (g + 1)] for x in range(3))
                tt(V, onehots[:, 1, GROUP * u:GROUP * (u + 1), :], over(iota, GROUP, 1), over(i2, P, 2), ALU.is_equal,
                   after=used[u])
                for t in range(GROUP):
                    onehot(V, onehots[:, 0, GROUP * u + t, :], c.iota[:, :], i1[:, t:t + 1], gate[:, t:t + 1])
                PE.wait([V.last] + c.bank_read[b])
                for t in range(GROUP):
                    mm(PE, c.bank(b)[:, P * t:P * t + P], onehots[:, 0, GROUP * u + t, :], onehots[:, 1, GROUP * u + t, :])
                used[u] = [PE.last]
                m = c.bank_read[b] = [act(S, gates[:, u, :], c.bank(b), ACT.Copy, after=[PE.last] + gated[u])]
                dst = experts[:, :, GROUP * g:GROUP * (g + 1)]
                gated[u] = [tt(G, dst, dst, gates[:, u, :].rearrange("p (t i) -> p i t", t=GROUP), ALU.mult,
                               after=m + [hidden_done])]

        NB = 2
        coef = c.sb(name + "_coef", [P, NB, 2, T], ctx, F32R)
        coef_read = [[] for _ in range(NB)]
        c.PE.wait([x for b in range(4) for x in c.bank_read[b]])
        made = [None] * NKEYS
        gated = G.last

        def make_coef(n):
            u = n % NB
            made[n] = c.split(experts[:, n, :], coef[:, u, 0, :], coef[:, u, 1, :], coef_read[u] + [gated])

        for n in range(NKEYS):
            def run(part, came, n=n):
                if n == NKEYS - 2:
                    make_coef(n + 1)
                u = n % NB
                PE.wait([came, made[n]])
                for i in range(NT):
                    tile = slice(P * i, P * i + P)
                    for half in range(2):
                        cols = slice(512 * half, 512 * half + 512)
                        c.product(c.bank(2 * i + half), (coef[:, u, 0, tile], coef[:, u, 1, tile]),
                                  (c.parts[:, part, 0, cols], c.parts[:, part, 1, cols]), n == 0, n == NKEYS - 1)
                c.parts_read[part] = coef_read[u] = [PE.last]
            if n == 0:
                make_coef(0)
            elif n >= c.AHEAD:
                make_coef(n - c.AHEAD + 1)
            c.submit(up[n], run)
        c.flush(*following)
        squares = experts[:, 0:KD, :]
        y = [work[:, 4 * i:4 * i + 4, :].rearrange("p k t -> p (k t)") for i in range(NT)]
        done = PE.last
        for i in range(NT):
            for b in (2 * i, 2 * i + 1):
                m = copy(V, y[i][:, 512 * (b % 2):512 * (b % 2) + 512], c.bank(b), after=[done])
                c.bank_read[b] = [m]
        for k in range(KD):
            b = c.take_bank()
            PE.wait([m] + c.bank_read[b])
            for i in range(NT):
                tr(PE, c.bank(b)[:, P * i:P * i + P], y[i][:, P * k:P * k + P], c.ident[:, :])
            c.bank_read[b] = [c.add_to_h(h, squares, k, c.bank(b)[:, 0:T], PE.last)]
        c.norm_sum(squares, KD - 1)
        c.barrier()
        c.rotation = list(range(7))





def hgrn(c, ctx, q, zf, zb, v, o):
    V, S, G, PE = c.V, c.S, c.G, c.PE
    lb = c.sb("hg_lb", [P, KD], ctx)
    one_minus = c.sb("hg_one_minus", [P, KD], ctx)
    t2 = c.sb("hg_t2", [P, 2, KD], ctx)
    lbl = c.gain("lb").rearrange("p (l k) -> p l k", l=2)
    tt(V, lb[:, :], lbl[:, 0, :], lbl[:, 1, :], ALU.max)
    m = tt(V, t2[:, :, :], lbl, over(lb[:, :], 2, 1), ALU.subtract)
    m = act(S, t2[:, :, :], t2[:, :, :], ACT.Exp, after=[m])
    tt(V, one_minus[:, :], t2[:, 0, :], t2[:, 1, :], ALU.add, after=[m])
    recip(V, one_minus[:, :], one_minus[:, :])
    tt(V, lb[:, :], t2[:, 0, :], one_minus[:, :], ALU.mult)
    ts(V, one_minus[:, :], lb[:, :], -1.0, ALU.mult, 1.0, ALU.add)
    kf = c.sb("hg_kf", [P, HG_H, T], ctx)
    kb = c.sb("hg_kb", [P, HG_H, T], ctx)
    for z, k in ((zf, kf), (zb, kb)):
        act(S, k[:, :, :], z[:, :, :], ACT.Sigmoid, scale=-1.0)
        m = act(S, z[:, :, :], z[:, :, :], ACT.Sigmoid)
        for hd in range(HG_H):
            ts(V, k[:, hd, :], k[:, hd, :], one_minus[:, hd:hd + 1], ALU.mult, after=[m])
            ts(V, z[:, hd, :], z[:, hd, :], one_minus[:, hd:hd + 1], ALU.mult, lb[:, hd:hd + 1], ALU.add)
        m = ts(V, z[:, :, :], z[:, :, :], 2.0 ** -62, ALU.max)
        yield
        act(S, z[:, :, :], z[:, :, :], ACT.Ln, after=[m])
        yield
    bf = c.sb("hg_bf", [P, HG_H, T], ctx)
    bb = c.sb("hg_bb", [P, HG_H, T], ctx)
    logs = S.last
    for hd in range(HG_H):
        scan(V, bf[:, hd, :], c.reset[:, :], zf[:, hd, :], [logs])
        scan(V, bb[:, hd, ::-1], c.reset[:, :], zb[:, hd, ::-1])
        if hd % 2:
            yield
    places = [(zf, zb), (c.sb("hg_q2", [P, HG_H, T], ctx), c.sb("hg_k2", [P, HG_H, T], ctx))]
    at = c.sb("hg_scores", [P, HG_H, NT, P], ctx)
    fwd = c.sb("hg_scores_fwd", [P, HG_H, P], ctx)
    bwd = c.sb("hg_scores_bwd", [P, HG_H, P], ctx)
    cleared = fill(G, at[:, :, :, :], 0.0)
    scanned = V.last
    read = [[], []]

    def level(n, m, u):
        ql, kl = places[u]
        if m:
            F, B, EQ, EK = (halves(x[:, :, :], m) for x in (bf, bb, ql, kl))
            rf, rb = over(F[:, :, 0, m - 1], m, 2), over(B[:, :, 1, 0], m, 2)
            if m == P:
                copy(V, EQ[:, :, 1, :], F[:, :, 1, :], read[u])
                a1 = copy(V, EQ[:, :, 0, :], B[:, :, 0, :])
            else:
                tt(V, EQ[:, :, 1, :], F[:, :, 1, :], rf, ALU.subtract, read[u])
                a1 = tt(V, EQ[:, :, 0, :], B[:, :, 0, :], rb, ALU.subtract)
            tt(G, EK[:, :, 0, :], rf, F[:, :, 0, :], ALU.subtract, [scanned] + read[u])
            a2 = tt(G, EK[:, :, 1, :], rb, B[:, :, 1, :], ALU.subtract)
            yield
            e1 = act(S, ql[:, :, :], ql[:, :, :], ACT.Exp, after=[a1])
            e2 = act(S, kl[:, :, :], kl[:, :, :], ACT.Exp, after=[a2])
            yield
            KF, KB, KK = halves(kf[:, :, :], m), halves(kb[:, :, :], m), halves(kl[:, :, :], m)
            tt(G, KK[:, :, 0, :], KF[:, :, 0, :], EK[:, :, 0, :], ALU.mult, after=[e2])
            a = tt(G, KK[:, :, 1, :], KB[:, :, 1, :], EK[:, :, 1, :], ALU.mult)
            b = tt(V, ql[:, :, :], q[:, :, :], ql[:, :, :], ALU.mult, after=[e1])
            yield
        else:
            a = b = tt(G, kl[:, :, :], kf[:, :, :], kb[:, :, :], ALU.add, [scanned] + read[u])
            ql = q
            yield
        for part in range(2):
            heads = slice(4 * part, 4 * part + 4)
            b0 = 2 * u
            PE.wait([a, b] + c.bank_read[b0] + c.bank_read[b0 + 1])
            area = c.bank(b0, 2).rearrange("p (h i t) -> p h i t", h=4, i=NT)
            for hh in range(4):
                for i in range(NT):
                    s_tile = slice(P * i, P * i + P)
                    t_tile = slice(P * (1 - i), P * (1 - i) + P) if m == P else s_tile
                    mm(PE, area[:, hh, i, :], kl[:, 4 * part + hh, s_tile], ql[:, 4 * part + hh, t_tile])
            done = PE.last
            yield
            if m == P:
                copy(V, fwd[:, heads, :], area[:, :, 0, :], after=[done])
                x = copy(V, bwd[:, heads, :], area[:, :, 1, :])
            else:
                mask = c.masks[:, len(LEVELS) + n - 1, :] if m else c.ident[:, :]
                x = overwrite(V, at[:, heads, :, :].rearrange("p h i t -> p (h i) t"), over(mask, 4 * NT, 1),
                              c.bank(b0, 2).rearrange("p (x t) -> p x t", t=P), [done, cleared])
            c.bank_read[b0] = c.bank_read[b0 + 1] = [x]
        read[u] = [done]
        yield

    yield from pipeline([lambda u, n=n, m=m: level(n, m, u) for n, m in enumerate([P] + LEVELS + [0])], 2)
    for hd in range(HG_H):
        bk = hd % 4
        PE.wait([V.last] + c.bank_read[bk])
        v0, v1 = v[:, 0, P * hd:P * hd + P], v[:, 1, P * hd:P * hd + P]
        out = c.bank(bk)
        mm(PE, out[:, 0:P], v0, at[:, hd, 0, :], True, False)
        mm(PE, out[:, 0:P], v1, bwd[:, hd, :], False, True)
        mm(PE, out[:, P:T], v0, fwd[:, hd, :], True, False)
        mm(PE, out[:, P:T], v1, at[:, hd, 1, :], False, True)
        c.bank_read[bk] = [act(S, o[:, hd, :], out[:, 0:T], ACT.Copy, after=[PE.last])]
        yield


def filters(c, ctx, both):
    V, S, PE = c.V, c.S, c.PE
    z = c.sb("filt_z", [EMB, T], ctx)
    w1 = c.sb("filt_w1", [EMB, FILT_H], ctx)
    w2 = c.sb("filt_w2", [FILT_H, FILT_H], ctx)
    w3 = c.sb("filt_w3", [FILT_H, 2 * D], ctx)
    vec = c.sb("filt_vec", [FILT_H, 4], ctx)
    decay = c.sb("filt_decay", [P, 2 * D], ctx)
    window = c.sb("filt_window", [P, 2 * D], ctx)
    cols = c.sb("filt_cols", [P, 2 * NT], ctx)
    hid = c.sb("filt_hid", [FILT_H, T], ctx)
    turns = c.sb("filt_turns", [FILT_H, T], ctx)
    came = [c.load(z[:, :], c.dram["filter_z"]), c.load(w1[:, :], c.dram["filt_w1_2"]),
            c.load(w2[:, :], c.dram["filt_w2_2"]), c.load(w3[:, :], c.dram["filt_w3_2"]),
            c.load(vec[:, :], c.dram["filt_vec"]), c.load(decay[:, :], c.dram["filt_decay_2"].partition_broadcast(P)),
            c.load(cols[:, 0:NT], c.dram["minus_t"]), c.load(cols[:, NT:2 * NT], c.dram["not_first"])]
    ROUND = 1.5 * 2.0 ** 23
    TWO_PI = [6.28125, 0.0019350051879882812, 3.019916e-07]
    act(S, decay[:, :], decay[:, :], ACT.Abs, after=came)
    last = None
    for n, (w, x) in enumerate(((w1, z), (w2, hid))):
        bk = 3
        mm(PE, c.bank(bk)[0:FILT_H, 0:T], w[:, :], x[:, :], after=came + c.bank_read[bk] + ([last] if last else []))
        m = ts(V, hid[:, :], c.bank(bk)[0:FILT_H, 0:T], vec[:, 2 * n:2 * n + 1], ALU.add,
               vec[:, 2 * n + 1:2 * n + 2], ALU.mult, after=[PE.last] + came)
        c.bank_read[bk] = [m]
        ts(V, turns[:, :], hid[:, :], 1.0 / (2.0 * np.pi), ALU.mult, ROUND, ALU.add)
        ts(V, turns[:, :], turns[:, :], ROUND, ALU.subtract)
        yield
        for part in TWO_PI:
            stt(V, hid[:, :], turns[:, :], -part, hid[:, :], ALU.mult, ALU.add)
        ts(V, hid[:, :], hid[:, :], 3.1415925, ALU.min)
        m = ts(V, hid[:, :], hid[:, :], -3.1415925, ALU.max)
        last = act(S, hid[:, :], hid[:, :], ACT.Sin, after=[m])
        yield
    for i in range(NT):
        wide = act(S, window[:, :], decay[:, :], ACT.Exp, scale=cols[:, i:i + 1], after=[V.last])
        PE.wait([last] + [x for b in range(4) for x in c.bank_read[b]])
        for b in range(4):
            mm(PE, c.bank(b), hid[:, P * i:P * i + P], w3[:, 512 * b:512 * b + 512])
        yield
        m = tt(V, window[:, :], window[:, :], c.bank(0, 4), ALU.mult, after=[wide, PE.last])
        for b in range(4):
            c.bank_read[b] = [m]
        ts(V, window[:, D:2 * D], window[:, D:2 * D], cols[:, NT + i:NT + i + 1], ALU.mult)
        yield
        tt(V, both[:, i, 0, :], window[:, 0:D], window[:, D:2 * D], ALU.add)
        tt(V, both[:, i, 1, :], window[:, 0:D], window[:, D:2 * D], ALU.subtract)
        yield


def transform(c, dst, src, basis, j, a, half):
    bk = c.take_bank()
    cols = slice(512 * half, 512 * half + 512)
    c.PE.wait(c.bank_read[bk])
    for i in range(NT):
        mm(c.PE, c.bank(bk), basis[("cos_sj", "sin_sj")[a]][:, i, P * j:P * j + P], src(i)[:, cols], i == 0, i == NT - 1)
    c.bank_read[bk] = [act(c.S, dst[:, j, a, cols], c.bank(bk), ACT.Copy, after=[c.PE.last])]


def second_mixer(c, h, xn, work, tmp, following):
    V, S, G, PE = c.V, c.S, c.G, c.PE
    w = c.dram["w_in_2"]

    def keep(dst, func=ACT.Copy):
        return lambda out, done: act(S, dst, out, func, after=[done])

    conv_w = c.gain("conv_w").rearrange("p (j n) -> p j n", j=3)
    conv_b = c.gain("conv_b")

    def short_conv(n, dst):
        def evac(out, done):
            ts(V, dst, out, conv_w[:, 1, n:n + 1], ALU.mult, conv_b[:, n:n + 1], ALU.add, after=[done])
            stt(V, dst[:, 1:T], out[:, 0:T - 1], conv_w[:, 0, n:n + 1], dst[:, 1:T], ALU.mult, ALU.add)
            return stt(V, dst[:, 0:T - 1], out[:, 1:T], conv_w[:, 2, n:n + 1], dst[:, 0:T - 1], ALU.mult, ALU.add)
        return evac

    with ExitStack() as ctx:
        x0 = c.sb("hy_x0", [P, KD, T], ctx)
        u = c.sb("hy_u", [P, KD, T], ctx)
        og = c.sb("hg_og", [P, KD, T], ctx)
        with ExitStack() as inner:
            q = c.sb("hg_q", [P, HG_H, T], inner)
            zf = c.sb("hg_zf", [P, HG_H, T], inner)
            zb = c.sb("hg_zb", [P, HG_H, T], inner)
            v = c.sb("hg_v", [P, NT, D], inner)
            x = c.sb("hy_x", [P, T], inner)
            c.masks = c.sb("masks_2", [P, 2 * len(LEVELS), P], inner)
            c.reset = c.sb("reset_2", [P, T], inner)
            consts = [c.load(c.masks[:, :, :], c.dram["masks"]), c.load(c.reset[:, :], c.dram["reset"])]
            V.wait(consts)
            for n in range(KD):
                c.channels(w[8 + n], xn, keep(zf[:, n, :]))
            for n in range(KD):
                c.channels(w[16 + n], xn, keep(zb[:, n, :]))
            c.flush(w[0], w[1])
            o = work

            def projections():
                for n in range(KD):
                    c.channels(w[n], xn, keep(q[:, n, :], ACT.Silu))
                    yield
                for half in range(2):
                    cols = slice(512 * half, 512 * half + 512)
                    yield from c.tokens(c.dram["w_in_2_v"][half], xn, 512,
                                        lambda i, out, done, cols=cols: act(S, v[:, i, cols], out, ACT.Copy,
                                                                            after=[done]))

            def more():
                for n in range(KD):
                    def times_x1(out, done, n=n):
                        m = short_conv(16 + n, x[:, :])(out, done)
                        tt(V, u[:, n, :], u[:, n, :], x[:, :], ALU.mult)
                        return m

                    c.channels(w[32 + n], xn, short_conv(n, x0[:, n, :]))
                    yield
                    c.channels(w[40 + n], xn, short_conv(8 + n, u[:, n, :]))
                    yield
                    c.channels(w[48 + n], xn, times_x1)
                    yield
                for n in range(KD):
                    c.channels(w[24 + n], xn, keep(og[:, n, :], ACT.Silu))
                    yield

            first = projections()
            for _ in first:
                pass
            c.flush(w[32], w[40])
            c.rotation = [4, 5, 6]
            filler = more()
            together(hgrn(c, inner, q, zf, zb, v, o), filler, 2)
            for _ in filler:
                pass
            c.flush(w[56], w[57])
            c.barrier()
        sga = c.sb("gate_a", [P, KD, T], ctx)
        sgb = c.sb("gate_b", [P, KD, T], ctx)
        both = c.sb("filters", [P, NT, 2, D], ctx)
        with ExitStack() as inner:
            sq = c.sb("hg_sq", [P, HG_H, T], inner)
            tmps = c.sb("hg_tmp", [P, 2, T], inner)

            def mixer_gates():
                for n in range(KD):
                    c.channels(w[56 + n], xn, keep(sga[:, n, :], ACT.Sigmoid))
                    yield
                for n in range(KD):
                    c.channels(w[64 + n], xn, keep(sgb[:, n, :], ACT.Sigmoid))
                    yield

            filler = mixer_gates()
            gated_done = S.last
            together(pipeline([lambda b, hd=hd: head_norm(c, o, hd, b, sq, tmps, c.gain("hgrn_norm_g_2"), og,
                                                        gated_done)
                               for hd in range(HG_H)], 2), filler, 6)
            together(filters(c, inner, both), filler, 1)
            for _ in filler:
                pass
            c.flush(c.dram["w_branch_a_2"][0], c.dram["w_branch_a_2"][1])
            c.barrier()
        c.rotation = list(range(7))
        ya = c.sb("ya", [P, KD, T], ctx)
        basis, came = {}, []
        for name in ("cos_sj", "sin_sj", "cos_js", "sin_js"):
            basis[name] = c.sb(name, [P, NT, T], ctx)
            came.append(c.load(basis[name][:, :, :], c.dram[name]))
        ut = c.sb("hy_ut", [P, NT, D], ctx)
        fu = c.sb("hy_fu", [P, NT, 2, D], ctx)
        fk = c.sb("hy_fk", [P, NT, 2, D], ctx)
        for k in range(KD):
            c.split_chunk(o[:, k, :], xn, k)

        def branch_a():
            for n in range(KD):
                c.channels(c.dram["w_branch_a_2"][n], xn,
                           lambda out, done, n=n: tt(V, ya[:, n, :], out, sga[:, n, :], ALU.mult, after=[done]))
                yield

        filler = branch_a()
        PE.wait(came)
        for n in range(KD):
            bk = c.take_bank()
            PE.wait(c.bank_read[bk])
            for i in range(NT):
                tr(PE, c.bank(bk)[:, P * i:P * i + P], u[:, n, P * i:P * i + P], c.ident[:, :])
            c.bank_read[bk] = [act(S, ut[:, :, P * n:P * n + P], c.bank(bk)[:, 0:T].rearrange("p (i c) -> p i c", i=NT),
                                   ACT.Copy, after=[PE.last])]
        turned_u = S.last
        for j in range(NT):
            for a in range(2):
                for half in range(2):
                    transform(c, fk, lambda i, a=a: both[:, i, a, :], basis, j, a, half)
                    next(filler, None)
        PE.wait([turned_u])
        y = both
        for j in range(NT):
            for a in range(2):
                for half in range(2):
                    transform(c, fu, lambda i: ut[:, i, :], basis, j, a, half)
        transformed = [S.last, PE.last]
        for _ in filler:
            pass
        for j in range(NT):
            uc, us, kc, ks = fu[:, j, 0, :], fu[:, j, 1, :], fk[:, j, 0, :], fk[:, j, 1, :]
            t1, t2 = ut[:, 0, :], ut[:, 1, :]
            m1 = tt(G, t2, us, ks, ALU.mult, after=transformed + [V.last])
            tt(V, t1, uc, kc, ALU.mult, after=transformed)
            m1 = tt(V, y[:, j, 0, :], t1, t2, ALU.subtract, after=[m1])
            m2 = tt(G, t2, us, kc, ALU.mult, after=[m1])
            tt(V, t1, uc, ks, ALU.mult)
            m = tt(V, y[:, j, 1, :], t1, t2, ALU.add, after=[m2])
        c.flush(c.dram["w_branch_b_2"][0], c.dram["w_branch_b_2"][1])
        branch_a_done = PE.last
        for n in range(KD):
            bk = c.take_bank()
            PE.wait([m] + c.bank_read[bk])
            for step, (j, a) in enumerate(((0, 0), (0, 1), (1, 0), (1, 1))):
                mm(PE, c.bank(bk)[:, 0:T], y[:, j, a, P * n:P * n + P], basis[("cos_js", "sin_js")[a]][:, j, :],
                   step == 0, step == 3)
            ts(V, u[:, n, :], u[:, n, :], c.gain("hyena_bias_2")[:, n:n + 1], ALU.mult, after=[PE.last])
            c.bank_read[bk] = [stt(V, u[:, n, :], c.bank(bk)[:, 0:T], 1.0 / T, u[:, n, :], ALU.mult, ALU.add)]
            mu = tt(V, u[:, n, :], u[:, n, :], x0[:, n, :], ALU.mult)
            c.split_chunk(u[:, n, :], xn, n, [mu, branch_a_done])

        def merge(out, done, n):
            m = tt(V, sgb[:, n, :], out, sgb[:, n, :], ALU.mult, after=[done])
            tt(V, ya[:, n, :], ya[:, n, :], sgb[:, n, :], ALU.add)
            return m

        for n in range(KD):
            c.channels(c.dram["w_branch_b_2"][n], xn, lambda out, done, n=n: merge(out, done, n))
        c.flush(c.dram["w_out_2"][0], c.dram["w_out_2"][1])
        made = [V.last, PE.last]
        for k in range(KD):
            c.split_chunk(ya[:, k, :], xn, k, made)
        for n in range(KD):
            c.channels(c.dram["w_out_2"][n], xn, lambda out, done, n=n: c.add_to_h(h, work, n, out, done))
        c.flush(*following)
        c.barrier()


def program(nc, dram, out):
    with ExitStack() as ctx:
        c = Core(nc, ctx, dram)
        V, S, G, PE = c.V, c.S, c.G, c.PE
        h = c.sb("h", [P, KD, T])
        xn = Parts(*(c.sb(f"acts_{x}", [P, KD, T], dtype=F32R) for x in ("high", "low")))
        work = c.sb("work", [P, KD, T])
        tmp = c.sb("tmp", [P, T])
        c.gains = c.sb("gains", [P, N_GAINS])
        c.ident = c.sb("ident", [P, P])
        c.ones = c.sb("ones", [P, P])
        c.iota = c.sb("iota", [P, P])
        c.some_block = c.sb("some_block", [P, 1])
        c.gain = lambda name: c.gains[:, GAINS[name][0]:GAINS[name][1]]
        c.h_came = c.load(h[:, :, :], dram["xT"])
        c.gains_came = c.load(c.gains[:, :], dram["gains"])
        came = [c.gains_came] + [c.load(x[:, :], dram[n]) for x, n in (
            (c.ident, "ident"), (c.iota, "iota"), (c.some_block, "some_block"))]
        fill(V, c.ones[:, :], 1.0)
        for q in (V, S, G, PE):
            q.wait(came)
        PE.wait([V.last])

        with ExitStack() as shared:
            mem_kv = (c.sb("mem_k", [P, KD, T], shared), c.sb("mem_v", [P, NT, D], shared))
            with ExitStack() as mctx:
                c.masks = c.sb("masks", [P, 2 * len(LEVELS), P], mctx)
                c.reset = c.sb("reset", [P, T], mctx)
                V.wait([c.load(c.masks[:, :, :], dram["masks"]), c.load(c.reset[:, :], dram["reset"])])
                first_mixer(c, h, xn, work, tmp, mem_kv)
            cross_attention(c, h, xn, work, tmp, mem_kv, [dram["peer_wq"][0], dram["peer_wq"][1]])
        peer(c, h, xn, work, tmp, "peer_1", c.gain("norm_ffn"), 64, dram["peer_wq"], dram["peer_subkeys"],
             dram["peer_down"], dram["peer_up"], [dram["w_in_2"][8], dram["w_in_2"][9]])
        c.norm_finish(h, c.gain("norm_final"), h, work, tmp, summed=True,
                      each=lambda k, m: c.norm_add(h, work, k, [m]))
        c.norm_finish(h, c.gain("norm_mix_g_2"), work, work, tmp, xn)
        second_mixer(c, h, xn, work, tmp, [dram["peer_w_q_2"][0], dram["peer_w_q_2"][1]])
        peer(c, h, xn, work, tmp, "peer_2", c.gain("norm_ffn_g_2"), 128, dram["peer_w_q_2"],
             dram["peer_subkeys_2"], dram["peer_u_2"], dram["peer_v_2"])
        m = c.norm_finish(h, c.gain("norm_final_g_2"), work, work, tmp, summed=True)
        c.DMA.wait([c.load(out, work[:, :, :], after=[m])])

        block = ctx.enter_context(nc.Block())

        @block.sync
        def _(engine):
            c.DMA.play(engine)

        @block.gpsimd
        def _(engine):
            G.play(engine)

        @block.scalar
        def _(engine):
            S.play(engine)

        @block.vector
        def _(engine):
            V.play(engine)

        @block.tensor
        def _(engine):
            PE.play(engine)


def lay_out(x):
    def blocks(w, cols=P):
        w = w.reshape(KD, P, -1, cols)
        return np.ascontiguousarray(w.transpose(2, 1, 0, 3)).reshape(w.shape[2], P, KD * cols)

    def token_blocks(w, cols):
        k = 1024 // cols
        w = w.reshape(KD // k, k, P, -1, cols).transpose(3, 0, 2, 1, 4)
        return np.ascontiguousarray(w).reshape(w.shape[0], KD // k, P, 1024)

    def channel(v):
        return v.reshape(-1, P).T

    def turned(a):
        return np.ascontiguousarray(a.reshape(T, KD, P).transpose(2, 1, 0))

    a = dict(constants())
    x = {k: np.asarray(v) for k, v in x.items()}
    a["xT"], a["memT"] = turned(x["x"][0]), turned(x["mem"][0])
    w = x["w_in"][0]
    nq = w[:, 1552:2064].reshape(D, NSA_G, HPG, NSA_DH).transpose(0, 2, 1, 3).reshape(D, 512)
    a["w_in"] = blocks(np.concatenate([w[:, 0:512], w[:, 1024:1536], nq, w[:, 2064:2448], w[:, 2576:2704]], 1))
    a["w_in_gv"] = token_blocks(w[:, 512:1024], 512)[0]
    a["w_in_v"] = token_blocks(np.concatenate([w[:, 2448:2576], w[:, 2704:2832]], 1), 256)[0]
    a["w_in_small"] = np.ascontiguousarray(
        np.concatenate([w[:, 1536:1552], w[:, 2832:2856]], 1).reshape(KD, P, 40).transpose(1, 0, 2))
    wo = x["w_out"][0]
    nsa_rows = wo[512:].reshape(NSA_G, HPG, NSA_DH, D).transpose(1, 0, 2, 3).reshape(512, D)
    a["w_out"] = blocks(np.concatenate([wo[0:512], nsa_rows], 0))
    a["xa_wv"] = token_blocks(x["xa_wv"][0], 512)
    w = x["w_in_2"][0]
    a["w_in_2"] = blocks(np.concatenate([w[:, 0:3 * D], w[:, 4 * D:]], 1))
    a["w_in_2_v"] = token_blocks(w[:, 3 * D:4 * D], 512)
    for name in ("xa_wq", "xa_wk", "xa_wo", "peer_wq", "w_branch_a_2", "w_branch_b_2", "w_out_2",
                 "peer_w_q_2"):
        a[name] = blocks(x[name][0])
    a["rel_bias"] = x["rel_bias"]
    a["gla_gate_w2"] = x["gla_gate_w2"][0]
    for n in ("k", "v"):
        a[f"pos_{n}"] = np.ascontiguousarray(x[f"cmp_pos_{n}"][0][::-1].T)
        w1 = x[f"cmp_{n}_w1"][0].reshape(CMP_BLOCK, NSA_DH, CMP_HIDDEN)
        w1 = w1[::-1].transpose(1, 0, 2).reshape(NSA_DH, 4, 1024).transpose(1, 0, 2)
        a[f"cmp_{n}_w1"] = np.ascontiguousarray(np.concatenate([w1, w1], 1))
        a[f"cmp_{n}_w2"] = x[f"cmp_{n}_w2"][0]
    sk = x["peer_subkeys"][0].transpose(1, 3, 0, 2)
    a["peer_subkeys"] = np.ascontiguousarray(sk.reshape(P, PEER_H, NKEYS))
    sk = x["peer_subkeys_2"][0].transpose(3, 0, 1, 2)
    a["peer_subkeys_2"] = np.ascontiguousarray(sk.reshape(P, 2 * PEER_H, NKEYS))
    for down, up in (("peer_down", "peer_up"), ("peer_u_2", "peer_v_2")):
        d = x[down][0].reshape(P, NKEYS, KD, P)
        a[down] = np.ascontiguousarray(d.transpose(1, 3, 2, 0)).reshape(NKEYS, P, KD * P)
        a[up] = np.ascontiguousarray(x[up][0].reshape(P, NKEYS, D).transpose(1, 0, 2))
    a["filt_w1_2"], a["filt_w2_2"], a["filt_w3_2"] = x["filt_w1_2"][0], x["filt_w2_2"][0], x["filt_w3_2"][0]
    a["filt_vec"] = np.stack([x[n][0] for n in ("filt_b1_2", "filt_freq1_2", "filt_b2_2", "filt_freq2_2")], 1)
    a["filt_decay_2"] = x["filt_decay_2"][0]
    cols = {"lb": np.concatenate([channel(v) for v in x["hgrn_lb_logits_2"]], 1),
            "conv_w": np.concatenate([channel(v) for v in x["hyena_conv_w_2"][0]], 1),
            "conv_b": channel(x["hyena_conv_b_2"][0])}
    for name in GAINS:
        if name not in cols:
            cols[name] = channel(x[name].reshape(-1))
    a["gains"] = np.concatenate([cols[name] for name in GAINS], 1)
    return {k: np.ascontiguousarray(v) for k, v in a.items()}


def kernel(**inputs):
    import concourse.bacc as bacc
    from concourse.bass_utils import run_bass_kernel_spmd

    nc = bacc.Bacc("TRN2", target_bir_lowering=False, num_devices=1)
    arrays, dram = {}, {}
    for name, a in lay_out(inputs).items():
        arrays[f"in_{name}"] = a
        dram[name] = nc.dram_tensor(f"in_{name}", a.shape, mybir.dt.from_np(a.dtype), kind="ExternalInput").ap()
    dram["bias_scratch"] = nc.dram_tensor("bias_scratch", (NSA_H, 2 * T), F32, kind="Internal").ap()
    out = nc.dram_tensor("out_yT", (P, KD, T), F32, kind="ExternalOutput").ap()
    program(nc, dram, out)
    result = run_bass_kernel_spmd(nc, [arrays], core_ids=[0]).results[0]["out_yT"]
    return np.ascontiguousarray(result.transpose(2, 1, 0)).reshape(1, T, D)
```
